# Optimizing a Trainium2 kernel written in Bass

```python
import math
import jax
import jax.numpy as jnp
from jax import lax
import numpy as np

D_MODEL = 1024
BATCH = 1
SEQ = 256
DEPTH = 2
DEC_BATCH = 8
DEC_SEQ = 4
PAST_LEN = 2048
PAGE_SIZE = 128

N_MIXERS = 2
N_MLSTM_LAYERS = (DEPTH + 1) // 2
N_NSA_LAYERS = DEPTH // 2
NORM_EPS = 1e-6

M_HEADS = 8
M_DK = D_MODEL // 16
M_DV = D_MODEL // M_HEADS
M_CHUNK = 64
M_PROJ = 2 * M_HEADS * M_DK + 2 * M_HEADS * M_DV + 2 * M_HEADS

A_HEADS = 16
A_KV = 4
A_REP = A_HEADS // A_KV
A_DH = D_MODEL // A_HEADS
ROT_DIM = A_DH // 4
ROPE_THETA = 500000.0
CMP_STRIDE = 16
CMP_LEN = 2 * CMP_STRIDE
CMP_HID = A_DH
SEL_BLK = 64
N_SEL = 16
WINDOW = 512
SEL_QBLK = 64
WIN_QBLK = 128
A_QW = A_HEADS * A_DH
A_KVW = 3 * 2 * A_KV * A_DH
A_PROJ = A_QW + A_KVW + 3 * A_HEADS
ATTN_SCALE = A_DH ** -0.5

P_HEADS = 8
P_NKEYS = 128
P_EXPERTS = P_NKEYS * P_NKEYS
P_QDIM = 256
P_TOPK = 16
P_TOK_BLK = 256

kernel_name = 'hybrid_mlstm_nsa_peer_step'

def rmsnorm(x, g):
    xf = x.astype(jnp.float32)
    xf = xf * lax.rsqrt(jnp.mean(xf * xf, axis=-1, keepdims=True) + NORM_EPS)
    return (xf * g.astype(jnp.float32)).astype(x.dtype)

def masked_softmax(s, valid, axis=-1):
    s = jnp.where(valid, s.astype(jnp.float32), -jnp.inf)
    m = jnp.max(s, axis=axis, keepdims=True)
    m = jnp.where(jnp.isfinite(m), m, 0.0)
    e = jnp.exp(s - m)
    return e / jnp.maximum(jnp.sum(e, axis=axis, keepdims=True), 1e-30)

def partial_rotary(x, pos):
    half = ROT_DIM // 2
    inv_freq = ROPE_THETA ** (-(jnp.arange(half, dtype=jnp.float32) * (2.0 / ROT_DIM)))
    ang = pos.astype(jnp.float32)[:, None] * inv_freq[None, :]
    shape = (1, x.shape[1]) + (1,) * (x.ndim - 3) + (half,)
    cos = jnp.cos(ang).reshape(shape)
    sin = jnp.sin(ang).reshape(shape)
    xf = x.astype(jnp.float32)
    x1 = xf[..., :half]
    x2 = xf[..., half:ROT_DIM]
    out = jnp.concatenate([x1 * cos - x2 * sin, x2 * cos + x1 * sin, xf[..., ROT_DIM:]], axis=-1)
    return out.astype(x.dtype)

def mlstm_mixer(h, c0, n0, m0, w_in, b_i, b_f, head_norm, w_out):
    bsz, t_len, _ = h.shape
    proj = h @ w_in
    o1 = M_HEADS * M_DK
    o2 = 2 * o1
    o3 = o2 + M_HEADS * M_DV
    o4 = o3 + M_HEADS * M_DV
    o5 = o4 + M_HEADS
    q = proj[..., :o1].reshape(bsz, t_len, M_HEADS, M_DK).astype(jnp.float32)
    k = proj[..., o1:o2].reshape(bsz, t_len, M_HEADS, M_DK).astype(jnp.float32) * (M_DK ** -0.5)
    v = proj[..., o2:o3].reshape(bsz, t_len, M_HEADS, M_DV).astype(jnp.float32)
    o_gate = jax.nn.sigmoid(proj[..., o3:o4].astype(jnp.float32))
    log_i = proj[..., o4:o5].astype(jnp.float32) + b_i.astype(jnp.float32)
    log_f = jax.nn.log_sigmoid(proj[..., o5:].astype(jnp.float32) + b_f.astype(jnp.float32))
    chunk = math.gcd(t_len, M_CHUNK)
    n_chunks = t_len // chunk

    def to_chunks(a):
        return jnp.moveaxis(a.reshape((bsz, n_chunks, chunk) + a.shape[2:]), 1, 0)

    causal = jnp.tril(jnp.ones((chunk, chunk), dtype=bool))

    def chunk_step(carry, xs):
        c_prev, n_prev, m_prev = carry
        qc, kc, vc, lic, lfc = xs
        b = jnp.cumsum(lfc, axis=1)
        a = b + m_prev[:, None, :]
        d = b[:, :, None, :] - b[:, None, :, :] + lic[:, None, :, :]
        d = jnp.where(causal[None, :, :, None], d, -jnp.inf)
        m_t = jnp.maximum(a, jnp.max(d, axis=2))
        w_d = jnp.exp(d - m_t[:, :, None, :])
        w_a = jnp.exp(a - m_t)
        s = jnp.einsum('bthd,bshd->btsh', qc, kc) * w_d
        num = w_a[..., None] * jnp.einsum('bthd,bhde->bthe', qc, c_prev) + jnp.einsum('btsh,bshe->bthe', s, vc)
        den = w_a * jnp.einsum('bthd,bhd->bth', qc, n_prev) + jnp.sum(s, axis=2)
        h_out = num / jnp.maximum(jnp.abs(den), jnp.exp(-m_t))[..., None]
        m_new = m_t[:, -1]
        w_last = jnp.exp(d[:, -1] - m_new[:, None, :])
        decay = jnp.exp(a[:, -1] - m_new)
        c_new = decay[..., None, None] * c_prev + jnp.einsum('bsh,bshd,bshe->bhde', w_last, kc, vc)
        n_new = decay[..., None] * n_prev + jnp.einsum('bsh,bshd->bhd', w_last, kc)
        return (c_new, n_new, m_new), h_out

    init = (c0.astype(jnp.float32), n0.astype(jnp.float32), m0.astype(jnp.float32))
    (c_t, n_t, m_t), h_chunks = lax.scan(
        chunk_step, init,
        (to_chunks(q), to_chunks(k), to_chunks(v), to_chunks(log_i), to_chunks(log_f)))
    hid = jnp.moveaxis(h_chunks, 0, 1).reshape(bsz, t_len, M_HEADS, M_DV)
    hid = hid * lax.rsqrt(jnp.mean(hid * hid, axis=-1, keepdims=True) + NORM_EPS)
    hid = hid.reshape(bsz, t_len, M_HEADS * M_DV) * head_norm.astype(jnp.float32)
    y = (o_gate * hid).astype(h.dtype) @ w_out
    return y, c_t, n_t, m_t

def nsa_project(h, pos, w_in):
    bsz, t_len, _ = h.shape
    proj = h @ w_in
    q = partial_rotary(proj[..., :A_QW].reshape(bsz, t_len, A_HEADS, A_DH), pos)
    kv = proj[..., A_QW:A_QW + A_KVW].reshape(bsz, t_len, 3, 2, A_KV, A_DH)
    k_rot = partial_rotary(kv[:, :, :, 0], pos)
    kv = jnp.stack([k_rot, kv[:, :, :, 1]], axis=3)
    gate_pre = proj[..., A_QW + A_KVW:].reshape(bsz, t_len, A_HEADS, 3)
    return q, kv[:, :, 0], kv[:, :, 1], kv[:, :, 2], gate_pre

def pad_to_blocks(kv):
    t_k = kv.shape[1]
    t_p = -(-t_k // SEL_BLK) * SEL_BLK
    return jnp.pad(kv, ((0, 0), (0, t_p - t_k), (0, 0), (0, 0), (0, 0)))

def compressed_branch(q, pos, kv, w1, b1, w2):
    bsz, t_q = q.shape[:2]
    kv = pad_to_blocks(kv)
    sub = kv.reshape(bsz, kv.shape[1] // CMP_STRIDE, CMP_STRIDE, 2, A_KV, A_DH)
    first = jnp.einsum('bnlcgd,cldh->bncgh', sub, w1[:, :CMP_STRIDE])
    second = jnp.einsum('bnlcgd,cldh->bncgh', sub, w1[:, CMP_STRIDE:])
    hid = jax.nn.gelu((first[:, :-1] + second[:, 1:]).astype(jnp.float32) + b1.astype(jnp.float32)[:, None, :], approximate=False)
    ckv = jnp.einsum('bncgh,chd->bncgd', hid.astype(kv.dtype), w2)
    n_cmp = ckv.shape[1]
    block_end = jnp.arange(n_cmp) * CMP_STRIDE + CMP_LEN - 1
    valid = block_end[None, :] <= pos[:, None]
    qg = q.reshape(bsz, t_q, A_KV, A_REP, A_DH)
    s = jnp.einsum('bqgrd,bngd->bgrqn', qg, ckv[:, :, 0]).astype(jnp.float32) * ATTN_SCALE
    p = masked_softmax(s, valid)
    o = jnp.einsum('bgrqn,bngd->bqgrd', p.astype(ckv.dtype), ckv[:, :, 1])
    return o.reshape(bsz, t_q, A_HEADS, A_DH), p

def selected_branch(q, pos, kv, p_cmp):
    bsz, t_q = q.shape[:2]
    kv = pad_to_blocks(kv)
    n_blk = kv.shape[1] // SEL_BLK
    n_cmp = p_cmp.shape[-1]
    c_start = jnp.arange(n_cmp) * CMP_STRIDE
    s_start = jnp.arange(n_blk) * SEL_BLK
    overlap = jnp.clip(jnp.minimum(c_start[:, None] + CMP_LEN, s_start[None, :] + SEL_BLK)
                       - jnp.maximum(c_start[:, None], s_start[None, :]), 0, None).astype(jnp.float32) / CMP_STRIDE
    imp = jnp.einsum('bgrqn,nj->bgqj', p_cmp, overlap)
    cur = pos // SEL_BLK
    j = jnp.arange(n_blk)
    forced = (j[None, :] == 0) | (j[None, :] == cur[:, None]) | (j[None, :] == cur[:, None] - 1)
    score = jnp.where(forced, jnp.inf, jnp.where(j[None, :] <= cur[:, None], imp, -jnp.inf))
    k_sel = min(N_SEL, n_blk)
    _, idx = lax.top_k(score, k_sel)
    blocks = kv.reshape(bsz, n_blk, SEL_BLK, 2, A_KV, A_DH).transpose(0, 4, 1, 2, 3, 5)
    qc_len = math.gcd(t_q, SEL_QBLK)
    n_q = t_q // qc_len
    q_all = jnp.moveaxis(q.reshape(bsz, n_q, qc_len, A_KV, A_REP, A_DH), 1, 0)
    idx_all = jnp.moveaxis(idx.reshape(bsz, A_KV, n_q, qc_len, k_sel), 2, 0)
    pos_all = pos.reshape(n_q, qc_len)
    b_ix = jnp.arange(bsz)[:, None, None, None]
    g_ix = jnp.arange(A_KV)[None, :, None, None]
    offs = jnp.arange(SEL_BLK)

    def one_block(args):
        qc, ic, pc = args
        kvg = blocks[b_ix, g_ix, ic]
        s = jnp.einsum('bqgrd,bgqksd->bgrqks', qc, kvg[..., 0, :]).astype(jnp.float32) * ATTN_SCALE
        kpos = ic[..., None] * SEL_BLK + offs
        valid = (kpos <= pc[None, None, :, None, None])[:, :, None]
        p = masked_softmax(s, valid, axis=(-2, -1))
        return jnp.einsum('bgrqks,bgqksd->bqgrd', p.astype(kvg.dtype), kvg[..., 1, :])

    o = lax.map(one_block, (q_all, idx_all, pos_all))
    return jnp.moveaxis(o, 0, 1).reshape(bsz, t_q, A_HEADS, A_DH)

def window_branch(q, pos, kv_ext):
    bsz, t_q = q.shape[:2]
    qb_len = math.gcd(t_q, WIN_QBLK)
    n_qb = t_q // qb_len
    band = WINDOW + qb_len
    q_all = jnp.moveaxis(q.reshape(bsz, n_qb, qb_len, A_KV, A_REP, A_DH), 1, 0)
    starts = jnp.arange(n_qb) * qb_len
    pos_all = pos.reshape(n_qb, qb_len)
    base = pos[0] - WINDOW

    def one_block(args):
        qc, st, qp = args
        kb = lax.dynamic_slice_in_dim(kv_ext, st, band, axis=1)
        kpos = base + st + jnp.arange(band)
        diff = qp[:, None] - kpos[None, :]
        valid = (diff >= 0) & (diff <= WINDOW) & (kpos >= 0)[None, :]
        s = jnp.einsum('bqgrd,bkgd->bgrqk', qc, kb[:, :, 0]).astype(jnp.float32) * ATTN_SCALE
        p = masked_softmax(s, valid)
        return jnp.einsum('bgrqk,bkgd->bqgrd', p.astype(kb.dtype), kb[:, :, 1])

    o = lax.map(one_block, (q_all, starts, pos_all))
    return jnp.moveaxis(o, 0, 1).reshape(bsz, t_q, A_HEADS, A_DH)

def nsa_mixer(h, pos, past_cmp, past_sel, past_win, w_in, b_gate, cmp_w1, cmp_b1, cmp_w2, w_out):
    bsz, t_len, _ = h.shape
    q, cmp_new, sel_new, win_new, gate_pre = nsa_project(h, pos, w_in)
    if past_cmp is None:
        cmp_all, sel_all = cmp_new, sel_new
        rows = min(WINDOW, t_len)
        win_ext = jnp.pad(win_new, ((0, 0), (WINDOW, 0), (0, 0), (0, 0), (0, 0)))
    else:
        cmp_all = jnp.concatenate([past_cmp, cmp_new], axis=1)
        sel_all = jnp.concatenate([past_sel, sel_new], axis=1)
        rows = past_win.shape[1]
        win_ext = jnp.concatenate(
            [jnp.pad(past_win, ((0, 0), (WINDOW - rows, 0), (0, 0), (0, 0), (0, 0))), win_new], axis=1)
    win_buf = win_ext[:, win_ext.shape[1] - rows:]
    o_cmp, p_cmp = compressed_branch(q, pos, cmp_all, cmp_w1, cmp_b1, cmp_w2)
    o_sel = selected_branch(q, pos, sel_all, p_cmp)
    o_win = window_branch(q, pos, win_ext)
    g = jax.nn.sigmoid((gate_pre + b_gate).astype(jnp.float32))
    o = g[..., 0:1] * o_cmp + g[..., 1:2] * o_sel + g[..., 2:3] * o_win
    y = o.reshape(bsz, t_len, A_QW).astype(h.dtype) @ w_out
    return y, cmp_new, sel_new, win_buf

def peer_ffn(h, w_q, sub_keys, u_tab, v_tab):
    bsz, t_len, d = h.shape
    n_tok = bsz * t_len
    blk = math.gcd(n_tok, P_TOK_BLK)
    half = P_QDIM // 2

    def one_block(x):
        q = (x @ w_q).reshape(blk, P_HEADS, P_QDIM)
        s1 = jnp.einsum('nhd,hkd->nhk', q[..., :half], sub_keys[:, 0]).astype(jnp.float32)
        s2 = jnp.einsum('nhd,hkd->nhk', q[..., half:], sub_keys[:, 1]).astype(jnp.float32)
        v1, i1 = lax.top_k(s1, P_TOPK)
        v2, i2 = lax.top_k(s2, P_TOPK)
        cand = (v1[..., :, None] + v2[..., None, :]).reshape(blk, P_HEADS, P_TOPK * P_TOPK)
        vals, ci = lax.top_k(cand, P_TOPK)
        expert = (jnp.take_along_axis(i1, ci // P_TOPK, axis=-1) * P_NKEYS
                  + jnp.take_along_axis(i2, ci % P_TOPK, axis=-1))
        gate = jax.nn.softmax(vals, axis=-1)
        u = u_tab[expert]
        v = v_tab[expert]
        act = jax.nn.gelu(jnp.einsum('nd,nhkd->nhk', x, u).astype(jnp.float32), approximate=False)
        return jnp.einsum('nhk,nhkd->nd', (gate * act).astype(v.dtype), v)

    out = lax.map(one_block, h.reshape(n_tok // blk, blk, d))
    return out.reshape(bsz, t_len, d)

def setup_inputs(seed: int = 0) -> dict:
    key = jax.random.key(seed)
    ks = jax.random.split(key, 32)
    n_pages = PAST_LEN // PAGE_SIZE
    n_used = DEC_BATCH * n_pages
    pool = n_used + n_used // 4
    win_rows = min(WINDOW, PAST_LEN)

    def nrm(k, shape, scale):
        return scale * jax.random.normal(k, shape, jnp.float32)

    page_table = jax.random.permutation(ks[0], pool)[:n_used].reshape(DEC_BATCH, n_pages).astype(jnp.int32)
    return {
        'x_prompt': nrm(ks[1], (BATCH, SEQ, D_MODEL), 1.0),
        'x_sample': nrm(ks[2], (DEC_BATCH, DEC_SEQ, D_MODEL), 1.0),
        'cache_cmp_kv': nrm(ks[3], (N_NSA_LAYERS, pool, PAGE_SIZE, 2, A_KV, A_DH), 1.0),
        'cache_sel_kv': nrm(ks[4], (N_NSA_LAYERS, pool, PAGE_SIZE, 2, A_KV, A_DH), 1.0),
        'state_win_kv': nrm(ks[5], (N_NSA_LAYERS, DEC_BATCH, win_rows, 2, A_KV, A_DH), 1.0),
        'state_C': nrm(ks[6], (N_MLSTM_LAYERS, DEC_BATCH, M_HEADS, M_DK, M_DV), 0.5),
        'state_n': nrm(ks[7], (N_MLSTM_LAYERS, DEC_BATCH, M_HEADS, M_DK), 0.5),
        'state_m': nrm(ks[8], (N_MLSTM_LAYERS, DEC_BATCH, M_HEADS), 1.0),
        'page_table': page_table,
        'norm_mix': 1.0 + nrm(ks[9], (DEPTH, D_MODEL), 0.05),
        'norm_ffn': 1.0 + nrm(ks[10], (DEPTH, D_MODEL), 0.05),
        'norm_final': 1.0 + nrm(ks[11], (D_MODEL,), 0.05),
        'mlstm_w_in': nrm(ks[12], (N_MLSTM_LAYERS, D_MODEL, M_PROJ), D_MODEL ** -0.5),
        'mlstm_b_i': nrm(ks[13], (N_MLSTM_LAYERS, M_HEADS), 0.1),
        'mlstm_b_f': 3.0 + nrm(ks[14], (N_MLSTM_LAYERS, M_HEADS), 0.5),
        'mlstm_head_norm': 1.0 + nrm(ks[15], (N_MLSTM_LAYERS, M_HEADS * M_DV), 0.05),
        'mlstm_w_out': nrm(ks[16], (N_MLSTM_LAYERS, M_HEADS * M_DV, D_MODEL), (M_HEADS * M_DV) ** -0.5),
        'nsa_w_in': nrm(ks[17], (N_NSA_LAYERS, D_MODEL, A_PROJ), D_MODEL ** -0.5),
        'nsa_b_gate': nrm(ks[18], (N_NSA_LAYERS, A_HEADS, 3), 0.1),
        'nsa_cmp_w1': nrm(ks[19], (N_NSA_LAYERS, 2, CMP_LEN, A_DH, CMP_HID), (CMP_LEN * A_DH) ** -0.5),
        'nsa_cmp_b1': nrm(ks[20], (N_NSA_LAYERS, 2, CMP_HID), 0.1),
        'nsa_cmp_w2': nrm(ks[21], (N_NSA_LAYERS, 2, CMP_HID, A_DH), CMP_HID ** -0.5),
        'nsa_w_out': nrm(ks[22], (N_NSA_LAYERS, A_QW, D_MODEL), A_QW ** -0.5),
        'peer_w_q': nrm(ks[23], (DEPTH, D_MODEL, P_HEADS * P_QDIM), D_MODEL ** -0.5),
        'peer_sub_keys': nrm(ks[24], (DEPTH, P_HEADS, 2, P_NKEYS, P_QDIM // 2), (P_QDIM // 2) ** -0.5),
        'peer_u': nrm(ks[25], (DEPTH, P_EXPERTS, D_MODEL), D_MODEL ** -0.5),
        'peer_v': nrm(ks[26], (DEPTH, P_EXPERTS, D_MODEL), P_HEADS ** -0.5),
    }

def reference(x_prompt, x_sample, cache_cmp_kv, cache_sel_kv, state_win_kv, state_C, state_n, state_m,
              page_table, norm_mix, norm_ffn, norm_final, mlstm_w_in, mlstm_b_i, mlstm_b_f,
              mlstm_head_norm, mlstm_w_out, nsa_w_in, nsa_b_gate, nsa_cmp_w1, nsa_cmp_b1, nsa_cmp_w2,
              nsa_w_out, peer_w_q, peer_sub_keys, peer_u, peer_v):
    bsz, t_len, _ = x_prompt.shape
    dbsz, t_s, _ = x_sample.shape
    past_len = page_table.shape[1] * PAGE_SIZE
    pos_p = jnp.arange(t_len, dtype=jnp.int32)
    pos_s = past_len + jnp.arange(t_s, dtype=jnp.int32)
    xp, xs = x_prompt, x_sample
    cmp_p, sel_p, win_p, c_p, n_p, m_p = [], [], [], [], [], []
    cmp_s, sel_s, win_s, c_s, n_s, m_s = [], [], [], [], [], []
    for layer in range(DEPTH):
        hp = rmsnorm(xp, norm_mix[layer])
        hs = rmsnorm(xs, norm_mix[layer])
        if layer % N_MIXERS == 0:
            a = layer // N_MIXERS
            zc = jnp.zeros((bsz, M_HEADS, M_DK, M_DV), jnp.float32)
            zn = jnp.zeros((bsz, M_HEADS, M_DK), jnp.float32)
            zm = jnp.zeros((bsz, M_HEADS), jnp.float32)
            yp, cpt, npt, mpt = mlstm_mixer(hp, zc, zn, zm, mlstm_w_in[a], mlstm_b_i[a], mlstm_b_f[a],
                                            mlstm_head_norm[a], mlstm_w_out[a])
            ys, cst, nst, mst = mlstm_mixer(hs, state_C[a], state_n[a], state_m[a], mlstm_w_in[a],
                                            mlstm_b_i[a], mlstm_b_f[a], mlstm_head_norm[a], mlstm_w_out[a])
            c_p.append(cpt.astype(state_C.dtype))
            n_p.append(npt.astype(state_n.dtype))
            m_p.append(mpt.astype(state_m.dtype))
            c_s.append(cst.astype(state_C.dtype))
            n_s.append(nst.astype(state_n.dtype))
            m_s.append(mst.astype(state_m.dtype))
        else:
            l = layer // N_MIXERS
            yp, ckp, skp, wkp = nsa_mixer(hp, pos_p, None, None, None, nsa_w_in[l], nsa_b_gate[l],
                                          nsa_cmp_w1[l], nsa_cmp_b1[l], nsa_cmp_w2[l], nsa_w_out[l])
            past_cmp = cache_cmp_kv[l, page_table].reshape(dbsz, past_len, 2, A_KV, A_DH)
            past_sel = cache_sel_kv[l, page_table].reshape(dbsz, past_len, 2, A_KV, A_DH)
            ys, cks, sks, wks = nsa_mixer(hs, pos_s, past_cmp, past_sel, state_win_kv[l], nsa_w_in[l],
                                          nsa_b_gate[l], nsa_cmp_w1[l], nsa_cmp_b1[l], nsa_cmp_w2[l],
                                          nsa_w_out[l])
            cmp_p.append(ckp)
            sel_p.append(skp)
            win_p.append(wkp)
            cmp_s.append(cks)
            sel_s.append(sks)
            win_s.append(wks)
        xp = xp + yp
        xs = xs + ys
        xp = xp + peer_ffn(rmsnorm(xp, norm_ffn[layer]), peer_w_q[layer], peer_sub_keys[layer],
                           peer_u[layer], peer_v[layer])
        xs = xs + peer_ffn(rmsnorm(xs, norm_ffn[layer]), peer_w_q[layer], peer_sub_keys[layer],
                           peer_u[layer], peer_v[layer])
    y_prompt = rmsnorm(xp, norm_final)
    y_sample = rmsnorm(xs, norm_final)
    return (y_prompt, y_sample,
            jnp.stack(cmp_p), jnp.stack(sel_p), jnp.stack(win_p),
            jnp.stack(c_p), jnp.stack(n_p), jnp.stack(m_p),
            jnp.stack(cmp_s), jnp.stack(sel_s), jnp.stack(win_s),
            jnp.stack(c_s), jnp.stack(n_s), jnp.stack(m_s))


_drawn_inputs = setup_inputs


def setup_inputs(seed=0):
    import zlib

    import numpy as np

    out = dict(_drawn_inputs(seed))
    spreads = {}
    factors = {'nsa_b_gate': 3.028}
    for name, (base, spread) in spreads.items():
        noise = np.random.default_rng([zlib.crc32(name.encode()), seed]).standard_normal(out[name].shape)
        drawn = base * np.exp(spread * noise) if base else spread * noise
        out[name] = jnp.asarray(drawn.astype(out[name].dtype))
    for name, factor in factors.items():
        out[name] = (out[name] * factor).astype(out[name].dtype)
    return out
```

```python
from contextlib import ExitStack

import numpy as np

import concourse.bass as bass
from concourse import mybir

F32 = mybir.dt.float32
I32 = mybir.dt.int32
U32 = mybir.dt.uint32
ALU = mybir.AluOpType
ACT = mybir.ActivationFunctionType
AX = mybir.AxisListType

P = 128
D = 1024
DC = D // P
SEQ = 256
DEC_B, DEC_S = 8, 4
NDEC = DEC_B * DEC_S
NTOK = SEQ + NDEC
TILES = [(0, 128), (128, 128), (256, NDEC)]
NT = len(TILES)
EPS = 1e-6
NEG = -1e30

MH, MDK, MDV = 8, 64, 128
VW = MDV + 1
AH, AG, AR, ADH = 16, 4, 4, 64
ROT = ADH // 4
CSTR, CLEN = 16, 32
SBLK, NSEL = 64, 16
WIN = 512
PAST, PAGE = 2048, 128
NPAGE = PAST // PAGE
PH, PK, PTOP = 8, 128, 16
AQW, AKVW = AH * ADH, 6 * AG * ADH


def constants():
    at, cols = {}, []

    def put(name, a):
        a = np.asarray(a, np.float32)
        full = np.zeros((P, int(np.prod(a.shape[1:]))), np.float32)
        full[: a.shape[0]] = a.reshape(a.shape[0], -1)
        at[name] = (sum(c.shape[1] for c in cols), a.shape)
        cols.append(full)

    i = np.arange(P)
    d = np.arange(NDEC)
    same = (d[:, None] // DEC_S) == (d[None, :] // DEC_S)
    put("ident", np.eye(P))
    put("tri", i[:, None] <= i[None, :])
    put("tri_dec", same & (d[:, None] <= d[None, :]))
    put("mask", np.where(i[:, None] <= i[None, :], 0, NEG))
    put("mask_dec", np.where(same & (d[:, None] <= d[None, :]), 0, NEG))
    put("sel_head", np.repeat(np.eye(MH)[:, :, None], P, 2))
    put("last", (i == P - 1)[:, None] * np.ones((1, P)))
    put("last_dec", same & (d[:, None] % DEC_S == DEC_S - 1))
    pb = i // 64
    put("last_state", [[[t == DEC_S * (2 * b4 + pb[p]) + DEC_S - 1 for p in range(P)] for b4 in range(4)] for t in d])
    put("seq_q", [[[t // DEC_S == 2 * b4 + pb[p] for t in d] for b4 in range(4)] for p in range(P)])
    put("seq_k", [[t // DEC_S == b for b in range(DEC_B)] for t in d])
    put("iota16", np.tile(np.arange(PTOP), (P, 1)))
    half = ROT // 2
    inv = np.float32(500000.0) ** (-(np.arange(half, dtype=np.float32) * np.float32(2.0 / ROT)))
    pos = np.zeros((P, NT), np.float32)
    pos[:, 0], pos[:, 1], pos[:NDEC, 2] = i, i + P, PAST + d % DEC_S
    ang = (pos[:, :, None] * inv.astype(np.float32)).astype(np.float32).astype(np.float64)
    put("cos", np.cos(ang))
    put("sin", np.sin(ang))
    put("causal", np.where(i[:, None] >= i[None, :], 0, NEG))
    n = np.arange(15)
    cm = [[np.where(n * CSTR + CLEN - 1 <= t + q, 0, NEG) for t in (0, P)] for q in i]
    put("cmp_mask", cm)
    put("cmp_any", [[float(t + q >= CLEN - 1) for t in (0, P)] for q in i])
    g, q = i // 16, i % DEC_S
    put("sum_heads", (g[:, None] == g[None, :]) & (q[:, None] == q[None, :]))
    put("new_mask", [[[0 if t // DEC_S == 2 * u + p // 64 and t % DEC_S <= p % DEC_S else NEG for t in d]
                      for u in range(4)] for p in i])
    put("group_one", [[float((p % 64) // 16 == k) for k in range(AG)] for p in i])
    put("win_mask", [[[NEG if 4 * n_ + j < q[p] else 0 for n_ in range(P)] for j in range(4)] for p in i])
    put("pos16", np.repeat(i[:, None] % 8, DEC_B, 1))
    put("page_rep", [[float(r // 8 == p) for r in range(P)] for p in range(NPAGE)])
    put("stack32", [[float(p % NDEC == t) for t in range(NDEC)] for p in range(P)])
    return at, np.concatenate(cols, 1)


CONST_AT, CONST = constants()


class Chain:

    def __init__(self, engine, sem):
        self.engine, self.sem, self.n = engine, sem, 0

    def __call__(self, instruction):
        self.n += 1
        instruction.then_inc(self.sem, 1)
        self.engine.wait_ge(self.sem, self.n)


class Stage:

    def __init__(self, nc, name):
        self.nc, self.name, self.sems, self.stack = nc, name, [], ExitStack()

    def __enter__(self):
        return self

    def sb(self, name, shape, dt=F32):
        return self.stack.enter_context(self.nc.sbuf_tensor(f"{self.name}_{name}", shape, dt))

    def ps(self, name, shape, dt=F32):
        return self.stack.enter_context(self.nc.psum_tensor(f"{self.name}_{name}", shape, dt))

    def sem(self, name):
        s = self.nc.alloc_semaphore(f"{self.name}_{name}")
        self.sems.append(s)
        return s

    def __exit__(self, *exc):
        self.stack.close()
        if exc[0] is None:
            self.nc.clear_and_free_semaphores(self.sems)
            self.nc.all_engine_barrier()
        return False


def view(tile, name, rows=None):
    at, shape = CONST_AT[name]
    n = int(np.prod(shape[1:]))
    a = tile[0:(rows or shape[0]), at:at + n]
    if len(shape) == 3:
        a = a.rearrange("p (a b) -> p a b", a=shape[1])
    if len(shape) == 4:
        a = a.rearrange("p (a b c) -> p a b c", a=shape[1], b=shape[2])
    return a


def norm_stage(nc, name, M, gain, keep=None):
    with Stage(nc, name) as st:
        gain_b = st.sb("gain", [P, D])
        h = keep if keep is not None else st.sb("h", [P, NT, D])
        sq = st.sb("sq", [P, 2, D])
        ss = st.sb("ss", [P, 3 * NT])
        tr = [st.ps(f"tr{i}", [P, 4, P]) for i in range(4)]
        gain_in = st.sem("gain_in")
        vec = st.sem("vec")
        mean_ready = st.sem("mean_ready")
        root_ready = st.sem("root_ready")
        h_ready = st.sem("h_ready")
        turned = st.sem("turned")
        copied = st.sem("copied")
        groups = [(t, g) for t in range(NT) for g in range(DC // 4)]
        with nc.Block() as block:

            @block.sync
            def _(sp):
                sp.dma_start(gain_b[:], gain.partition_broadcast(P)).then_inc(gain_in, 16)

            @block.vector
            def _(dve):
                step = Chain(dve, vec)
                for t, (_, n) in enumerate(TILES):
                    step(dve.tensor_tensor_reduce(sq[0:n, t % 2, :], M.x[0:n, t, :], M.x[0:n, t, :], 1.0, 0.0,
                                                  ALU.mult, ALU.add, ss[0:n, t:t + 1]))
                    dve.tensor_scalar(ss[0:n, NT + t:NT + t + 1], ss[0:n, t:t + 1], 1.0 / D, EPS,
                                      ALU.mult, ALU.add).then_inc(mean_ready, 1)
                dve.wait_ge(gain_in, 16)
                for t, (_, n) in enumerate(TILES):
                    dve.wait_ge(root_ready, t + 1)
                    step(dve.reciprocal(ss[0:n, 2 * NT + t:2 * NT + t + 1], ss[0:n, t:t + 1]))
                    dve.scalar_tensor_tensor(out=h[0:n, t, :], in0=M.x[0:n, t, :],
                                             scalar=ss[0:n, 2 * NT + t:2 * NT + t + 1], in1=gain_b[0:n, :],
                                             op0=ALU.mult, op1=ALU.mult).then_inc(h_ready, 1)

            @block.tensor
            def _(pe):
                for k, (t, g) in enumerate(groups):
                    n = TILES[t][1]
                    pe.wait_ge(h_ready, t + 1)
                    if k >= 4:
                        pe.wait_ge(copied, k - 3)
                    for c in range(4):
                        mm = pe.transpose(tr[k % 4][:, c, 0:n], h[0:n, t, (4 * g + c) * P:(4 * g + c + 1) * P],
                                          M.ident[0:n, 0:n])
                    mm.then_inc(turned, 1)

            @block.scalar
            def _(act):
                for t, (_, n) in enumerate(TILES):
                    act.wait_ge(mean_ready, t + 1)
                    act.activation(ss[0:n, t:t + 1], ss[0:n, NT + t:NT + t + 1], ACT.Sqrt).then_inc(root_ready, 1)
                for k, (t, g) in enumerate(groups):
                    t0, n = TILES[t]
                    act.wait_ge(turned, k + 1)
                    act.activation(M.h_T[:, 4 * g:4 * g + 4, t0:t0 + n], tr[k % 4][:, :, 0:n],
                                   ACT.Copy).then_inc(copied, 1)


def turn_stage(nc, name, M, src):
    with Stage(nc, name) as st:
        tr = [st.ps(f"tr{i}", [P, 4, P]) for i in range(4)]
        turned = st.sem("turned")
        copied = st.sem("copied")
        groups = [(t, g) for t in range(NT) for g in range(DC // 4)]
        with nc.Block() as block:

            @block.tensor
            def _(pe):
                for k, (t, g) in enumerate(groups):
                    n = TILES[t][1]
                    if k >= 4:
                        pe.wait_ge(copied, k - 3)
                    for c in range(4):
                        mm = pe.transpose(tr[k % 4][:, c, 0:n], src[0:n, t, (4 * g + c) * P:(4 * g + c + 1) * P],
                                          M.ident[0:n, 0:n])
                    mm.then_inc(turned, 1)

            @block.scalar
            def _(act):
                for k, (t, g) in enumerate(groups):
                    t0, n = TILES[t]
                    act.wait_ge(turned, k + 1)
                    act.activation(M.h_T[:, 4 * g:4 * g + 4, t0:t0 + n], tr[k % 4][:, :, 0:n],
                                   ACT.Copy).then_inc(copied, 1)


WB = 512
WRING = 3


def project_stage(nc, name, M, weight, jobs):
    w_view = weight.rearrange("(c p) n -> p c n", p=P)
    with Stage(nc, name) as st:
        w = st.sb("w", [P, WRING, DC, WB])
        acc = [st.ps(f"acc{i}", [P, 512]) for i in range(8)]
        w_in = [st.sem(f"w_in{i}") for i in range(WRING)]
        summed = st.sem("summed")
        stored = st.sem("stored")
        outs, ends = [], []
        for j, (col, n, kind, dst) in enumerate(jobs):
            for k in range(-(-n // P) if kind == "T" else NT):
                outs.append((j, k))
            ends.append(len(outs))
        with nc.Block() as block:

            @block.sync
            def _(sp):
                for j, (col, n, _, _) in enumerate(jobs):
                    if j >= WRING:
                        sp.wait_ge(summed, ends[j - WRING])
                    sp.dma_start(w[:, j % WRING, :, 0:n], w_view[:, :, col:col + n]).then_inc(w_in[j % WRING], 16)

            @block.tensor
            def _(pe):
                for q, (j, k) in enumerate(outs):
                    _, n, kind, _ = jobs[j]
                    pe.wait_ge(w_in[j % WRING], 16 * (j // WRING + 1))
                    if q >= 8:
                        pe.wait_ge(stored, q - 7)
                    t0, nt = TILES[k] if kind != "T" else (0, 0)
                    for c in range(DC):
                        if kind == "T":
                            mm = pe.matmul(acc[q % 8][:, 0:NTOK], w[:, j % WRING, c, k * P:(k + 1) * P],
                                           M.h_T[:, c, :], start=(c == 0), stop=(c == DC - 1))
                        else:
                            mm = pe.matmul(acc[q % 8][0:nt, 0:n], M.h_T[:, c, t0:t0 + nt],
                                           w[:, j % WRING, c, 0:n], start=(c == 0), stop=(c == DC - 1))
                    mm.then_inc(summed, 1)

            if jobs[0][2] == "add":

                @block.vector
                def _(dve):
                    for q, (j, k) in enumerate(outs):
                        col, n, _, _ = jobs[j]
                        nt = TILES[k][1]
                        dve.wait_ge(summed, q + 1)
                        dve.tensor_tensor(M.x[0:nt, k, col:col + n], acc[q % 8][0:nt, 0:n],
                                          M.x[0:nt, k, col:col + n], ALU.add).then_inc(stored, 1)
            else:

                @block.scalar
                def _(act):
                    for q, (j, k) in enumerate(outs):
                        _, n, kind, dst = jobs[j]
                        place, func, scale = dst(k)
                        act.wait_ge(summed, q + 1)
                        src = acc[q % 8][:, 0:NTOK] if kind == "T" else acc[q % 8][0:TILES[k][1], 0:n]
                        if len(place.shape) == 3:
                            src = src.rearrange("p (a b) -> p a b", a=place.shape[1])
                        if len(place.shape) == 4:
                            src = src.rearrange("p (a b c) -> p a b c", a=place.shape[1], b=place.shape[2])
                        act.activation(place, src, func, scale=scale).then_inc(stored, 1)


def add_jobs():
    return [(c, WB, "add", None) for c in range(0, D, WB)]


def mlstm_stage(nc, M, I, O):
    with Stage(nc, "mx") as outer:
        q_T = outer.sb("q_T", [P, 4, NTOK])
        k_T = outer.sb("k_T", [P, 4, NTOK])
        v = outer.sb("v", [P, NT, MH, VW])
        og = outer.sb("og", [P, NT, D])
        gates = outer.sb("gates", [P, NT, 2 * MH])
        state = outer.sb("state", [P, 4, MH, VW])
        m_nat = outer.sb("m_nat", [NDEC, MH])
        m_T = outer.sb("m_T", [MH, DEC_B])
        bias = outer.sb("bias", [P, 2 * MH])
        hn = outer.sb("hn", [P, D])
        hid = outer.sb("hid", [P, NT, D])
        w_in, C_in = I["mlstm_w_in"][0], I["state_C"][0]
        loads_done = outer.sem("loads_done")
        zeroed = outer.sem("zeroed")

        with nc.Block() as block:

            @block.gpsimd
            def _(pool):
                pool.memset(v[:, :, :, MDV:VW], 1.0).then_inc(zeroed, 1)
                pool.memset(gates[:], 0.0).then_inc(zeroed, 1)
                pool.memset(og[:], 0.0).then_inc(zeroed, 1)
                pool.wait_ge(zeroed, 3)

            @block.scalar
            def _(act):
                for b2 in range(2):
                    for b4 in range(4):
                        act.dma_start(state[64 * b2:64 * b2 + 64, b4, :, 0:MDV],
                                      C_in[2 * b4 + b2].rearrange("h k v -> k h v")).then_inc(loads_done, 16)
                with nc.allow_non_contiguous_dma(reason="the normaliser's and stabiliser's few scalars"):
                    for b2 in range(2):
                        for b4 in range(4):
                            act.dma_start(state[64 * b2:64 * b2 + 64, b4, :, MDV:VW],
                                          I["state_n"][0, 2 * b4 + b2].rearrange("h (k u) -> k h u", u=1)
                                          ).then_inc(loads_done, 16)
                    act.dma_start(m_T[:], I["state_m"][0].rearrange("b h -> h b")).then_inc(loads_done, 16)
                for b in range(DEC_B):
                    act.dma_start(m_nat[DEC_S * b:DEC_S * b + DEC_S, :],
                                  I["state_m"][0, b].partition_broadcast(DEC_S)).then_inc(loads_done, 16)
                act.dma_start(bias[:, 0:MH], I["mlstm_b_i"][0].partition_broadcast(P)).then_inc(loads_done, 16)
                act.dma_start(bias[:, MH:2 * MH], I["mlstm_b_f"][0].partition_broadcast(P)).then_inc(loads_done, 16)
                act.dma_start(hn[:], I["mlstm_head_norm"][0].partition_broadcast(P)).then_inc(loads_done, 16)
                act.wait_ge(loads_done, 16 * 28)

        def v_dst(j):
            return lambda t: (v[0:TILES[t][1], t, 4 * j:4 * j + 4, 0:MDV], ACT.Copy, 1.0)

        def o_dst(j):
            return lambda t: (og[0:TILES[t][1], t, WB * j:WB * j + WB], ACT.Sigmoid, 1.0)

        o2, o3, o4 = 2 * MH * MDK, 2 * MH * MDK + D, 2 * MH * MDK + 2 * D
        project_stage(nc, "mp", M, w_in, [
            (0, WB, "T", lambda c: (q_T[:, c, :], ACT.Copy, 1.0)),
            (WB, WB, "T", lambda c: (k_T[:, c, :], ACT.Copy, MDK ** -0.5)),
            (o2, WB, "N", v_dst(0)), (o2 + WB, WB, "N", v_dst(1)),
            (o4, 2 * MH, "N", lambda t: (gates[0:TILES[t][1], t, :], ACT.Copy, 1.0)),
            (o3, WB, "N", o_dst(0)), (o3 + WB, WB, "N", o_dst(1))])

        with Stage(nc, "mr") as st:
            kn = st.sb("kn", [P, NT, MH, MDK])
            z = st.sb("z", [P, 4, NT, MH])
            lf = st.sb("lf", [P, NT, MH])
            li = st.sb("li", [P, NT, MH])
            b_cum = st.sb("b_cum", [P, NT, MH])
            g = st.sb("g", [P, NT, MH])
            g_T = st.sb("g_T", [MH, NT, P])
            top_T = st.sb("top_T", [MH, NT, P])
            ntop_T = st.sb("ntop_T", [MH, NT, P])
            top = st.sb("top", [P, NT, MH])
            m_prev = st.sb("m_prev", [P, NT, MH])
            m_all = st.sb("m_all", [P, NT, MH])
            m_end = st.sb("m_end", [MH, NT, P])
            zero_T = st.sb("zero_T", [MH, 1])
            w_all = st.sb("w_all", [P, 3, NT, MH])
            arg = st.sb("arg", [P, 3, NT, MH])
            dec = st.sb("dec", [P, 5, MH])
            kw = st.sb("kw", [P, NT, MH, MDK])
            kws = st.sb("kws", [NDEC, MH, DEC_B, MDK])
            qd = st.sb("qd", [P, MH, NDEC])
            qs = st.sb("qs", [P, MH, 4, NDEC])
            C = st.sb("C", [P, 4, VW])
            W = st.sb("W", [P, 2, P])
            PT = st.sb("PT", [P, 2, P])
            carry = st.sb("carry", [P, 2, VW])
            nd = st.sb("nd", [P, NT, MH, VW])
            fl = st.sb("fl", [P, 4, NT, MH])
            ps_a = st.ps("ps_a", [P, 512])
            ps_s = [st.ps(f"ps_s{i}", [P, 512]) for i in range(2)]
            ps_n = [st.ps(f"ps_n{i}", [P, 512]) for i in range(2)]
            ps_i = st.ps("ps_i", [P, 512])
            ps_c = [st.ps(f"ps_c{i}", [P, 2, VW]) for i in range(2)]
            vec, sca, ten = st.sem("vec"), st.sem("sca"), st.sem("ten")
            az_ready, l_ready = st.sem("az_ready"), st.sem("l_ready")
            gate_mm, gate_cp = st.sem("gate_mm"), st.sem("gate_cp")
            arg_ready, w_ready = st.sem("arg_ready"), st.sem("w_ready")
            kn_mm, kn_cp = st.sem("kn_mm"), st.sem("kn_cp")
            scored, weighed, probs = st.sem("scored"), st.sem("weighed"), st.sem("probs")
            summed, carried, joined = st.sem("summed"), st.sem("carried"), st.sem("joined")
            ms_ready, rt_ready = st.sem("ms_ready"), st.sem("rt_ready")
            out_done, prep = st.sem("out_done"), st.sem("prep")
            cm = {n: M.c(n) for n in ("tri", "tri_dec", "mask", "mask_dec", "sel_head", "last", "last_dec",
                                      "last_state", "seq_q", "seq_k")}
            tri = [cm["tri"], cm["tri"], cm["tri_dec"]]
            mask = [cm["mask"], cm["mask"], cm["mask_dec"]]
            last = [cm["last"], cm["last"], cm["last_dec"]]
            GP = 7

            with nc.Block() as block:

                @block.tensor
                def _(pe):
                    for t, (t0, n) in enumerate(TILES):
                        if t >= 1:
                            pe.wait_ge(kn_cp, t)
                        for c in range(4):
                            mm = pe.transpose(ps_i[0:n, c * P:(c + 1) * P], k_T[:, c, t0:t0 + n], M.ident[:, :])
                        mm.then_inc(kn_mm, 1)
                    for t, (t0, n) in enumerate(TILES):
                        def turn(k):
                            pe.wait_ge(gate_cp, GP * t + k + 1)

                        turn(0)
                        pe.matmul(ps_a[0:n, 0:MH], tri[t][0:n, 0:n], lf[0:n, t, :],
                                  start=True, stop=True).then_inc(gate_mm, 1)
                        turn(1)
                        pe.transpose(ps_a[0:MH, 0:n], g[0:n, t, :], M.ident[0:n, 0:n]).then_inc(gate_mm, 1)
                        turn(2)
                        pe.transpose(ps_a[0:n, 0:MH], top_T[:, t, 0:n], M.ident[0:MH, 0:MH]).then_inc(gate_mm, 1)
                        turn(3)
                        pe.matmul(ps_a[0:n, 0:MH], last[t][0:n, 0:n], top[0:n, t, :],
                                  start=True, stop=True).then_inc(gate_mm, 1)
                        turn(4)
                        pe.transpose(ps_a[0:MH, 0:n], m_all[0:n, t, :], M.ident[0:n, 0:n]).then_inc(gate_mm, 1)
                        turn(5)
                        pe.matmul(ps_a[0:n, 0:MH], last[t][0:n, 0:n], m_all[0:n, t, :],
                                  start=True, stop=True).then_inc(gate_mm, 1)
                        turn(6)
                        pe.wait_ge(w_ready, t + 1)
                        if t < 2:
                            mm = pe.matmul(ps_a[:, 0:MH], cm["last"], w_all[:, 0, t, :], start=True, stop=True)
                        else:
                            for b4 in range(4):
                                mm = pe.matmul(ps_a[:, b4 * MH:(b4 + 1) * MH], cm["last_state"][:, b4, :],
                                               w_all[0:n, 0, t, :], start=True, stop=True)
                        mm.then_inc(gate_mm, 1)
                        pe.wait_ge(gate_cp, GP * (t + 1))

                        def scores(h):
                            u = t * MH + h
                            hp, hb = h // 2, 64 * (h % 2)
                            if u >= 2:
                                pe.wait_ge(probs, u - 1)
                            pe.matmul(ps_s[u % 2][0:n, 0:n], k_T[hb:hb + MDK, hp, t0:t0 + n],
                                      q_T[hb:hb + MDK, hp, t0:t0 + n], start=True, stop=True)
                            pe.matmul(ps_s[u % 2][0:n, P:P + n], cm["sel_head"][:, h, 0:n], ntop_T[:, t, 0:n],
                                      start=True, stop=False)
                            pe.matmul(ps_s[u % 2][0:n, P:P + n], M.ident[0:n, 0:n], mask[t][0:n, 0:n],
                                      start=False, stop=True).then_inc(scored, 1)

                        scores(0)
                        for h in range(MH):
                            u = t * MH + h
                            hp, hb = h // 2, 64 * (h % 2)
                            if h + 1 < MH:
                                scores(h + 1)
                            pe.wait_ge(probs, u + 1)
                            if u >= 1:
                                pe.wait_ge(joined, u)
                            pe.wait_ge(prep, t + 1)
                            mm = pe.matmul(ps_n[u % 2][0:n, 0:VW], PT[0:n, u % 2, 0:n], v[0:n, t, h, :],
                                           start=True, stop=True)
                            if t == 1:
                                pe.matmul(ps_i[0:n, 0:VW], q_T[hb:hb + MDK, hp, t0:t0 + n], C[hb:hb + MDK, hp, :],
                                          start=True, stop=True)
                            if t == 2:
                                for b4 in range(4):
                                    pe.matmul(ps_i[0:n, 0:VW], qs[:, h, b4, :], state[:, b4, h, :],
                                              start=(b4 == 0), stop=(b4 == 3))
                                for b4 in range(4):
                                    mm = pe.matmul(ps_c[b4 // 2][:, b4 % 2, :],
                                                   kws[:, h, 2 * b4:2 * b4 + 2, :].rearrange("p b k -> p (b k)"),
                                                   v[0:n, t, h, :], start=True, stop=True)
                            else:
                                mm = pe.matmul(ps_c[0][hb:hb + MDK, 0, :], kw[0:n, t, h, :], v[0:n, t, h, :],
                                               start=True, stop=True)
                            mm.then_inc(summed, 1)

                def carry_of(act, t, h):
                    u, n = t * MH + h, TILES[t][1]
                    act.wait_ge(summed, u + 1)
                    act.wait_ge(joined, u - 1)
                    act.activation(carry[0:n, u % 2, :], ps_i[0:n, 0:VW], ACT.Copy,
                                   scale=w_all[0:n, 0, t, h:h + 1]).then_inc(carried, 1)

                @block.scalar
                def _(act):
                    step = Chain(act, sca)
                    act.wait_ge(az_ready, 1)
                    step(act.activation(z[:, 2], z[:, 1], ACT.Exp, scale=-1.0))
                    act.activation(z[:, 3], z[:, 2], ACT.Ln, bias=1.0).then_inc(l_ready, 1)
                    for t, (t0, n) in enumerate(TILES):
                        act.wait_ge(arg_ready, t + 1)
                        act.activation(w_all[0:n, :, t, :], arg[0:n, :, t, :], ACT.Exp).then_inc(w_ready, 1)
                        for h in range(MH):
                            u = t * MH + h
                            act.wait_ge(scored, u + 1)
                            if u >= 2:
                                act.wait_ge(probs, u - 1)
                            act.activation(W[0:n, u % 2, 0:n], ps_s[u % 2][0:n, P:P + n], ACT.Exp,
                                           bias=g[0:n, t, h:h + 1]).then_inc(weighed, 1)
                            if t >= 1 and h >= 1:
                                carry_of(act, t, h - 1)
                        if t >= 1:
                            carry_of(act, t, MH - 1)
                    act.wait_ge(ms_ready, 1)
                    act.activation(fl[:, 3], fl[:, 2], ACT.Sqrt).then_inc(rt_ready, 1)

                @block.vector
                def _(dve):
                    step = Chain(dve, vec)
                    for t, (t0, n) in enumerate(TILES):
                        dve.wait_ge(kn_mm, t + 1)
                        dve.tensor_copy(kn[0:n, t], ps_i[0:n, :].rearrange("p (h k) -> p h k", h=MH)
                                        ).then_inc(kn_cp, 1)
                    bcast = bias[:, None, 0:MH].to_broadcast([P, NT, MH])
                    bcast_f = bias[:, None, MH:2 * MH].to_broadcast([P, NT, MH])
                    step(dve.tensor_tensor(li[:], gates[:, :, 0:MH], bcast, ALU.add))
                    step(dve.tensor_tensor(z[:, 0], gates[:, :, MH:2 * MH], bcast_f, ALU.add))
                    step(dve.tensor_scalar(z[:, 1], z[:, 0], -1.0, None, ALU.mult))
                    step(dve.tensor_tensor(z[:, 1], z[:, 0], z[:, 1], ALU.max))
                    dve.nop().then_inc(az_ready, 1)
                    step(dve.tensor_scalar(z[:, 0], z[:, 0], 0.0, None, ALU.min))
                    dve.wait_ge(l_ready, 1)
                    step(dve.tensor_tensor(lf[:], z[:, 0], z[:, 3], ALU.subtract))
                    step(dve.memset(zero_T[:], 0.0))
                    step(dve.memset(m_prev[:, 0, :], 0.0))
                    step(dve.tensor_copy(m_prev[0:NDEC, 2, :], m_nat[:]))
                    step(dve.memset(nd[:, 2], 1.0))
                    step(dve.memset(w_all[:], 1.0))
                    for hp in range(4):
                        for h2 in range(2):
                            for b2 in range(2):
                                step(dve.tensor_copy(qd[64 * b2:64 * b2 + 64, 2 * hp + h2, :],
                                                     q_T[64 * h2:64 * h2 + 64, hp, SEQ:NTOK]))
                    for h in range(MH):
                        step(dve.tensor_tensor(qs[:, h], qd[:, h, None, :].to_broadcast([P, 4, NDEC]),
                                               cm["seq_q"], ALU.mult))
                    dve.nop().then_inc(gate_cp, 1)
                    for t, (t0, n) in enumerate(TILES):
                        mm = GP * t
                        if t >= 1:
                            dve.nop().then_inc(gate_cp, 1)
                        dve.wait_ge(gate_mm, mm + 1)
                        step(dve.tensor_copy(b_cum[0:n, t], ps_a[0:n, 0:MH]))
                        step(dve.tensor_tensor(g[0:n, t], li[0:n, t], b_cum[0:n, t], ALU.subtract))
                        dve.nop().then_inc(gate_cp, 1)
                        dve.wait_ge(gate_mm, mm + 2)
                        step(dve.tensor_copy(g_T[:, t, 0:n], ps_a[0:MH, 0:n]))
                        if t < 2:
                            start = zero_T[:] if t == 0 else m_end[:, 0, P - 1:P]
                            step(dve.tensor_tensor_scan(top_T[:, t, :], g_T[:, t, :], g_T[:, t, :], start,
                                                        ALU.max, ALU.max))
                        else:
                            gs = g_T[:, t, 0:n].rearrange("p (b s) -> p b s", s=DEC_S)
                            ts = top_T[:, t, 0:n].rearrange("p (b s) -> p b s", s=DEC_S)
                            for s in range(DEC_S):
                                before = m_T[:] if s == 0 else ts[:, :, s - 1]
                                step(dve.tensor_tensor(ts[:, :, s], gs[:, :, s], before, ALU.max))
                        step(dve.tensor_scalar(ntop_T[:, t, 0:n], top_T[:, t, 0:n], -1.0, None, ALU.mult))
                        dve.nop().then_inc(gate_cp, 1)
                        dve.wait_ge(gate_mm, mm + 3)
                        step(dve.tensor_copy(top[0:n, t], ps_a[0:n, 0:MH]))
                        step(dve.tensor_tensor(m_all[0:n, t], top[0:n, t], b_cum[0:n, t], ALU.add))
                        dve.nop().then_inc(gate_cp, 1)
                        dve.wait_ge(gate_mm, mm + 4)
                        step(dve.tensor_tensor(arg[0:n, 1, t], g[0:n, t], ps_a[0:n, 0:MH], ALU.subtract))
                        step(dve.tensor_tensor(arg[0:n, 0, t], m_prev[0:n, t], top[0:n, t], ALU.subtract))
                        step(dve.tensor_scalar(arg[0:n, 2, t], m_all[0:n, t], -1.0, None, ALU.mult))
                        dve.nop().then_inc(arg_ready, 1)
                        dve.nop().then_inc(gate_cp, 1)
                        dve.wait_ge(gate_mm, mm + 5)
                        step(dve.tensor_copy(m_end[:, t, 0:n], ps_a[0:MH, 0:n]))
                        dve.nop().then_inc(gate_cp, 1)
                        dve.wait_ge(gate_mm, mm + 6)
                        if t == 0:
                            step(dve.tensor_copy(m_prev[:, 1, :], ps_a[:, 0:MH]))
                        dve.nop().then_inc(gate_cp, 1)
                        dve.wait_ge(gate_mm, mm + 7)
                        if t < 2:
                            step(dve.tensor_copy(dec[:, 0, :], ps_a[:, 0:MH]))
                        else:
                            step(dve.tensor_copy(dec[:, 1:5, :], ps_a[:, 0:4 * MH].rearrange("p (b h) -> p b h", b=4)))
                        dve.wait_ge(w_ready, t + 1)
                        step(dve.tensor_tensor(kw[0:n, t], kn[0:n, t],
                                               w_all[0:n, 1, t, :, None].to_broadcast([n, MH, MDK]), ALU.mult))
                        if t == 2:
                            for h in range(MH):
                                step(dve.tensor_tensor(kws[:, h], kw[0:n, t, h, None, :].to_broadcast([n, DEC_B, MDK]),
                                                       cm["seq_k"][:, :, None].to_broadcast([n, DEC_B, MDK]),
                                                       ALU.mult))
                        dve.nop().then_inc(prep, 1)
                        if t < 2:
                            dve.wait_ge(vec, step.n)
                        dve.nop().then_inc(gate_cp, 1) if False else None
                        for h in range(MH):
                            u = t * MH + h
                            hp, hb = h // 2, 64 * (h % 2)
                            dve.wait_ge(weighed, u + 1)
                            if u >= 2:
                                dve.wait_ge(summed, u - 1)
                            dve.tensor_tensor(PT[0:n, u % 2, 0:n], ps_s[u % 2][0:n, 0:n], W[0:n, u % 2, 0:n],
                                              ALU.mult).then_inc(probs, 1)
                            dve.wait_ge(summed, u + 1)
                            if t == 0:
                                step(dve.tensor_copy(C[hb:hb + MDK, hp, :], ps_c[0][hb:hb + MDK, 0, :]))
                                dve.tensor_copy(nd[0:n, t, h, :], ps_n[u % 2][0:n, 0:VW]).then_inc(joined, 1)
                            else:
                                if t == 1:
                                    step(dve.scalar_tensor_tensor(
                                        out=C[hb:hb + MDK, hp, :], in0=C[hb:hb + MDK, hp, :],
                                        scalar=dec[hb:hb + MDK, 0, h:h + 1], in1=ps_c[0][hb:hb + MDK, 0, :],
                                        op0=ALU.mult, op1=ALU.add))
                                else:
                                    for b4 in range(4):
                                        step(dve.scalar_tensor_tensor(
                                            out=state[:, b4, h, :], in0=state[:, b4, h, :],
                                            scalar=dec[:, 1 + b4, h:h + 1], in1=ps_c[b4 // 2][:, b4 % 2, :],
                                            op0=ALU.mult, op1=ALU.add))
                                dve.wait_ge(carried, (t - 1) * MH + h + 1)
                                dve.tensor_tensor(nd[0:n, t, h, :], ps_n[u % 2][0:n, 0:VW], carry[0:n, u % 2, :],
                                                  ALU.add).then_inc(joined, 1)
                    dve.wait_ge(joined, NT * MH)
                    den = nd[:, :, :, MDV]
                    step(dve.tensor_scalar(fl[:, 0], den, -1.0, None, ALU.mult))
                    step(dve.tensor_tensor(fl[:, 0], fl[:, 0], den, ALU.max))
                    step(dve.tensor_tensor(fl[:, 0], fl[:, 0], w_all[:, 2], ALU.max))
                    step(dve.reciprocal(fl[:, 1], fl[:, 0]))
                    hv = hid[:].rearrange("p t (h v) -> p t h v", h=MH)
                    for t in range(NT):
                        step(dve.tensor_tensor(hv[:, t], nd[:, t, :, 0:MDV],
                                               fl[:, 1, t, :, None].to_broadcast([P, MH, MDV]), ALU.mult))
                        step(dve.tensor_tensor(nd[:, t, :, 0:MDV], hv[:, t], hv[:, t], ALU.mult))
                        step(dve.tensor_reduce(fl[:, 0, t], nd[:, t, :, 0:MDV], AX.X, ALU.add))
                    dve.tensor_scalar(fl[:, 2], fl[:, 0], 1.0 / MDV, EPS, ALU.mult, ALU.add).then_inc(ms_ready, 1)
                    dve.wait_ge(rt_ready, 1)
                    step(dve.reciprocal(fl[:, 1], fl[:, 3]))
                    for t in range(NT):
                        step(dve.tensor_tensor(hv[:, t], hv[:, t],
                                               fl[:, 1, t, :, None].to_broadcast([P, MH, MDV]), ALU.mult))
                        step(dve.tensor_tensor(hid[:, t], hid[:, t], hn[:], ALU.mult))
                        step(dve.tensor_tensor(hid[:, t], hid[:, t], og[:, t], ALU.mult))

                @block.sync
                def _(sp):
                    sp.wait_ge(joined, NT * MH)
                    for b2 in range(2):
                        sp.dma_start(O["C_p"][0, 0].rearrange("(a b) k v -> b k a v", b=2)[b2],
                                     C[64 * b2:64 * b2 + 64, :, 0:MDV]).then_inc(out_done, 16)
                        for b4 in range(4):
                            sp.dma_start(O["C_s"][0, 2 * b4 + b2].rearrange("h k v -> k h v"),
                                         state[64 * b2:64 * b2 + 64, b4, :, 0:MDV]).then_inc(out_done, 16)
                    with nc.allow_non_contiguous_dma(reason="the normaliser's and stabiliser's few scalars"):
                        for b2 in range(2):
                            sp.dma_start(O["n_p"][0, 0].rearrange("(a b) (k u) -> b k a u", b=2, u=1)[b2],
                                         C[64 * b2:64 * b2 + 64, :, MDV:VW]).then_inc(out_done, 16)
                            for b4 in range(4):
                                sp.dma_start(O["n_s"][0, 2 * b4 + b2].rearrange("h (k u) -> k h u", u=1),
                                             state[64 * b2:64 * b2 + 64, b4, :, MDV:VW]).then_inc(out_done, 16)
                        sp.dma_start(O["m_p"][0, 0].rearrange("(h u) -> h u", u=1), m_end[:, 1, P - 1:P]
                                     ).then_inc(out_done, 16)
                        sp.dma_start(O["m_s"][0].rearrange("b h -> h b"),
                                     m_end[:, 2, DEC_S - 1:NDEC:DEC_S]).then_inc(out_done, 16)
                    sp.wait_ge(out_done, 16 * 22)

        turn_stage(nc, "mt", M, hid)
        project_stage(nc, "mo", M, I["mlstm_w_out"][0], add_jobs())


GRP = 4
COLS = [P, P, P // 4]
TURNS = [c // (2 * GRP) for c in COLS]
NCOL = sum(COLS)


def top16(dve, vec, values, work, top, index, groups):
    n0 = vec[1]
    steps = (
        lambda k: dve.max(top[k][:, 0:8], values[k]),
        lambda k: dve.max_index(index[k][:, 0:8], top[k][:, 0:8], values[k]),
        lambda k: dve.match_replace(work[k], top[k][:, 0:8], values[k], NEG),
        lambda k: dve.max(top[k][:, 8:16], work[k]),
        lambda k: dve.max_index(index[k][:, 8:16], top[k][:, 8:16], work[k]),
    )
    for s, make in enumerate(steps):
        for k in range(groups):
            if s:
                dve.wait_ge(vec[0], n0 + (s - 1) * groups + k + 1)
            make(k).then_inc(vec[0], 1)
    vec[1] = n0 + len(steps) * groups


def peer_stage(nc, name, M, I, layer):
    HH = 2 * PH
    with Stage(nc, name) as outer:
        h = outer.sb("h", [P, NT, D])
        idx = outer.sb("idx", [P, NCOL], U32)
        gate = outer.sb("gate", [P, NCOL])
        cleared = outer.sem("cleared")
        with nc.Block() as block:

            @block.gpsimd
            def _(pool):
                pool.memset(h[:, NT - 1, :], 0.0).then_inc(cleared, 1)
                pool.wait_ge(cleared, 1)

        norm_stage(nc, name + "n", M, I["norm_ffn"][layer], keep=h)

        with Stage(nc, name + "r") as route:
            q_T = route.sb("q_T", [P, HH, NTOK])
            keys = route.sb("keys", [P, HH, P])
            keys_T = route.sb("keys_T", [P, HH, P])
            keys_in = route.sem("keys_in")
            keys_turned, keys_copied = route.sem("keys_turned"), route.sem("keys_copied")
            jobs = [(WB * j, WB, "T", (lambda j: lambda c: (q_T[:, 4 * j + c, :], ACT.Copy, 1.0))(j))
                    for j in range(HH // 4)]
            with nc.Block() as block:

                @block.gpsimd
                def _(pool):
                    pool.dma_start(keys[:], I["peer_sub_keys"][layer].rearrange("h s k d -> k (h s) d")
                                   ).then_inc(keys_in, 16)
                    pool.wait_ge(keys_in, 16)

            project_stage(nc, name + "q", M, I["peer_w_q"][layer], jobs)

            with Stage(nc, name + "s") as st:
                sc = st.sb("sc", [P, 2, HH, P])
                work = st.sb("work", [P, HH, P])
                v = st.sb("v", [P, HH, PTOP])
                ix = st.sb("ix", [P, HH, PTOP], U32)
                ixf = st.sb("ixf", [P, HH, PTOP])
                cand = st.sb("cand", [P, PH, PTOP * PTOP])
                cwork = st.sb("cwork", [P, PH, PTOP * PTOP])
                vals = st.sb("vals", [P, PH, PTOP])
                ci = st.sb("ci", [P, PH, PTOP], U32)
                half = st.sb("half", [P, 2, PH, PTOP], U32)
                halff = st.sb("halff", [P, 2, PH, PTOP])
                hot = st.sb("hot", [P, PH, PTOP, PTOP])
                part = st.sb("part", [P, 3, PH, PTOP])
                ids = st.sb("ids", [P, PH * PTOP], U32)
                gt = st.sb("gt", [P, PH, PTOP])
                tot = st.sb("tot", [P, 2, PH])
                ps = [st.ps(f"ps{i}", [P, 4, P]) for i in range(8)]
                vecs = st.sem("vecs")
                scored, copied = st.sem("scored"), st.sem("copied")
                shifted, expd, used = st.sem("shifted"), st.sem("expd"), st.sem("used")
                iota = M.c("iota16")
                QG = HH // 4
                with nc.Block() as block:

                    @block.tensor
                    def _(pe):
                        for k in range(QG):
                            for c in range(4):
                                mm = pe.transpose(ps[k][:, c, :], keys[:, 4 * k + c, :], M.ident)
                            mm.then_inc(keys_turned, 1)
                        pe.wait_ge(keys_copied, QG)
                        for t, (t0, n) in enumerate(TILES):
                            for k in range(QG):
                                q = t * QG + k
                                if q >= 4:
                                    pe.wait_ge(copied, q - 3)
                                for c in range(4):
                                    hh = 4 * k + c
                                    mm = pe.matmul(ps[4 + q % 4][0:n, c, :], q_T[:, hh, t0:t0 + n], keys_T[:, hh, :],
                                                   start=True, stop=True)
                                mm.then_inc(scored, 1)

                    def softmax(act, t):
                        n = TILES[t][1]
                        act.wait_ge(shifted, t + 1)
                        act.activation(gt[0:n], gt[0:n], ACT.Exp).then_inc(expd, 1)

                    @block.scalar
                    def _(act):
                        for k in range(QG):
                            act.wait_ge(keys_turned, k + 1)
                            act.activation(keys_T[:, 4 * k:4 * k + 4, :], ps[k][:], ACT.Copy).then_inc(keys_copied, 1)
                        for t, (t0, n) in enumerate(TILES):
                            if t >= 2:
                                act.wait_ge(used, t - 1)
                            for k in range(QG):
                                q = t * QG + k
                                act.wait_ge(scored, q + 1)
                                act.activation(sc[0:n, t % 2, 4 * k:4 * k + 4, :], ps[4 + q % 4][0:n], ACT.Copy
                                               ).then_inc(copied, 1)
                            if t >= 1:
                                softmax(act, t - 1)
                        softmax(act, NT - 1)

                    @block.vector
                    def _(dve):
                        vec = [vecs, 0]

                        def step(ins):
                            vec[1] += 1
                            ins.then_inc(vecs, 1)
                            dve.wait_ge(vecs, vec[1])

                        for t, (t0, n) in enumerate(TILES):
                            dve.wait_ge(copied, (t + 1) * QG)
                            top16(dve, vec, [sc[0:n, t % 2, k, :] for k in range(HH)],
                                  [work[0:n, k, :] for k in range(HH)], [v[0:n, k, :] for k in range(HH)],
                                  [ix[0:n, k, :] for k in range(HH)], HH)
                            dve.wait_ge(vecs, vec[1])
                            dve.nop().then_inc(used, 1)
                            step(dve.tensor_copy(ixf[0:n], ix[0:n]))
                            vv = v[0:n].rearrange("p (h s) k -> p h s k", s=2)
                            iv = ixf[0:n].rearrange("p (h s) k -> p h s k", s=2)
                            full = [n, PH, PTOP, PTOP]
                            step(dve.tensor_tensor(cand[0:n].rearrange("p h (a b) -> p h a b", a=PTOP),
                                                   vv[:, :, 0, :, None].to_broadcast(full),
                                                   vv[:, :, 1, None, :].to_broadcast(full), ALU.add))
                            top16(dve, vec, [cand[0:n, k, :] for k in range(PH)], [cwork[0:n, k, :] for k in range(PH)],
                                  [vals[0:n, k, :] for k in range(PH)], [ci[0:n, k, :] for k in range(PH)], PH)
                            dve.wait_ge(vecs, vec[1])
                            dve.tensor_tensor(gt[0:n], vals[0:n], vals[0:n, :, 0:1].to_broadcast([n, PH, PTOP]),
                                              ALU.subtract).then_inc(shifted, 1)
                            step(dve.tensor_scalar(half[0:n, 0], ci[0:n], 4, None, ALU.logical_shift_right))
                            step(dve.tensor_scalar(half[0:n, 1], ci[0:n], PTOP - 1, None, ALU.bitwise_and))
                            step(dve.tensor_copy(halff[0:n], half[0:n]))
                            for s in range(2):
                                step(dve.tensor_tensor(hot[0:n], halff[0:n, s, :, :, None].to_broadcast(full),
                                                       iota[0:n, None, None, :].to_broadcast(full), ALU.is_equal))
                                step(dve.tensor_tensor(hot[0:n], hot[0:n],
                                                       iv[:, :, s, None, :].to_broadcast(full), ALU.mult))
                                step(dve.tensor_reduce(part[0:n, s], hot[0:n], AX.X, ALU.add))
                            step(dve.scalar_tensor_tensor(out=part[0:n, 2], in0=part[0:n, 0], scalar=float(PK),
                                                          in1=part[0:n, 1], op0=ALU.mult, op1=ALU.add))
                            flat = part[0:n, 2].rearrange("p h k -> p (h k)")
                            c0 = sum(COLS[:t])
                            dve.wait_ge(expd, t + 1)
                            step(dve.tensor_reduce(tot[0:n, 0], gt[0:n], AX.X, ALU.add))
                            step(dve.reciprocal(tot[0:n, 1], tot[0:n, 0]))
                            step(dve.tensor_tensor(gt[0:n], gt[0:n],
                                                   tot[0:n, 1, :, None].to_broadcast([n, PH, PTOP]), ALU.mult))
                            gflat = gt[0:n].rearrange("p h k -> p (h k)")
                            if t < 2:
                                step(dve.tensor_copy(idx[:, c0:c0 + P], flat))
                                step(dve.tensor_copy(gate[:, c0:c0 + P], gflat))
                            else:
                                for j in range(4):
                                    c = COLS[2]
                                    step(dve.tensor_copy(idx[32 * j:32 * j + 32, c0:c0 + c], flat[:, c * j:c * j + c]))
                                    step(dve.tensor_copy(gate[32 * j:32 * j + 32, c0:c0 + c], gflat[:, c * j:c * j + c]))
                                for j in range(1, 4):
                                    step(dve.tensor_copy(h[32 * j:32 * j + 32, 2, :], h[0:32, 2, :]))

        with Stage(nc, name + "g") as st:
            u = st.sb("u", [P, 2 * GRP, D])
            vrow = st.sb("vrow", [P, 2 * GRP, D])
            cur = st.sb("cur", [P, 2, GRP], U32)
            dot = st.sb("dot", [P, 2, GRP])
            gelu = st.sb("gelu", [P, 2, GRP])
            w = st.sb("w", [P, 2, GRP])
            diag = st.sb("diag", [P, 2 * GRP, P])
            zero = st.sb("zero", [P, P])
            acc = [st.ps(f"acc{t}", [P, 2, 512]) for t in range(NT)]
            zeroed = st.sem("zeroed")
            cur_ready = st.sem("cur_ready")
            u_in = [st.sem(f"u_in{i}") for i in range(2)]
            v_in = [st.sem(f"v_in{i}") for i in range(2)]
            dotted, gelu_ready, w_ready = st.sem("dotted"), st.sem("gelu_ready"), st.sem("w_ready")
            diag_ready, applied, closed, added = st.sem("diag_ready"), st.sem("applied"), st.sem("closed"), st.sem("added")
            total = sum(TURNS)
            tables = (I["peer_u"][layer], I["peer_v"][layer])
            starts = [sum(TURNS[:t]) for t in range(NT)]
            off = layer * PK * PK * D
            with nc.Block() as block:

                @block.gpsimd
                def _(pool):
                    with pool.Fori(0, total) as i:
                        for s in range(2):
                            pool.wait_ge(dotted, 2 * i + s + 1)
                            pool.wait_ge(applied, 2 * i + s + 1)
                            pool.tensor_copy(cur[:, s, :], idx[:, bass.ds((2 * i + s) * GRP, GRP)]).then_inc(cur_ready, 1)
                            pool.wait_ge(dotted, 1)
                            pool.wait_ge(cur_ready, 2 * i + s + 1)
                            for k in range(GRP):
                                pool.indirect_dma_start(u[:, s * GRP + k, :], None, I["peer_u"].rearrange("l e d -> (l e) d"),
                                                        bass.IndirectOffsetOnAxis(ap=cur[:, s, k:k + 1], axis=0),
                                                        element_offset=off).then_inc(u_in[s], 16)
                            for k in range(GRP):
                                pool.indirect_dma_start(vrow[:, s * GRP + k, :], None, I["peer_v"].rearrange("l e d -> (l e) d"),
                                                        bass.IndirectOffsetOnAxis(ap=cur[:, s, k:k + 1], axis=0),
                                                        element_offset=off).then_inc(v_in[s], 16)

                @block.vector
                def _(dve):
                    dve.memset(zero[:], 0.0).then_inc(zeroed, 1)
                    dve.nop().then_inc(dotted, 2)
                    for t in range(NT):
                        with dve.Fori(starts[t], starts[t] + TURNS[t]) as i:
                            for s in range(2):
                                dve.wait_ge(u_in[s], (i + 1) * (16 * GRP))
                                for k in range(GRP):
                                    row = u[:, s * GRP + k, :]
                                    ins = dve.tensor_tensor_reduce(row, row, h[:, t, :], 1.0, 0.0, ALU.mult, ALU.add,
                                                                   dot[:, s, k:k + 1])
                                ins.then_inc(dotted, 1)
                                dve.wait_ge(gelu_ready, 2 * i + s + 1)
                                dve.tensor_tensor(w[:, s, :], gelu[:, s, :], gate[:, bass.ds((2 * i + s) * GRP, GRP)],
                                                  ALU.mult).then_inc(w_ready, 1)
                    for t, (_, n) in enumerate(TILES):
                        dve.wait_ge(closed, t + 1)
                        dve.tensor_tensor(M.x[0:n, t, :].rearrange("p (a b) -> p a b", a=2), acc[t][0:n],
                                          M.x[0:n, t, :].rearrange("p (a b) -> p a b", a=2), ALU.add
                                          ).then_inc(added, 1)

                @block.scalar
                def _(act):
                    for t in range(NT):
                        base = M.ident if t < 2 else M.c("stack32")
                        n = TILES[t][1]
                        with act.Fori(starts[t], starts[t] + TURNS[t]) as i:
                            for s in range(2):
                                act.wait_ge(dotted, 2 * i + s + 3)
                                act.activation(gelu[:, s, :], dot[:, s, :], ACT.Gelu).then_inc(gelu_ready, 1)
                                act.wait_ge(w_ready, 2 * i + s + 1)
                                act.wait_ge(applied, 2 * i + s + 1)
                                for k in range(GRP):
                                    ins = act.activation(diag[:, s * GRP + k, 0:n], base, ACT.Copy,
                                                         scale=w[:, s, k:k + 1])
                                ins.then_inc(diag_ready, 1)

                @block.tensor
                def _(pe):
                    pe.wait_ge(zeroed, 1)
                    for t, (_, n) in enumerate(TILES):
                        for a in range(2):
                            mm = pe.matmul(acc[t][0:n, a, :], zero[:, 0:n], h[:, 0, 0:512], start=True, stop=False,
                                           skip_group_check=True)
                            if t == 0:
                                mm.then_inc(applied, 1)
                    for t, (_, n) in enumerate(TILES):
                        with pe.Fori(starts[t], starts[t] + TURNS[t]) as i:
                            for s in range(2):
                                pe.wait_ge(diag_ready, 2 * i + s + 1)
                                pe.wait_ge(v_in[s], (i + 1) * (16 * GRP))
                                for k in range(GRP):
                                    for a in range(2):
                                        mm = pe.matmul(acc[t][0:n, a, :], diag[:, s * GRP + k, 0:n],
                                                       vrow[:, s * GRP + k, a * 512:a * 512 + 512],
                                                       start=False, stop=False, skip_group_check=True)
                                mm.then_inc(applied, 1)
                        for a in range(2):
                            mm = pe.matmul(acc[t][0:n, a, :], zero[:, 0:n], h[:, 0, 0:512], start=False, stop=True,
                                           skip_group_check=True)
                        mm.then_inc(closed, 1)


KEY_ROWS = PAST // CSTR
N_CMP = KEY_ROWS - 1
SUBW = CSTR * 2 * AG * ADH
GD = AG * ADH
NPC = SEQ // CSTR - 1


def nsa_stage(nc, M, I, O):
    o_dec = nc.dram_tensor("o_dec_scratch", [3, NDEC, D], F32, kind="Internal").ap()
    with Stage(nc, "na") as outer:
        q = outer.sb("q", [P, NT, D])
        kv = outer.sb("kv", [P, NT, 3, 2, GD])
        gate = outer.sb("gate", [P, NT, AH, 3])
        q_T = outer.sb("q_T", [P, 2, AR, NTOK])
        k_T = outer.sb("k_T", [P, 2, 2, NTOK])
        row_idx = outer.sb("row_idx", [P, DEC_B], U32)
        cmp_kT = outer.sb("cmp_kT", [P, DEC_B, 2, KEY_ROWS])
        cmp_v = outer.sb("cmp_v", [P, DEC_B, GD])
        pcmp_kT = outer.sb("pcmp_kT", [P, 2, KEY_ROWS])
        pcmp_v = outer.sb("pcmp_v", [P, GD])
        norm_stage(nc, "nn", M, I["norm_mix"][1])
        by_head = q[:].rearrange("p t (a r g d) -> p t a g r d", a=2, r=AR, g=2)
        jobs = [(a * WB, WB, "N", (lambda a: lambda t: (by_head[0:TILES[t][1], t, a], ACT.Copy, 1.0))(a))
                for a in range(2)]
        for br in range(3):
            jobs.append((AQW + br * 2 * GD, WB, "N", (lambda br: lambda t: (
                kv[0:TILES[t][1], t, br].rearrange("p c g -> p (c g)"), ACT.Copy, 1.0))(br)))
        jobs.append((AQW + AKVW, 3 * AH, "N", lambda t: (
            gate[0:TILES[t][1], t].rearrange("p h b -> p (h b)"), ACT.Copy, 1.0)))
        project_stage(nc, "np", M, I["nsa_w_in"][0], jobs)
        rotate_stage(nc, M, I, O, q, kv, gate, q_T, k_T, row_idx)
        compress_stage(nc, M, I, O, row_idx, cmp_kT, cmp_v, pcmp_kT, pcmp_v)
        prompt_stage(nc, M, q, kv, gate, q_T, k_T, pcmp_kT, pcmp_v)
        with Stage(nc, "nd") as st:
            q_blk = st.sb("q_blk", [P, DEC_B, 2, 2 * AR * DEC_S])
            block_mask = st.sb("block_mask", [P, 4, PAST // SBLK])
            group_one = M.c("group_one")
            blocks_stage(nc, M, q_T, q_blk, cmp_kT, cmp_v, block_mask, o_dec[0])
            decode_stage(nc, M, "ds", q_blk, k_T[:, 0], kv[0:NDEC, NT - 1, 1, 1], CSTR, o_dec[1], block_mask,
                         rows=I["cache_sel_kv"][0].rearrange("a (n l) c g d -> (a n) (l c g d)", l=CSTR),
                         row_idx=row_idx)
            decode_stage(nc, M, "dw", q_blk, k_T[:, 1], kv[0:NDEC, NT - 1, 2, 1], WIN // P, o_dec[2], None,
                         rows=I["state_win_kv"][0], row_idx=None)
        mix_stage(nc, M, q, gate, o_dec)
        turn_stage(nc, "nt", M, q)
        project_stage(nc, "no", M, I["nsa_w_out"][0], add_jobs())


def rotate_stage(nc, M, I, O, q, kv, gate, q_T, k_T, row_idx):
    with Stage(nc, "rt") as st:
        b_gate = st.sb("b_gate", [P, AH, 3])
        tmp = st.sb("tmp", [P, 4, AH, ROT // 2])
        pages = st.sb("pages", [NPAGE, DEC_B], I32)
        pages_f = st.sb("pages_f", [NPAGE, DEC_B])
        tr = [st.ps(f"tr{i}", [P, 4, P]) for i in range(4)]
        ps_rows = st.ps("ps_rows", [P, DEC_B])
        loaded, vec = st.sem("loaded"), st.sem("vec")
        biased, gated, rotated = st.sem("biased"), st.sem("gated"), st.sem("rotated")
        pages_ready, rows_ready = st.sem("pages_ready"), st.sem("rows_ready")
        turned, copied, out_done = st.sem("turned"), st.sem("copied"), st.sem("out_done")
        half = ROT // 2
        cos, sin = M.c("cos"), M.c("sin")
        qh = q[:].rearrange("p t (h d) -> p t h d", h=AH)
        kvh = kv[:].rearrange("p t b c (g d) -> p t b c g d", g=AG)
        with nc.Block() as block:

            @block.scalar
            def _(act):
                act.dma_start(b_gate[:], I["nsa_b_gate"][0].partition_broadcast(P)).then_inc(loaded, 16)
                with nc.allow_non_contiguous_dma(reason="128 page numbers"):
                    act.dma_start(pages[:], I["page_table"].rearrange("b k -> k b")).then_inc(loaded, 16)
                for t, (_, n) in enumerate(TILES):
                    act.wait_ge(biased, t + 1)
                    act.activation(gate[0:n, t], gate[0:n, t], ACT.Sigmoid).then_inc(gated, 1)
                for t, (t0, n) in enumerate(TILES):
                    for k in range(3):
                        act.wait_ge(turned, 3 * t + k + 1)
                        dst = q_T[:, k, :, t0:t0 + n] if k < 2 else (
                            k_T[:, :, :, t0:t0 + n].rearrange("p b a t -> p (b a) t"))
                        act.activation(dst, tr[(3 * t + k) % 4][:, :, 0:n], ACT.Copy,
                                       scale=ADH ** -0.5 if k < 2 else 1.0).then_inc(copied, 1)

            @block.vector
            def _(dve):
                step = Chain(dve, vec)
                dve.wait_ge(loaded, 32)
                dve.tensor_copy(pages_f[:], pages[:]).then_inc(pages_ready, 1)
                for t, (_, n) in enumerate(TILES):
                    dve.tensor_tensor(gate[0:n, t], gate[0:n, t], b_gate[0:n], ALU.add).then_inc(biased, 1)
                for t, (_, n) in enumerate(TILES):
                    places = [qh[0:n, t]] + [kvh[0:n, t, br, 0] for br in range(3)]
                    for x in places:
                        heads = x.shape[1]
                        full = [n, heads, half]
                        c = cos[0:n, t, None, :].to_broadcast(full)
                        s = sin[0:n, t, None, :].to_broadcast(full)
                        x1, x2 = x[:, :, 0:half], x[:, :, half:ROT]
                        tt = [tmp[0:n, i, 0:heads] for i in range(4)]
                        step(dve.tensor_tensor(tt[0], x1, c, ALU.mult))
                        step(dve.tensor_tensor(tt[1], x2, s, ALU.mult))
                        step(dve.tensor_tensor(tt[2], x2, c, ALU.mult))
                        step(dve.tensor_tensor(tt[3], x1, s, ALU.mult))
                        step(dve.tensor_tensor(x1, tt[0], tt[1], ALU.subtract))
                        step(dve.tensor_tensor(x2, tt[2], tt[3], ALU.add))
                    dve.nop().then_inc(rotated, 1)
                dve.wait_ge(rows_ready, 1)
                dve.scalar_tensor_tensor(out=row_idx[:], in0=ps_rows[:], scalar=float(PAGE // CSTR),
                                         in1=M.c("pos16")[:, 0:DEC_B], op0=ALU.mult, op1=ALU.add).then_inc(vec, 1)

            @block.tensor
            def _(pe):
                pe.wait_ge(pages_ready, 1)
                pe.matmul(ps_rows[:], M.c("page_rep"), pages_f[:], start=True, stop=True).then_inc(rows_ready, 1)
                for t, (t0, n) in enumerate(TILES):
                    pe.wait_ge(rotated, t + 1)
                    for k in range(3):
                        e = 3 * t + k
                        if e >= 4:
                            pe.wait_ge(copied, e - 3)
                        for r in range(4):
                            if k < 2:
                                src = q[0:n, t, (k * AR + r) * P:(k * AR + r + 1) * P]
                            else:
                                src = kv[0:n, t, 1 + r // 2, 0, (r % 2) * P:(r % 2) * P + P]
                            mm = pe.transpose(tr[e % 4][:, r, 0:n], src, M.ident[0:n, 0:n])
                        mm.then_inc(turned, 1)

            @block.sync
            def _(sp):
                def flat(ap):
                    return ap.rearrange("s c g d -> s (c g d)")

                def rows(t, n, br):
                    return kv[0:n, t, br].rearrange("p c g -> p (c g)")

                sp.dma_start(O["win_s"][0, :, 0:WIN - DEC_S], I["state_win_kv"][0, :, DEC_S:WIN]).then_inc(out_done, 16)
                for t in range(2):
                    sp.wait_ge(rotated, t + 1)
                    for br, name in enumerate(("cmp_p", "sel_p", "win_p")):
                        sp.dma_start(flat(O[name][0, 0, t * P:(t + 1) * P]), rows(t, P, br)).then_inc(out_done, 16)
                sp.wait_ge(rotated, 3)
                for br, name in enumerate(("cmp_s", "sel_s")):
                    sp.dma_start(O[name][0].rearrange("b s c g d -> (b s) (c g d)"), rows(2, NDEC, br)).then_inc(out_done, 16)
                for b in range(DEC_B):
                    sp.dma_start(flat(O["win_s"][0, b, WIN - DEC_S:WIN]),
                                 kv[DEC_S * b:DEC_S * b + DEC_S, 2, 2].rearrange("p c g -> p (c g)")).then_inc(out_done, 16)
                sp.wait_ge(out_done, 16 * 17)


def compress_stage(nc, M, I, O, row_idx, cmp_kT, cmp_v, pcmp_kT, pcmp_v):
    NL = CSTR // 2
    GK = 2 * NL
    with Stage(nc, "cp") as st:
        rows = st.sb("rows", [P, 2, SUBW])
        cur = st.sb("cur", [P, 2], U32)
        w1 = st.sb("w1", [P, 2, 2, NL, ADH])
        w1h = st.sb("w1h", [P, 2, NL, 2, ADH])
        w2 = st.sb("w2", [ADH, 2, ADH])
        b1 = st.sb("b1", [ADH, 2])
        sub_T = st.sb("sub_T", [P, 4, 4, P])
        second = st.sb("second", [ADH, 2, AG, P])
        pre = st.sb("pre", [ADH, 2, AG, P])
        hid = st.sb("hid", [ADH, 2, AG, P])
        tr = [st.ps(f"tr{i}", [P, 4, P]) for i in range(4)]
        ps_h = [st.ps(f"ps_h{i}", [P, AG, P]) for i in range(2)]
        ps_k = st.ps("ps_k", [P, 2, P])
        ps_v = st.ps("ps_v", [P, GD])
        loaded, arranged, cur_ready = st.sem("loaded"), st.sem("arranged"), st.sem("cur_ready")
        rows_in = [st.sem(f"rows_in{i}") for i in range(2)]
        turned = st.sem("turned")
        copied = [st.sem("copied_act"), st.sem("copied_dve")]
        multiplied = st.sem("multiplied")
        second_ready, pre_ready, hid_ready = st.sem("second_ready"), st.sem("pre_ready"), st.sem("hid_ready")
        out_mm, out_cp = st.sem("out_mm"), st.sem("out_cp")
        cache = I["cache_cmp_kv"][0].rearrange("a (n l) c g d -> (a n) (l c g d)", l=CSTR)
        prompt_rows = O["cmp_p"][0, 0].rearrange("(n l) c g d -> n (l c g d)", l=CSTR)

        def sequences(engine, body):
            with engine.Fori(0, DEC_B // 2) as i:
                for s in range(2):
                    body(2 * i + s, i, s, KEY_ROWS)
            body(DEC_B, DEC_B // 2, 0, NPC + 1)

        with nc.Block() as block:

            @block.sync
            def _(sp):
                for c in range(2):
                    for f in range(2):
                        sp.dma_start(w1[:, c, f], I["nsa_cmp_w1"][0, c, f * CSTR:(f + 1) * CSTR].rearrange(
                            "(k l) d h -> (l d) k h", k=NL)).then_inc(loaded, 16)
                    sp.dma_start(w2[:, c], I["nsa_cmp_w2"][0, c]).then_inc(loaded, 16)
                with nc.allow_non_contiguous_dma(reason="128 biases"):
                    sp.dma_start(b1[:], I["nsa_cmp_b1"][0].rearrange("c h -> h c")).then_inc(loaded, 16)

            @block.gpsimd
            def _(pool):
                def body(b, i, s, n):
                    pool.wait_ge(pre_ready, 2 * b + 1)
                    if n == KEY_ROWS:
                        pool.tensor_copy(cur[:, s:s + 1], row_idx[:, bass.ds(b, 1)]).then_inc(cur_ready, 2)
                        pool.wait_ge(pre_ready, 1)
                        pool.wait_ge(cur_ready, 2 * b + 1)
                        pool.indirect_dma_start(rows[:, s, :], None, cache,
                                                bass.IndirectOffsetOnAxis(ap=cur[:, s:s + 1], axis=0)
                                                ).then_inc(rows_in[s], 16)
                    else:
                        pool.dma_start(rows[0:n, s, :], prompt_rows).then_inc(rows_in[s], 16)

                sequences(pool, body)

            @block.tensor
            def _(pe):
                pe.nop()
                pe.wait_ge(arranged, 1)

                def body(b, i, s, n):
                    tile = rows[0:n, s, :].rearrange("p (k l c a gd) -> p k l c a gd", k=NL, l=2, c=2, a=2)
                    pe.wait_ge(rows_in[s], 16 * i + 16)

                    def turn(k):
                        c, kk = k // NL, k % NL
                        pe.wait_ge(copied[k % 2], NL * b + k // 2 + 1)
                        for l in range(2):
                            for a in range(2):
                                mm = pe.transpose(tr[k % 4][:, 2 * l + a, 0:n], tile[:, kk, l, c, a, :],
                                                  M.ident[0:n, 0:n])
                        mm.then_inc(turned, 1)

                    def product(k):
                        c, kk = k // NL, k % NL
                        pe.wait_ge(copied[k % 2], NL * b + k // 2 + 3)
                        if kk == 0:
                            pe.wait_ge(pre_ready, 2 * b + c + 1)
                        pe.matmul(ps_h[c][:, :, 0:n], w1h[:, c, kk].rearrange("p f h -> p (f h)"),
                                  sub_T[:, k % 4, :, 0:n], start=(kk == 0), stop=(kk == NL - 1)
                                  ).then_inc(multiplied, 1)

                    def outputs(c):
                        for g in range(AG):
                            if c == 0:
                                mm = pe.matmul(ps_k[ADH * (g % 2):ADH * (g % 2) + ADH, g // 2, 0:n - 1], w2[:, 0, :],
                                               hid[:, 0, g, 0:n - 1], start=True, stop=True)
                            else:
                                mm = pe.matmul(ps_v[0:n - 1, g * ADH:(g + 1) * ADH], hid[:, 1, g, 0:n - 1],
                                               w2[:, 1, :], start=True, stop=True)
                        mm.then_inc(out_mm, 1)

                    turn(0)
                    turn(1)
                    for k in range(GK):
                        if k + 2 < GK:
                            turn(k + 2)
                        if k == NL + 4:
                            pe.wait_ge(hid_ready, 2 * b + 3)
                            pe.wait_ge(out_cp, 2 * b + 1)
                        product(k)
                        if k == NL + 4:
                            outputs(0)
                    pe.wait_ge(hid_ready, 2 * b + 4)
                    pe.wait_ge(out_cp, 2 * b + 2)
                    outputs(1)

                sequences(pe, body)

            def copy_group(engine, which, b, k, n):
                engine.wait_ge(turned, GK * b + k + 1)
                engine.wait_ge(multiplied, GK * b + k + 1)
                for l in range(2):
                    for g2 in range(2):
                        dst = sub_T[ADH * l:ADH * l + ADH, k % 4].rearrange("p (a g) n -> p a g n", g=2)[:, :, g2, 0:n]
                        src = tr[k % 4][ADH * g2:ADH * g2 + ADH, 2 * l:2 * l + 2, 0:n]
                        if which == 0:
                            ins = engine.activation(dst, src, ACT.Copy)
                        else:
                            ins = engine.tensor_copy(dst, src)
                ins.then_inc(copied[which], 1)

            @block.scalar
            def _(act):
                act.nop().then_inc(copied[0], 2)
                act.nop().then_inc(hid_ready, 2)
                act.nop().then_inc(out_cp, 2)
                act.nop().then_inc(multiplied, 4)
                act.nop().then_inc(out_mm, 2)
                act.wait_ge(loaded, 16 * 7)

                def body(b, i, s, n):
                    def split(c):
                        act.wait_ge(multiplied, GK * b + NL * (c + 1) + 4)
                        act.wait_ge(pre_ready, 2 * b + c + 1)
                        act.activation(second[:, c, :, 0:n], ps_h[c][ADH:P, :, 0:n], ACT.Copy).then_inc(second_ready, 1)

                    def squash(c):
                        act.wait_ge(pre_ready, 2 * b + c + 3)
                        act.wait_ge(out_mm, 2 * b + c + 1)
                        act.activation(hid[:, c, :, 0:n - 1], pre[:, c, :, 0:n - 1], ACT.Gelu,
                                       bias=b1[:, c:c + 1]).then_inc(hid_ready, 1)

                    def store(c):
                        act.wait_ge(out_mm, 2 * b + c + 3)
                        if c == 0:
                            dst = pcmp_kT[:, :, 0:n - 1] if n < KEY_ROWS else (
                                cmp_kT[:, bass.ds(b, 1), :, 0:n - 1].rearrange("p o a k -> p (o a) k"))
                            act.activation(dst, ps_k[:, :, 0:n - 1], ACT.Copy).then_inc(out_cp, 1)
                        else:
                            dst = pcmp_v[0:n - 1] if n < KEY_ROWS else (
                                cmp_v[0:n - 1, bass.ds(b, 1), :].rearrange("p o a -> p (o a)"))
                            act.activation(dst, ps_v[0:n - 1], ACT.Copy).then_inc(out_cp, 1)

                    for k in range(0, GK, 2):
                        copy_group(act, 0, b, k, n)
                        if k == NL:
                            split(0)
                        if k == NL + 2:
                            squash(0)
                    store(0)
                    split(1)
                    squash(1)
                    store(1)

                sequences(act, body)

            @block.vector
            def _(dve):
                dve.nop().then_inc(copied[1], 2)
                dve.nop().then_inc(pre_ready, 2)
                dve.wait_ge(loaded, 16 * 7)
                dve.tensor_copy(w1h[:, 0], w1[:, 0].rearrange("p f k h -> p k f h")).then_inc(arranged, 1)
                dve.tensor_copy(w1h[:, 1], w1[:, 1].rearrange("p f k h -> p k f h")).then_inc(arranged, 1)
                dve.wait_ge(arranged, 2)

                def body(b, i, s, n):
                    def meet(c):
                        dve.wait_ge(second_ready, 2 * b + c + 1)
                        dve.wait_ge(hid_ready, 2 * b + c + 1)
                        dve.tensor_tensor(pre[:, c, :, 0:n - 1], ps_h[c][0:ADH, :, 0:n - 1], second[:, c, :, 1:n],
                                          ALU.add).then_inc(pre_ready, 1)

                    for k in range(1, GK, 2):
                        copy_group(dve, 1, b, k, n)
                        if k == NL + 1:
                            meet(0)
                    meet(1)

                sequences(dve, body)


def prompt_stage(nc, M, q, kv, gate, q_T, k_T, pcmp_kT, pcmp_v):
    units = [(br, t, g) for t in range(2) for br in (1, 2) for g in range(AG)]
    with Stage(nc, "pa") as st:
        nmax = st.sb("nmax", [P, 2, AR])
        total = st.sb("total", [P, 2, AR])
        share = st.sb("share", [P, 2, 2, AR])
        e = st.sb("e", [P, 2, AR, 2 * P])
        e_T = st.sb("e_T", [P, 2, 2, AR, P])
        cs = st.sb("cs", [P, AH, NPC])
        csum = st.sb("csum", [P, 3, AH])
        ce_T = st.sb("ce_T", [NPC, AH, P])
        part = st.sb("part", [P, 2, AR, ADH])
        ps_s = [st.ps(f"ps_s{i}", [P, AR, 2 * P]) for i in range(2)]
        ps_t = st.ps("ps_t", [P, 2, AR, P])
        ps_o = [st.ps(f"ps_o{i}", [P, 8, ADH]) for i in range(2)]
        vec = st.sem("vec")
        c_scored, c_ready, c_turned, c_copied, c_summed, c_exp = (st.sem(n) for n in (
            "c_scored", "c_ready", "c_turned", "c_copied", "c_summed", "c_exp"))
        c_gone = st.sem("c_gone")
        scored, maxed, expd, turned, copied, summed, stored = (st.sem(n) for n in (
            "scored", "maxed", "expd", "turned", "copied", "summed", "stored"))
        causal = M.c("causal")
        with nc.Block() as block:

            @block.tensor
            def _(pe):
                for t in range(2):
                    if t:
                        pe.wait_ge(c_ready, t)
                    for h in range(AH):
                        a, g2, r = h // 8, (h // 4) % 2, h % 4
                        d0 = ADH * g2
                        mm = pe.matmul(ps_s[g2][:, a, r * NPC:(r + 1) * NPC], q_T[d0:d0 + ADH, a, r, t * P:(t + 1) * P],
                                       pcmp_kT[d0:d0 + ADH, a, 0:NPC], start=True, stop=True)
                    mm.then_inc(c_scored, 1)
                    pe.wait_ge(c_exp, t + 1)
                    for k in range(2):
                        if k or t:
                            pe.wait_ge(c_copied, 2 * t + k)
                        for h in range(8):
                            mm = pe.transpose(ps_t[0:NPC, h // 4, h % 4, :], cs[:, 8 * k + h, :], M.ident)
                        mm.then_inc(c_turned, 1)
                    pe.wait_ge(c_copied, 2 * t + 2)
                    if t:
                        pe.wait_ge(c_gone, t)
                    for h in range(AH):
                        mm = pe.matmul(ps_o[h // 8][:, h % 8, :], ce_T[:, h, :],
                                       pcmp_v[0:NPC, (h // 4) * ADH:(h // 4 + 1) * ADH], start=True, stop=True)
                    mm.then_inc(c_summed, 1)
                pe.wait_ge(c_gone, 2)

                def scores(u):
                    br, t, g = units[u]
                    d0, nk = ADH * (g % 2), P * (t + 1)
                    if u >= 2:
                        pe.wait_ge(expd, u - 1)
                    for r in range(AR):
                        pe.matmul(ps_s[u % 2][:, r, 0:nk], q_T[d0:d0 + ADH, g // 2, r, t * P:(t + 1) * P],
                                  k_T[d0:d0 + ADH, br - 1, g // 2, 0:nk], start=True, stop=False)
                        mm = pe.matmul(ps_s[u % 2][:, r, nk - P:nk], M.ident, causal, start=False, stop=True)
                    mm.then_inc(scored, 1)

                scores(0)
                for u, (br, t, g) in enumerate(units):
                    if u + 1 < len(units):
                        scores(u + 1)
                    pe.wait_ge(expd, u + 1)
                    if u:
                        pe.wait_ge(copied, u)
                    for kt in range(t + 1):
                        for r in range(AR):
                            mm = pe.transpose(ps_t[:, kt, r, :], e[:, u % 2, r, kt * P:(kt + 1) * P], M.ident)
                    mm.then_inc(turned, 1)
                    pe.wait_ge(copied, u + 1)
                    if u >= 2:
                        pe.wait_ge(stored, u - 1)
                    for r in range(AR):
                        for kt in range(t + 1):
                            mm = pe.matmul(ps_o[u % 2][:, r, :], e_T[:, u % 2, kt, r, :],
                                           kv[:, kt, br, 1, g * ADH:(g + 1) * ADH], start=(kt == 0), stop=(kt == t))
                    mm.then_inc(summed, 1)

            @block.scalar
            def _(act):
                for t in range(2):
                    act.wait_ge(c_ready, t + 1)
                    act.activation(cs[:], cs[:], ACT.Exp).then_inc(c_exp, 1)
                    for k in range(2):
                        act.wait_ge(c_turned, 2 * t + k + 1)
                        act.activation(ce_T[:, 8 * k:8 * k + 8, :], ps_t[0:NPC].rearrange("p a b c -> p (a b) c"),
                                       ACT.Copy).then_inc(c_copied, 1)
                for u, (br, t, g) in enumerate(units):
                    nk = P * (t + 1)
                    act.wait_ge(maxed, u + 1)
                    if u >= 2:
                        act.wait_ge(turned, u - 1)
                    for r in range(AR):
                        ins = act.activation(e[:, u % 2, r, 0:nk], ps_s[u % 2][:, r, 0:nk], ACT.Exp,
                                             bias=nmax[:, u % 2, r:r + 1], accum_out=total[:, u % 2, r:r + 1])
                    ins.then_inc(expd, 1)
                    act.wait_ge(turned, u + 1)
                    if u >= 2:
                        act.wait_ge(summed, u - 1)
                    act.activation(e_T[:, u % 2, 0:t + 1], ps_t[:, 0:t + 1], ACT.Copy).then_inc(copied, 1)

            def finish(dve, step, u):
                br, t, g = units[u]
                s = u % 2
                dve.wait_ge(expd, u + 1)
                step(dve.reciprocal(share[:, s, 0], total[:, s]))
                step(dve.tensor_tensor(share[:, s, 1], share[:, s, 0], gate[:, t, g * AR:(g + 1) * AR, br], ALU.mult))
                dve.wait_ge(summed, u + 1)
                step(dve.tensor_tensor(part[:, s], ps_o[s][:, 0:AR, :],
                                       share[:, s, 1, :, None].to_broadcast([P, AR, ADH]), ALU.mult))
                out = q[:, t, g * AR * ADH:(g + 1) * AR * ADH].rearrange("p (h d) -> p h d", h=AR)
                dve.tensor_tensor(out, out, part[:, s], ALU.add).then_inc(stored, 1)
                dve.wait_ge(stored, u + 1)

            @block.vector
            def _(dve):
                step = Chain(dve, vec)
                for t in range(2):
                    full = [P, AH, NPC]
                    dve.wait_ge(c_scored, t + 1)
                    if t:
                        dve.wait_ge(c_turned, 2 * t)
                    by_group = cs[:].rearrange("p (a g r) k -> p a g r k", a=2, g=2)
                    for a in range(2):
                        for g2 in range(2):
                            step(dve.tensor_tensor(
                                by_group[:, a, g2], ps_s[g2][:, a, 0:AR * NPC].rearrange("p (r k) -> p r k", r=AR),
                                M.c("cmp_mask")[:, t, None, :].to_broadcast([P, AR, NPC]), ALU.add))
                    step(dve.tensor_reduce(csum[:, 0], cs[:], AX.X, ALU.max))
                    dve.tensor_tensor(cs[:], cs[:], csum[:, 0, :, None].to_broadcast(full),
                                      ALU.subtract).then_inc(c_ready, 1)
                    dve.wait_ge(c_exp, t + 1)
                    step(dve.tensor_reduce(csum[:, 1], cs[:], AX.X, ALU.add))
                    step(dve.reciprocal(csum[:, 2], csum[:, 1]))
                    step(dve.scalar_tensor_tensor(out=csum[:, 1], in0=csum[:, 2], scalar=M.c("cmp_any")[:, t:t + 1],
                                                  in1=gate[:, t, :, 0], op0=ALU.mult, op1=ALU.mult))
                    dve.wait_ge(c_summed, t + 1)
                    for k in range(2):
                        step(dve.tensor_tensor(
                            q[:, t, k * 512:k * 512 + 512].rearrange("p (h d) -> p h d", h=8), ps_o[k][:],
                            csum[:, 1, 8 * k:8 * k + 8, None].to_broadcast([P, 8, ADH]), ALU.mult))
                    dve.nop().then_inc(c_gone, 1)
                for u, (br, t, g) in enumerate(units):
                    nk = P * (t + 1)
                    dve.wait_ge(scored, u + 1)
                    if u >= 2:
                        dve.wait_ge(expd, u - 1)
                    dve.tensor_reduce(nmax[:, u % 2], ps_s[u % 2][:, :, 0:nk], AX.X, ALU.max, negate=True
                                      ).then_inc(maxed, 1)
                    if u:
                        finish(dve, step, u - 1)
                finish(dve, step, len(units) - 1)


def blocks_stage(nc, M, q_T, q_blk, cmp_kT, cmp_v, block_mask, o_out):
    NB = PAST // SBLK
    with Stage(nc, "db") as st:
        p = st.sb("p", [P, 2, KEY_ROWS])
        p_T = st.sb("p_T", [P, 2, P])
        small = st.sb("small", [P, 4, 4])
        imp = st.sb("imp", [P, 4, NB])
        imp_p = st.sb("imp_p", [P, KEY_ROWS])
        score = st.sb("score", [P, 3, NB + 1])
        top = st.sb("top", [P, 2, 8])
        o = st.sb("o", [P, 4, ADH])
        ps_s = [st.ps(f"ps_s{i}", [P, KEY_ROWS]) for i in range(2)]
        ps_i = [st.ps(f"ps_i{i}", [P, KEY_ROWS]) for i in range(2)]
        ps_t = [st.ps(f"ps_t{i}", [P, P]) for i in range(2)]
        ps_o = [st.ps(f"ps_o{i}", [P, AG, ADH]) for i in range(2)]
        names = ("vec", "blk_ready", "scored", "maxed", "expd", "normed", "turned", "copied", "summed", "o_ready",
                 "saved", "cleared")
        vec, blk_ready, scored, maxed, expd, normed, turned, copied, summed, o_ready, saved, cleared = (
            st.sem(n) for n in names)
        with nc.Block() as block:

            @block.gpsimd
            def _(pool):
                pool.memset(q_blk[:], 0.0).then_inc(cleared, 1)
                pool.memset(p[:], 0.0).then_inc(cleared, 1)

            @block.tensor
            def _(pe):
                pe.wait_ge(blk_ready, 1)
                for u in range(4):
                    for b2 in range(2):
                        for a in range(2):
                            r0 = 64 * b2 + 32 * a
                            mm = pe.matmul(ps_s[u % 2][r0:r0 + 32, 0:N_CMP], q_blk[:, 2 * u + b2, a, :],
                                           cmp_kT[:, 2 * u + b2, a, 0:N_CMP], start=True, stop=True)
                    mm.then_inc(scored, 1)
                    pe.wait_ge(normed, u + 1)
                    pe.matmul(ps_i[u % 2][:], M.c("sum_heads"), p[:, u % 2, :], start=True, stop=True)
                    pe.transpose(ps_t[u % 2][:], p[:, u % 2, :], M.ident).then_inc(turned, 1)
                    pe.wait_ge(copied, u + 1)
                    if u >= 2:
                        pe.wait_ge(o_ready, u - 1)
                    for b2 in range(2):
                        mm = pe.matmul(ps_o[u % 2][64 * b2:64 * b2 + 64].rearrange("p g d -> p (g d)"),
                                       p_T[0:N_CMP, u % 2, 64 * b2:64 * b2 + 64], cmp_v[0:N_CMP, 2 * u + b2, :],
                                       start=True, stop=True)
                    mm.then_inc(summed, 1)

            @block.scalar
            def _(act):
                for u in range(4):
                    act.wait_ge(maxed, u + 1)
                    act.activation(p[:, u % 2, 0:N_CMP], ps_s[u % 2][:, 0:N_CMP], ACT.Exp, bias=small[:, u, 0:1],
                                   accum_out=small[:, u, 1:2]).then_inc(expd, 1)
                    act.wait_ge(turned, u + 1)
                    act.activation(p_T[:, u % 2, :], ps_t[u % 2][:], ACT.Copy).then_inc(copied, 1)

            @block.vector
            def _(dve):
                step = Chain(dve, vec)
                dve.wait_ge(cleared, 2)
                for a in range(2):
                    for g2 in range(2):
                        for r in range(AR):
                            d0 = ADH * g2
                            c0 = (g2 * AR + r) * DEC_S
                            step(dve.tensor_copy(q_blk[d0:d0 + ADH, :, a, c0:c0 + DEC_S],
                                                 q_T[d0:d0 + ADH, a, r, SEQ:NTOK].rearrange("p (b s) -> p b s", s=DEC_S)))
                dve.nop().then_inc(blk_ready, 1)
                for u in range(4):
                    dve.wait_ge(scored, u + 1)
                    dve.tensor_reduce(small[:, u, 0:1], ps_s[u % 2][:, 0:N_CMP], AX.X, ALU.max, negate=True
                                      ).then_inc(maxed, 1)
                    dve.wait_ge(expd, u + 1)
                    step(dve.reciprocal(small[:, u, 2:3], small[:, u, 1:2]))
                    dve.tensor_scalar(p[:, u % 2, 0:N_CMP], p[:, u % 2, 0:N_CMP], small[:, u, 2:3], None, ALU.mult
                                      ).then_inc(normed, 1)
                    dve.wait_ge(turned, u + 1)
                    step(dve.tensor_copy(imp_p[:], ps_i[u % 2][:]))
                    four = imp_p[:].rearrange("p (j k) -> p j k", k=4)
                    step(dve.tensor_reduce(imp[:, 0], four, AX.X, ALU.add))
                    step(dve.tensor_reduce(imp[:, 1], four[:, :, 0:3], AX.X, ALU.add))
                    step(dve.tensor_tensor(imp[:, 2], imp[:, 0], imp[:, 1], ALU.add))
                    step(dve.memset(score[:, 0], -NEG))
                    step(dve.tensor_tensor(score[:, 0, 1:NB - 1], imp[:, 2, 1:NB - 1], four[:, 0:NB - 2, 3], ALU.add))
                    for k in range(2):
                        step(dve.max(top[:, k], score[:, k]))
                        step(dve.match_replace(score[:, k + 1], top[:, k], score[:, k], -3e38))
                    step(dve.tensor_scalar(block_mask[:, u], score[:, 2, 0:NB], -1e38, NEG, ALU.is_gt, ALU.mult))
                    dve.wait_ge(summed, u + 1)
                    for g in range(AG):
                        if g == 0:
                            step(dve.tensor_scalar(o[:, u], ps_o[u % 2][:, 0, :], M.c("group_one")[:, 0:1], None,
                                                   ALU.mult))
                        else:
                            step(dve.scalar_tensor_tensor(out=o[:, u], in0=ps_o[u % 2][:, g, :],
                                                          scalar=M.c("group_one")[:, g:g + 1], in1=o[:, u],
                                                          op0=ALU.mult, op1=ALU.add))
                    dve.nop().then_inc(o_ready, 1)

            @block.sync
            def _(sp):
                for u in range(4):
                    sp.wait_ge(o_ready, u + 1)
                    for b2 in range(2):
                        b = 2 * u + b2
                        sp.dma_start(o_out[DEC_S * b:DEC_S * (b + 1)].rearrange("s (h d) -> h s d", h=AH),
                                     o[64 * b2:64 * b2 + 64, u, :]).then_inc(saved, 16)
                sp.wait_ge(saved, 16 * 8)


def decode_stage(nc, M, name, q_blk, new_kT, new_v, tiles, o_out, block_mask, rows, row_idx):
    QUADS = tiles // 4
    NK = tiles * P
    with Stage(nc, name) as st:
        width = tiles * 2 * GD
        kvr = st.sb("kvr", [P, 2, width])
        kt = st.sb("kt", [P, 3, 4, P])
        s = st.sb("s", [P, NK + NDEC])
        e_T = st.sb("e_T", [P, tiles + 1, P])
        small = st.sb("small", [P, 4, 4])
        scale = st.sb("scale", [P, AG])
        o = st.sb("o", [P, 4, ADH])
        tr = [st.ps(f"tr{i}", [P, 4, P]) for i in range(3)]
        ps_s = [st.ps(f"ps_s{i}", [P, 4, P]) for i in range(2)]
        ps_t = [st.ps(f"ps_t{i}", [P, 4, P]) for i in range(2)]
        ps_o = st.ps("ps_o", [P, AG, ADH])
        vec = st.sem("vec")
        kv_in = [st.sem(f"kv_in{i}") for i in range(2)]
        copied = [st.sem("copied_act"), st.sem("copied_dve")]
        turned, scored, masked, maxed, expd = (st.sem(n) for n in ("turned", "scored", "masked", "maxed", "expd"))
        e_turned, e_copied, summed, o_ready, saved, multiplied = (st.sem(n) for n in (
            "e_turned", "e_copied", "summed", "o_ready", "saved", "multiplied"))
        tile = [kvr[:, b2, :].rearrange("p (l c g) -> p l c g", l=tiles, c=2) for b2 in range(2)]
        GK = QUADS * 4
        TQ = QUADS + 1
        SQ = QUADS + 1
        new_mask = M.c("new_mask")
        with nc.Block() as block:

            @block.gpsimd
            def _(pool):
                for u in range(4):
                    if u:
                        pool.wait_ge(summed, u)
                    for b2 in range(2):
                        b = 2 * u + b2
                        if row_idx is not None:
                            pool.indirect_dma_start(kvr[:, b2, :], None, rows,
                                                    bass.IndirectOffsetOnAxis(ap=row_idx[:, b:b + 1], axis=0)
                                                    ).then_inc(kv_in[b2], 16)
                        else:
                            pool.dma_start(kvr[:, b2, :], rows[b].rearrange("(n l) c g d -> n (l c g d)", l=tiles)
                                           ).then_inc(kv_in[b2], 16)

            @block.tensor
            def _(pe):
                for u in range(4):
                    def turn(k):
                        lq, b2, a = k // 4, (k // 2) % 2, k % 2
                        e = GK * u + k
                        if k < 4 and a == 0:
                            pe.wait_ge(kv_in[b2], 16 * (u + 1))
                        if e >= 3:
                            pe.wait_ge(copied[(e - 3) % 2], (e - 3) // 2 + 1)
                        for l in range(4):
                            mm = pe.transpose(tr[e % 3][:, l, :], tile[b2][:, 4 * lq + l, 0, a * P:(a + 1) * P], M.ident)
                        mm.then_inc(turned, 1)

                    def product(k):
                        lq, b2, a = k // 4, (k // 2) % 2, k % 2
                        e, bank = GK * u + k, SQ * u + k // 4
                        pe.wait_ge(copied[e % 2], e // 2 + 1)
                        if k % 4 == 0 and bank >= 2:
                            pe.wait_ge(masked, bank - 1)
                        r0 = 64 * b2 + 32 * a
                        pe.matmul(ps_s[bank % 2][r0:r0 + 32], q_blk[:, 2 * u + b2, a, :], kt[:, e % 3],
                                  start=True, stop=True).then_inc(multiplied, 1)

                    turn(0)
                    for k in range(GK):
                        if k + 1 < GK:
                            turn(k + 1)
                        product(k)
                    bank = SQ * u + QUADS
                    if bank >= 2:
                        pe.wait_ge(masked, bank - 1)
                    for b2 in range(2):
                        for a in range(2):
                            r0 = 64 * b2 + 32 * a
                            mm = pe.matmul(ps_s[bank % 2][r0:r0 + 32, 0, 0:NDEC], q_blk[:, 2 * u + b2, a, :],
                                           new_kT[:, a, SEQ:NTOK], start=True, stop=True)
                    mm.then_inc(scored, 1)
                    pe.wait_ge(expd, u + 1)

                    def turn_e(k):
                        e = TQ * u + k
                        if e >= 2:
                            pe.wait_ge(e_copied, e - 1)
                        if k < QUADS:
                            for l in range(4):
                                mm = pe.transpose(ps_t[e % 2][:, l, :], s[:, (4 * k + l) * P:(4 * k + l + 1) * P], M.ident)
                        else:
                            mm = pe.transpose(ps_t[e % 2][0:NDEC, 0, :], s[:, NK:NK + NDEC], M.ident)
                        mm.then_inc(e_turned, 1)

                    turn_e(0)
                    if u:
                        pe.wait_ge(o_ready, u)
                    for k in range(TQ):
                        if k + 1 < TQ:
                            turn_e(k + 1)
                        pe.wait_ge(e_copied, TQ * u + k + 1)
                        for l in range(4 if k < QUADS else 1):
                            for b2 in range(2):
                                out = ps_o[64 * b2:64 * b2 + 64].rearrange("p g d -> p (g d)")
                                if k < QUADS:
                                    mm = pe.matmul(out, e_T[:, 4 * k + l, 64 * b2:64 * b2 + 64],
                                                   tile[b2][:, 4 * k + l, 1, :], start=(k + l == 0), stop=False)
                                else:
                                    mm = pe.matmul(out, e_T[0:NDEC, tiles, 64 * b2:64 * b2 + 64], new_v,
                                                   start=False, stop=True)
                    mm.then_inc(summed, 1)

            def copy_keys(engine, e):
                engine.wait_ge(turned, e + 1)
                if e >= 3:
                    engine.wait_ge(multiplied, e - 2)
                if e % 2 == 0:
                    engine.activation(kt[:, e % 3], tr[e % 3][:], ACT.Copy).then_inc(copied[0], 1)
                else:
                    engine.tensor_copy(kt[:, e % 3], tr[e % 3][:]).then_inc(copied[1], 1)

            @block.scalar
            def _(act):
                for u in range(4):
                    for k in range(0, GK, 2):
                        copy_keys(act, GK * u + k)
                    act.wait_ge(maxed, u + 1)
                    act.activation(s[:], s[:], ACT.Exp, bias=small[:, u, 0:1], accum_out=small[:, u, 1:2]
                                   ).then_inc(expd, 1)
                    for k in range(TQ):
                        act.wait_ge(e_turned, TQ * u + k + 1)
                        if u and k == 0:
                            act.wait_ge(summed, u)
                        if k < QUADS:
                            act.activation(e_T[:, 4 * k:4 * k + 4, :], ps_t[(TQ * u + k) % 2][:], ACT.Copy
                                           ).then_inc(e_copied, 1)
                        else:
                            act.activation(e_T[0:NDEC, tiles, :], ps_t[(TQ * u + k) % 2][0:NDEC, 0, :], ACT.Copy
                                           ).then_inc(e_copied, 1)

            @block.vector
            def _(dve):
                step = Chain(dve, vec)
                for u in range(4):
                    if u:
                        dve.wait_ge(e_turned, TQ * u)

                    def mask(lq):
                        out = s[:, lq * 4 * P:(lq + 1) * 4 * P]
                        bank = SQ * u + lq
                        dve.wait_ge(multiplied, GK * u + 4 * lq + 4)
                        if block_mask is not None:
                            full = [P, 4, PAST // SBLK, 4]
                            dve.tensor_tensor(out.rearrange("p (l j k) -> p l j k", l=4, k=4),
                                              ps_s[bank % 2][:].rearrange("p l (j k) -> p l j k", k=4),
                                              block_mask[:, u, None, :, None].to_broadcast(full), ALU.add
                                              ).then_inc(masked, 1)
                        else:
                            dve.tensor_tensor(out.rearrange("p (l j) -> p l j", l=4), ps_s[bank % 2][:],
                                              M.c("win_mask"), ALU.add).then_inc(masked, 1)

                    for k in range(1, GK, 2):
                        copy_keys(dve, GK * u + k)
                        if k % 4 == 1 and k > 4:
                            mask(k // 4 - 1)
                    mask(QUADS - 1)
                    dve.wait_ge(scored, u + 1)
                    dve.tensor_tensor(s[:, NK:NK + NDEC], ps_s[(SQ * u + QUADS) % 2][:, 0, 0:NDEC], new_mask[:, u, :],
                                      ALU.add).then_inc(masked, 1)
                    dve.wait_ge(masked, SQ * (u + 1))
                    dve.tensor_reduce(small[:, u, 0:1], s[:], AX.X, ALU.max, negate=True).then_inc(maxed, 1)
                    dve.wait_ge(expd, u + 1)
                    step(dve.reciprocal(small[:, u, 2:3], small[:, u, 1:2]))
                    step(dve.tensor_scalar(scale[:], M.c("group_one"), small[:, u, 2:3], None, ALU.mult))
                    dve.wait_ge(summed, u + 1)
                    for g in range(AG):
                        if g == 0:
                            step(dve.tensor_scalar(o[:, u], ps_o[:, 0, :], scale[:, 0:1], None, ALU.mult))
                        else:
                            step(dve.scalar_tensor_tensor(out=o[:, u], in0=ps_o[:, g, :], scalar=scale[:, g:g + 1],
                                                          in1=o[:, u], op0=ALU.mult, op1=ALU.add))
                    dve.nop().then_inc(o_ready, 1)

            @block.sync
            def _(sp):
                for u in range(4):
                    sp.wait_ge(o_ready, u + 1)
                    for b2 in range(2):
                        b = 2 * u + b2
                        sp.dma_start(o_out[DEC_S * b:DEC_S * (b + 1)].rearrange("s (h d) -> h s d", h=AH),
                                     o[64 * b2:64 * b2 + 64, u, :]).then_inc(saved, 16)
                sp.wait_ge(saved, 16 * 8)


def mix_stage(nc, M, q, gate, o_dec):
    with Stage(nc, "mg") as st:
        parts = st.sb("parts", [NDEC, 3, AH, ADH])
        loaded, vec = st.sem("loaded"), st.sem("vec")
        with nc.Block() as block:

            @block.sync
            def _(sp):
                sp.dma_start(parts[:].rearrange("p b h d -> p b (h d)"), o_dec.rearrange("b t d -> t b d")
                             ).then_inc(loaded, 16)

            @block.vector
            def _(dve):
                step = Chain(dve, vec)
                dve.wait_ge(loaded, 16)
                for br in range(3):
                    step(dve.tensor_tensor(parts[:, br], parts[:, br],
                                           gate[0:NDEC, 2, :, br, None].to_broadcast([NDEC, AH, ADH]), ALU.mult))
                step(dve.tensor_tensor(parts[:, 0], parts[:, 0], parts[:, 1], ALU.add))
                step(dve.tensor_tensor(q[0:NDEC, 2, :].rearrange("p (h d) -> p h d", h=AH), parts[:, 0], parts[:, 2],
                                       ALU.add))


class Memory:

    def __init__(self, nc, stack):
        self.x = stack.enter_context(nc.sbuf_tensor("x", [P, NT, D], F32))
        self.h_T = stack.enter_context(nc.sbuf_tensor("h_T", [P, DC, NTOK], F32))
        self.const = stack.enter_context(nc.sbuf_tensor("const", [P, CONST.shape[1]], F32))
        self.ident = view(self.const, "ident")

    def c(self, name, rows=None):
        return view(self.const, name, rows)


def load_stage(nc, M, I):
    with Stage(nc, "ld") as st:
        loaded = st.sem("loaded")
        cleared = st.sem("cleared")
        with nc.Block() as block:

            @block.vector
            def _(dve):
                dve.memset(M.x[:, NT - 1, :], 0.0).then_inc(cleared, 1)

            @block.sync
            def _(sp):
                sp.dma_start(M.x[:, 0:2, :], I["x_prompt"][0].rearrange("(t p) d -> p t d", p=P)).then_inc(loaded, 16)
                sp.wait_ge(cleared, 1)
                sp.dma_start(M.x[0:NDEC, 2, :], I["x_sample"].rearrange("b s d -> (b s) d")).then_inc(loaded, 16)
                sp.dma_start(M.const[:], I["const"]).then_inc(loaded, 16)
                sp.wait_ge(loaded, 48)


def final_stage(nc, M, I, O):
    with Stage(nc, "fi") as st:
        gain_b = st.sb("gain", [P, D])
        y = st.sb("y", [P, NT, D])
        sq = st.sb("sq", [P, 2, D])
        ss = st.sb("ss", [P, 3, NT])
        gain_in, vec, mean_ready, root_ready, y_ready, saved = (
            st.sem(n) for n in ("gain_in", "vec", "mean_ready", "root_ready", "y_ready", "saved"))
        with nc.Block() as block:

            @block.sync
            def _(sp):
                sp.dma_start(gain_b[:], I["norm_final"].partition_broadcast(P)).then_inc(gain_in, 16)
                for t, (t0, n) in enumerate(TILES):
                    sp.wait_ge(y_ready, t + 1)
                    out = O["y_p"][0, t0:t0 + n] if t < 2 else O["y_s"].rearrange("b s d -> (b s) d")
                    sp.dma_start(out, y[0:n, t, :]).then_inc(saved, 16)
                sp.wait_ge(saved, 16 * NT)

            @block.scalar
            def _(act):
                for t, (_, n) in enumerate(TILES):
                    act.wait_ge(mean_ready, t + 1)
                    act.activation(ss[0:n, 0, t:t + 1], ss[0:n, 1, t:t + 1], ACT.Sqrt).then_inc(root_ready, 1)

            @block.vector
            def _(dve):
                step = Chain(dve, vec)
                for t, (_, n) in enumerate(TILES):
                    step(dve.tensor_tensor_reduce(sq[0:n, t % 2, :], M.x[0:n, t, :], M.x[0:n, t, :], 1.0, 0.0,
                                                  ALU.mult, ALU.add, ss[0:n, 0, t:t + 1]))
                    dve.tensor_scalar(ss[0:n, 1, t:t + 1], ss[0:n, 0, t:t + 1], 1.0 / D, EPS,
                                      ALU.mult, ALU.add).then_inc(mean_ready, 1)
                dve.wait_ge(gain_in, 16)
                for t, (_, n) in enumerate(TILES):
                    dve.wait_ge(root_ready, t + 1)
                    step(dve.reciprocal(ss[0:n, 2, t:t + 1], ss[0:n, 0, t:t + 1]))
                    dve.scalar_tensor_tensor(out=y[0:n, t, :], in0=M.x[0:n, t, :], scalar=ss[0:n, 2, t:t + 1],
                                             in1=gain_b[0:n, :], op0=ALU.mult, op1=ALU.mult).then_inc(y_ready, 1)


def program(nc, I, O):
    with ExitStack() as stack:
        M = Memory(nc, stack)
        load_stage(nc, M, I)
        norm_stage(nc, "n0", M, I["norm_mix"][0])
        mlstm_stage(nc, M, I, O)
        peer_stage(nc, "f0", M, I, 0)
        nsa_stage(nc, M, I, O)
        peer_stage(nc, "f1", M, I, 1)
        final_stage(nc, M, I, O)


OUTPUTS = [
    ("y_p", (1, SEQ, D)), ("y_s", (DEC_B, DEC_S, D)),
    ("cmp_p", (1, 1, SEQ, 2, AG, ADH)), ("sel_p", (1, 1, SEQ, 2, AG, ADH)), ("win_p", (1, 1, SEQ, 2, AG, ADH)),
    ("C_p", (1, 1, MH, MDK, MDV)), ("n_p", (1, 1, MH, MDK)), ("m_p", (1, 1, MH)),
    ("cmp_s", (1, DEC_B, DEC_S, 2, AG, ADH)), ("sel_s", (1, DEC_B, DEC_S, 2, AG, ADH)),
    ("win_s", (1, DEC_B, WIN, 2, AG, ADH)),
    ("C_s", (1, DEC_B, MH, MDK, MDV)), ("n_s", (1, DEC_B, MH, MDK)), ("m_s", (1, DEC_B, MH)),
]


def kernel(**inputs):
    import concourse.bacc as bacc
    from concourse.bass_utils import run_bass_kernel_spmd

    nc = bacc.Bacc("TRN2", target_bir_lowering=False, num_devices=1)
    arrays, I, O = {}, {}, {}
    for name, value in {**inputs, "const": CONST}.items():
        a = np.ascontiguousarray(value)
        arrays[f"in_{name}_dram"] = a
        I[name] = nc.dram_tensor(f"in_{name}_dram", a.shape, mybir.dt.from_np(a.dtype), kind="ExternalInput").ap()
    for name, shape in OUTPUTS:
        O[name] = nc.dram_tensor(f"out_{name}_dram", shape, F32, kind="ExternalOutput").ap()
    program(nc, I, O)
    r = run_bass_kernel_spmd(nc, [arrays], core_ids=[0])
    return tuple(r.results[0][f"out_{name}_dram"] for name, _ in OUTPUTS)
```

```python
from contextlib import ExitStack

import numpy as np

import concourse.bass as bass
from concourse import mybir

F32 = mybir.dt.float32
I32 = mybir.dt.int32
U32 = mybir.dt.uint32
ALU = mybir.AluOpType
ACT = mybir.ActivationFunctionType
AX = mybir.AxisListType

P = 128
D = 1024
DC = D // P
SEQ = 256
DEC_B, DEC_S = 8, 4
NDEC = DEC_B * DEC_S
NTOK = SEQ + NDEC
TILES = [(0, 128), (128, 128), (256, NDEC)]
NT = len(TILES)
EPS = 1e-6
NEG = -1e30

MH, MDK, MDV = 8, 64, 128
VW = MDV + 1
AH, AG, AR, ADH = 16, 4, 4, 64
ROT = ADH // 4
CSTR, CLEN = 16, 32
SBLK, NSEL = 64, 16
WIN = 512
PAST, PAGE = 2048, 128
NPAGE = PAST // PAGE
PH, PK, PTOP = 8, 128, 16
AQW, AKVW = AH * ADH, 6 * AG * ADH


def constants():
    at, cols = {}, []

    def put(name, a):
        a = np.asarray(a, np.float32)
        full = np.zeros((P, int(np.prod(a.shape[1:]))), np.float32)
        full[: a.shape[0]] = a.reshape(a.shape[0], -1)
        at[name] = (sum(c.shape[1] for c in cols), a.shape)
        cols.append(full)

    i = np.arange(P)
    d = np.arange(NDEC)
    same = (d[:, None] // DEC_S) == (d[None, :] // DEC_S)
    put("ident", np.eye(P))
    put("tri", i[:, None] <= i[None, :])
    put("tri_dec", same & (d[:, None] <= d[None, :]))
    put("mask", np.where(i[:, None] <= i[None, :], 0, NEG))
    put("mask_dec", np.where(same & (d[:, None] <= d[None, :]), 0, NEG))
    put("sel_head", np.repeat(np.eye(MH)[:, :, None], P, 2))
    put("last", (i == P - 1)[:, None] * np.ones((1, P)))
    put("last_dec", same & (d[:, None] % DEC_S == DEC_S - 1))
    pb = i // 64
    put("last_state", [[[t == DEC_S * (2 * b4 + pb[p]) + DEC_S - 1 for p in range(P)] for b4 in range(4)] for t in d])
    put("seq_q", [[[t // DEC_S == 2 * b4 + pb[p] for t in d] for b4 in range(4)] for p in range(P)])
    put("seq_k", [[t // DEC_S == b for b in range(DEC_B)] for t in d])
    put("iota16", np.tile(np.arange(PTOP), (P, 1)))
    half = ROT // 2
    inv = np.float32(500000.0) ** (-(np.arange(half, dtype=np.float32) * np.float32(2.0 / ROT)))
    pos = np.zeros((P, NT), np.float32)
    pos[:, 0], pos[:, 1], pos[:NDEC, 2] = i, i + P, PAST + d % DEC_S
    ang = (pos[:, :, None] * inv.astype(np.float32)).astype(np.float32).astype(np.float64)
    put("cos", np.cos(ang))
    put("sin", np.sin(ang))
    put("causal", np.where(i[:, None] >= i[None, :], 0, NEG))
    n = np.arange(15)
    cm = [[np.where(n * CSTR + CLEN - 1 <= t + q, 0, NEG) for t in (0, P)] for q in i]
    put("cmp_mask", cm)
    put("cmp_any", [[float(t + q >= CLEN - 1) for t in (0, P)] for q in i])
    g, q = i // 16, i % DEC_S
    put("sum_heads", (g[:, None] == g[None, :]) & (q[:, None] == q[None, :]))
    put("new_mask", [[[0 if t // DEC_S == 2 * u + p // 64 and t % DEC_S <= p % DEC_S else NEG for t in d]
                      for u in range(4)] for p in i])
    put("group_one", [[float((p % 64) // 16 == k) for k in range(AG)] for p in i])
    put("win_mask", [[[NEG if 4 * n_ + j < q[p] else 0 for n_ in range(P)] for j in range(4)] for p in i])
    put("pos16", np.repeat(i[:, None] % 8, DEC_B, 1))
    put("page_rep", [[float(r // 8 == p) for r in range(P)] for p in range(NPAGE)])
    put("stack32", [[float(p % NDEC == t) for t in range(NDEC)] for p in range(P)])
    return at, np.concatenate(cols, 1)


CONST_AT, CONST = constants()


class Chain:

    def __init__(self, engine, sem):
        self.engine, self.sem, self.n = engine, sem, 0

    def __call__(self, instruction):
        self.n += 1
        instruction.then_inc(self.sem, 1)
        self.engine.wait_ge(self.sem, self.n)


class Stage:

    def __init__(self, nc, name):
        self.nc, self.name, self.sems, self.stack = nc, name, [], ExitStack()

    def __enter__(self):
        return self

    def sb(self, name, shape, dt=F32):
        return self.stack.enter_context(self.nc.sbuf_tensor(f"{self.name}_{name}", shape, dt))

    def ps(self, name, shape, dt=F32):
        return self.stack.enter_context(self.nc.psum_tensor(f"{self.name}_{name}", shape, dt))

    def sem(self, name):
        s = self.nc.alloc_semaphore(f"{self.name}_{name}")
        self.sems.append(s)
        return s

    def __exit__(self, *exc):
        self.stack.close()
        if exc[0] is None:
            self.nc.clear_and_free_semaphores(self.sems)
            self.nc.all_engine_barrier()
        return False


def view(tile, name, rows=None):
    at, shape = CONST_AT[name]
    n = int(np.prod(shape[1:]))
    a = tile[0:(rows or shape[0]), at:at + n]
    if len(shape) == 3:
        a = a.rearrange("p (a b) -> p a b", a=shape[1])
    if len(shape) == 4:
        a = a.rearrange("p (a b c) -> p a b c", a=shape[1], b=shape[2])
    return a


def norm_stage(nc, name, M, gain_b, gain_in, keep=None, pe_first=None, act_first=None):
    with Stage(nc, name) as st:
        h = keep if keep is not None else st.sb("h", [P, NT, D])
        sq = st.sb("sq", [P, 2, D])
        ss = st.sb("ss", [P, 3 * NT])
        tr = [st.ps(f"tr{i}", [P, 4, P]) for i in range(4)]
        vec = st.sem("vec")
        mean_ready = st.sem("mean_ready")
        root_ready = st.sem("root_ready")
        h_ready = st.sem("h_ready")
        turned = st.sem("turned")
        copied = st.sem("copied")
        groups = [(t, g) for t in range(NT) for g in range(DC // 4)]
        with nc.Block() as block:

            @block.vector
            def _(dve):
                step = Chain(dve, vec)
                for t, (_, n) in enumerate(TILES):
                    step(dve.tensor_tensor_reduce(sq[0:n, t % 2, :], M.x[0:n, t, :], M.x[0:n, t, :], 1.0, 0.0,
                                                  ALU.mult, ALU.add, ss[0:n, t:t + 1]))
                    dve.tensor_scalar(ss[0:n, NT + t:NT + t + 1], ss[0:n, t:t + 1], 1.0 / D, EPS,
                                      ALU.mult, ALU.add).then_inc(mean_ready, 1)
                dve.wait_ge(gain_in, 16)
                for t, (_, n) in enumerate(TILES):
                    dve.wait_ge(root_ready, t + 1)
                    step(dve.reciprocal(ss[0:n, 2 * NT + t:2 * NT + t + 1], ss[0:n, t:t + 1]))
                    dve.scalar_tensor_tensor(out=h[0:n, t, :], in0=M.x[0:n, t, :],
                                             scalar=ss[0:n, 2 * NT + t:2 * NT + t + 1], in1=gain_b[0:n, :],
                                             op0=ALU.mult, op1=ALU.mult).then_inc(h_ready, 1)

            @block.tensor
            def _(pe):
                if pe_first is not None:
                    pe_first(pe)
                for k, (t, g) in enumerate(groups):
                    n = TILES[t][1]
                    pe.wait_ge(h_ready, t + 1)
                    if k >= 4:
                        pe.wait_ge(copied, k - 3)
                    for c in range(4):
                        mm = pe.transpose(tr[k % 4][:, c, 0:n], h[0:n, t, (4 * g + c) * P:(4 * g + c + 1) * P],
                                          M.ident[0:n, 0:n])
                    mm.then_inc(turned, 1)

            @block.scalar
            def _(act):
                for t, (_, n) in enumerate(TILES):
                    act.wait_ge(mean_ready, t + 1)
                    act.activation(ss[0:n, t:t + 1], ss[0:n, NT + t:NT + t + 1], ACT.Sqrt).then_inc(root_ready, 1)
                if act_first is not None:
                    act_first(act)
                for k, (t, g) in enumerate(groups):
                    t0, n = TILES[t]
                    act.wait_ge(turned, k + 1)
                    act.activation(M.h_T[:, 4 * g:4 * g + 4, t0:t0 + n], tr[k % 4][:, :, 0:n],
                                   ACT.Copy).then_inc(copied, 1)


def turn_stage(nc, name, M, src):
    with Stage(nc, name) as st:
        tr = [st.ps(f"tr{i}", [P, 4, P]) for i in range(4)]
        turned = st.sem("turned")
        copied = st.sem("copied")
        groups = [(t, g) for t in range(NT) for g in range(DC // 4)]
        with nc.Block() as block:

            @block.tensor
            def _(pe):
                for k, (t, g) in enumerate(groups):
                    n = TILES[t][1]
                    if k >= 4:
                        pe.wait_ge(copied, k - 3)
                    for c in range(4):
                        mm = pe.transpose(tr[k % 4][:, c, 0:n], src[0:n, t, (4 * g + c) * P:(4 * g + c + 1) * P],
                                          M.ident[0:n, 0:n])
                    mm.then_inc(turned, 1)

            @block.scalar
            def _(act):
                for k, (t, g) in enumerate(groups):
                    t0, n = TILES[t]
                    act.wait_ge(turned, k + 1)
                    act.activation(M.h_T[:, 4 * g:4 * g + 4, t0:t0 + n], tr[k % 4][:, :, 0:n],
                                   ACT.Copy).then_inc(copied, 1)


WB = 512
WRING = 3


def project_stage(nc, name, M, weight, jobs, gain=None, turn=None, loads=None):
    w_view = weight.rearrange("(c p) n -> p c n", p=P)
    with Stage(nc, name) as st:
        w = st.sb("w", [P, WRING, DC, WB])
        gain_b = st.sb("gain", [P, D]) if gain is not None else None
        w_in = [st.sem(f"w_in{i}") for i in range(WRING)]
        gain_in = st.sem("gain_in")

        def load(sp, j):
            col, n, _, _ = jobs[j]
            sp.dma_start(w[:, j % WRING, :, 0:n], w_view[:, :, col:col + n]).then_inc(w_in[j % WRING], 16)

        with nc.Block() as block:

            @block.sync
            def _(sp):
                if gain is not None:
                    sp.dma_start(gain_b[:], gain.partition_broadcast(P)).then_inc(gain_in, 16)
                for j in range(min(WRING, len(jobs))):
                    load(sp, j)

        if gain is not None:
            norm_stage(nc, name + "n", M, gain_b, gain_in)
        else:
            turn_stage(nc, name + "t", M, turn)

        acc = [st.ps(f"acc{i}", [P, 512]) for i in range(8)]
        summed = st.sem("summed")
        stored = st.sem("stored")
        outs, ends = [], []
        for j, (col, n, kind, dst) in enumerate(jobs):
            for k in range(-(-n // P) if kind == "T" else NT):
                outs.append((j, k))
            ends.append(len(outs))
        with nc.Block() as block:

            @block.sync
            def _(sp):
                for j in range(WRING, len(jobs)):
                    sp.wait_ge(summed, ends[j - WRING])
                    load(sp, j)

            if loads is not None:

                @block.gpsimd
                def _(pool):
                    loads(pool)

            @block.tensor
            def _(pe):
                for q, (j, k) in enumerate(outs):
                    _, n, kind, _ = jobs[j]
                    pe.wait_ge(w_in[j % WRING], 16 * (j // WRING + 1))
                    if q >= 8:
                        pe.wait_ge(stored, q - 7)
                    t0, nt = TILES[k] if kind != "T" else (0, 0)
                    for c in range(DC):
                        if kind == "T":
                            mm = pe.matmul(acc[q % 8][:, 0:NTOK], w[:, j % WRING, c, k * P:(k + 1) * P],
                                           M.h_T[:, c, :], start=(c == 0), stop=(c == DC - 1))
                        else:
                            mm = pe.matmul(acc[q % 8][0:nt, 0:n], M.h_T[:, c, t0:t0 + nt],
                                           w[:, j % WRING, c, 0:n], start=(c == 0), stop=(c == DC - 1))
                    mm.then_inc(summed, 1)

            if jobs[0][2] == "add":

                @block.vector
                def _(dve):
                    for q, (j, k) in enumerate(outs):
                        col, n, _, _ = jobs[j]
                        nt = TILES[k][1]
                        dve.wait_ge(summed, q + 1)
                        dve.tensor_tensor(M.x[0:nt, k, col:col + n], acc[q % 8][0:nt, 0:n],
                                          M.x[0:nt, k, col:col + n], ALU.add).then_inc(stored, 1)
            else:

                @block.scalar
                def _(act):
                    for q, (j, k) in enumerate(outs):
                        _, n, kind, dst = jobs[j]
                        place, func, scale = dst(k)
                        act.wait_ge(summed, q + 1)
                        src = acc[q % 8][:, 0:NTOK] if kind == "T" else acc[q % 8][0:TILES[k][1], 0:n]
                        if len(place.shape) == 3:
                            src = src.rearrange("p (a b) -> p a b", a=place.shape[1])
                        if len(place.shape) == 4:
                            src = src.rearrange("p (a b c) -> p a b c", a=place.shape[1], b=place.shape[2])
                        act.activation(place, src, func, scale=scale).then_inc(stored, 1)


def add_jobs():
    return [(c, WB, "add", None) for c in range(0, D, WB)]


def mlstm_stage(nc, M, I, O):
    with Stage(nc, "mx") as outer:
        q_T = outer.sb("q_T", [P, 4, NTOK])
        k_T = outer.sb("k_T", [P, 4, NTOK])
        v = outer.sb("v", [P, NT, MH, VW])
        og = outer.sb("og", [P, NT, D])
        gates = outer.sb("gates", [P, NT, 2 * MH])
        state = outer.sb("state", [P, 4, MH, VW])
        m_nat = outer.sb("m_nat", [NDEC, MH])
        m_T = outer.sb("m_T", [MH, DEC_B])
        bias = outer.sb("bias", [P, 2 * MH])
        hn = outer.sb("hn", [P, D])
        hid = outer.sb("hid", [P, NT, D])
        w_in, C_in = I["mlstm_w_in"][0], I["state_C"][0]
        loads_done = outer.sem("loads_done")
        zeroed = outer.sem("zeroed")

        with nc.Block() as block:

            @block.vector
            def _(dve):
                dve.memset(v[:, :, :, MDV:VW], 1.0).then_inc(zeroed, 1)
                dve.memset(gates[:], 0.0).then_inc(zeroed, 1)
                dve.wait_ge(zeroed, 2)

        def load_state(pool):
            for b2 in range(2):
                for b4 in range(4):
                    pool.dma_start(state[64 * b2:64 * b2 + 64, b4, :, 0:MDV],
                                   C_in[2 * b4 + b2].rearrange("h k v -> k h v")).then_inc(loads_done, 16)
            with nc.allow_non_contiguous_dma(reason="the normaliser's and stabiliser's few scalars"):
                for b2 in range(2):
                    for b4 in range(4):
                        pool.dma_start(state[64 * b2:64 * b2 + 64, b4, :, MDV:VW],
                                       I["state_n"][0, 2 * b4 + b2].rearrange("h (k u) -> k h u", u=1)
                                       ).then_inc(loads_done, 16)
                pool.dma_start(m_T[:], I["state_m"][0].rearrange("b h -> h b")).then_inc(loads_done, 16)
            for b in range(DEC_B):
                pool.dma_start(m_nat[DEC_S * b:DEC_S * b + DEC_S, :],
                               I["state_m"][0, b].partition_broadcast(DEC_S)).then_inc(loads_done, 16)
            pool.dma_start(bias[:, 0:MH], I["mlstm_b_i"][0].partition_broadcast(P)).then_inc(loads_done, 16)
            pool.dma_start(bias[:, MH:2 * MH], I["mlstm_b_f"][0].partition_broadcast(P)).then_inc(loads_done, 16)
            pool.dma_start(hn[:], I["mlstm_head_norm"][0].partition_broadcast(P)).then_inc(loads_done, 16)

        def v_dst(j):
            return lambda t: (v[0:TILES[t][1], t, 4 * j:4 * j + 4, 0:MDV], ACT.Copy, 1.0)

        def o_dst(j):
            return lambda t: (og[0:TILES[t][1], t, WB * j:WB * j + WB], ACT.Sigmoid, 1.0)

        o2, o3, o4 = 2 * MH * MDK, 2 * MH * MDK + D, 2 * MH * MDK + 2 * D
        project_stage(nc, "mp", M, w_in, [
            (0, WB, "T", lambda c: (q_T[:, c, :], ACT.Copy, 1.0)),
            (WB, WB, "T", lambda c: (k_T[:, c, :], ACT.Copy, MDK ** -0.5)),
            (o2, WB, "N", v_dst(0)), (o2 + WB, WB, "N", v_dst(1)),
            (o4, 2 * MH, "N", lambda t: (gates[0:TILES[t][1], t, :], ACT.Copy, 1.0)),
            (o3, WB, "N", o_dst(0)), (o3 + WB, WB, "N", o_dst(1))], gain=I["norm_mix"][0], loads=load_state)

        with Stage(nc, "mr") as st:
            kn = st.sb("kn", [P, NT, MH, MDK])
            z = st.sb("z", [P, 4, NT, MH])
            lf = st.sb("lf", [P, NT, MH])
            li = st.sb("li", [P, NT, MH])
            b_cum = st.sb("b_cum", [P, NT, MH])
            g = st.sb("g", [P, NT, MH])
            g_T = st.sb("g_T", [MH, NT, P])
            top_T = st.sb("top_T", [MH, NT, P])
            ntop_T = st.sb("ntop_T", [MH, NT, P])
            top = st.sb("top", [P, NT, MH])
            m_prev = st.sb("m_prev", [P, NT, MH])
            m_all = st.sb("m_all", [P, NT, MH])
            m_end = st.sb("m_end", [MH, NT, P])
            zero_T = st.sb("zero_T", [MH, 1])
            w_all = st.sb("w_all", [P, 3, NT, MH])
            arg = st.sb("arg", [P, 3, NT, MH])
            dec = st.sb("dec", [P, 5, MH])
            kw = st.sb("kw", [P, NT, MH, MDK])
            kws = st.sb("kws", [NDEC, MH, DEC_B, MDK])
            qd = st.sb("qd", [P, MH, NDEC])
            qs = st.sb("qs", [P, MH, 4, NDEC])
            C = st.sb("C", [P, 4, VW])
            W = st.sb("W", [P, 2, P])
            PT = st.sb("PT", [P, 2, P])
            carry = st.sb("carry", [P, 2, VW])
            nd = st.sb("nd", [P, NT, MH, VW])
            fl = st.sb("fl", [P, 4, NT, MH])
            ps_a = st.ps("ps_a", [P, 512])
            ps_s = [st.ps(f"ps_s{i}", [P, 512]) for i in range(2)]
            ps_n = [st.ps(f"ps_n{i}", [P, 512]) for i in range(2)]
            ps_i = st.ps("ps_i", [P, 512])
            ps_kn = [ps_i, *ps_n]
            ps_c = [st.ps(f"ps_c{i}", [P, 2, VW]) for i in range(2)]
            vec, sca, ten = st.sem("vec"), st.sem("sca"), st.sem("ten")
            az_ready, l_ready = st.sem("az_ready"), st.sem("l_ready")
            gate_mm, gate_cp = st.sem("gate_mm"), st.sem("gate_cp")
            arg_ready, w_ready = st.sem("arg_ready"), st.sem("w_ready")
            kn_mm, kn_cp = st.sem("kn_mm"), st.sem("kn_cp")
            scored, weighed, probs = st.sem("scored"), st.sem("weighed"), st.sem("probs")
            summed, carried, joined = st.sem("summed"), st.sem("carried"), st.sem("joined")
            ms_ready, rt_ready = st.sem("ms_ready"), st.sem("rt_ready")
            out_done, prep = st.sem("out_done"), st.sem("prep")
            pooled, spread, gained, kws_ready = (st.sem(n) for n in ("pooled", "spread", "gained", "kws_ready"))
            cm = {n: M.c(n) for n in ("tri", "tri_dec", "mask", "mask_dec", "sel_head", "last", "last_dec",
                                      "last_state", "seq_q", "seq_k")}
            tri = [cm["tri"], cm["tri"], cm["tri_dec"]]
            mask = [cm["mask"], cm["mask"], cm["mask_dec"]]
            last = [cm["last"], cm["last"], cm["last_dec"]]
            GP = 7
            LOADS = 28

            with nc.Block() as block:

                @block.tensor
                def _(pe):
                    pe.wait_ge(loads_done, 16 * LOADS)

                    def gate_product(t, k):
                        n = TILES[t][1]
                        pe.wait_ge(gate_cp, GP * t + k + 1)
                        if k == 0:
                            mm = pe.matmul(ps_a[0:n, 0:MH], tri[t][0:n, 0:n], lf[0:n, t, :], start=True, stop=True)
                        elif k == 1:
                            mm = pe.transpose(ps_a[0:MH, 0:n], g[0:n, t, :], M.ident[0:n, 0:n])
                        elif k == 2:
                            mm = pe.transpose(ps_a[0:n, 0:MH], top_T[:, t, 0:n], M.ident[0:MH, 0:MH])
                        elif k == 3:
                            mm = pe.matmul(ps_a[0:n, 0:MH], last[t][0:n, 0:n], top[0:n, t, :], start=True, stop=True)
                        elif k == 4:
                            mm = pe.transpose(ps_a[0:MH, 0:n], m_all[0:n, t, :], M.ident[0:n, 0:n])
                        elif k == 5:
                            mm = pe.matmul(ps_a[0:n, 0:MH], last[t][0:n, 0:n], m_all[0:n, t, :], start=True, stop=True)
                        else:
                            pe.wait_ge(w_ready, t + 1)
                            if t < 2:
                                mm = pe.matmul(ps_a[:, 0:MH], cm["last"], w_all[:, 0, t, :], start=True, stop=True)
                            else:
                                for b4 in range(4):
                                    mm = pe.matmul(ps_a[:, b4 * MH:(b4 + 1) * MH], cm["last_state"][:, b4, :],
                                                   w_all[0:n, 0, t, :], start=True, stop=True)
                        mm.then_inc(gate_mm, 1)

                    for t, (t0, n) in enumerate(TILES):
                        for c in range(4):
                            mm = pe.transpose(ps_kn[t][0:n, c * P:(c + 1) * P], k_T[:, c, t0:t0 + n], M.ident[:, :])
                        mm.then_inc(kn_mm, 1)
                    for k in range(GP):
                        gate_product(0, k)
                    pe.wait_ge(kn_cp, NT)
                    for t, (t0, n) in enumerate(TILES):

                        def scores(h):
                            u = t * MH + h
                            hp, hb = h // 2, 64 * (h % 2)
                            if u >= 2:
                                pe.wait_ge(probs, u - 1)
                            pe.matmul(ps_s[u % 2][0:n, 0:n], k_T[hb:hb + MDK, hp, t0:t0 + n],
                                      q_T[hb:hb + MDK, hp, t0:t0 + n], start=True, stop=True)
                            pe.matmul(ps_s[u % 2][0:n, P:P + n], cm["sel_head"][:, h, 0:n], ntop_T[:, t, 0:n],
                                      start=True, stop=False)
                            pe.matmul(ps_s[u % 2][0:n, P:P + n], M.ident[0:n, 0:n], mask[t][0:n, 0:n],
                                      start=False, stop=True).then_inc(scored, 1)

                        pe.wait_ge(prep, t + 1)
                        if t == 2:
                            pe.wait_ge(spread, 1)
                        scores(0)
                        for h in range(MH):
                            u = t * MH + h
                            hp, hb = h // 2, 64 * (h % 2)
                            if h + 1 < MH:
                                scores(h + 1)
                            pe.wait_ge(probs, u + 1)
                            if u >= 2:
                                pe.wait_ge(joined, u - 1)
                            mm = pe.matmul(ps_n[u % 2][0:n, 0:VW], PT[0:n, u % 2, 0:n], v[0:n, t, h, :],
                                           start=True, stop=True)
                            if t == 1:
                                pe.wait_ge(joined, h + 1)
                                pe.matmul(ps_n[u % 2][0:n, 2 * P:2 * P + VW], q_T[hb:hb + MDK, hp, t0:t0 + n],
                                          C[hb:hb + MDK, hp, :], start=True, stop=True)
                            if t == 2:
                                for b4 in range(4):
                                    pe.matmul(ps_n[u % 2][0:n, 2 * P:2 * P + VW], qs[:, h, b4, :], state[:, b4, h, :],
                                              start=(b4 == 0), stop=(b4 == 3))
                                pe.wait_ge(joined, u)
                                if h == 0:
                                    pe.wait_ge(kws_ready, 1)
                                for b4 in range(4):
                                    mm = pe.matmul(ps_c[b4 // 2][:, b4 % 2, :],
                                                   kws[:, h, 2 * b4:2 * b4 + 2, :].rearrange("p b k -> p (b k)"),
                                                   v[0:n, t, h, :], start=True, stop=True)
                            else:
                                mm = pe.matmul(ps_c[u % 2][hb:hb + MDK, 0, :], kw[0:n, t, h, :], v[0:n, t, h, :],
                                               start=True, stop=True)
                            mm.then_inc(summed, 1)
                            if t + 1 < NT and h < GP:
                                gate_product(t + 1, h)

                @block.gpsimd
                def _(pool):
                    for hp in range(4):
                        for h2 in range(2):
                            for b2 in range(2):
                                pool.tensor_copy(qd[64 * b2:64 * b2 + 64, 2 * hp + h2, :],
                                                 q_T[64 * h2:64 * h2 + 64, hp, SEQ:NTOK]).then_inc(pooled, 1)
                    pool.wait_ge(pooled, 2 * MH)
                    for h in range(MH):
                        ins = pool.tensor_tensor(qs[:, h], qd[:, h, None, :].to_broadcast([P, 4, NDEC]),
                                                 cm["seq_q"], ALU.mult).then_inc(pooled, 1)
                    pool.wait_ge(pooled, 3 * MH)
                    pool.nop().then_inc(spread, 1)
                    pool.wait_ge(loads_done, 16 * LOADS)
                    for t, (_, n) in enumerate(TILES):
                        pool.tensor_tensor(og[0:n, t], og[0:n, t], hn[0:n], ALU.mult).then_inc(gained, 1)
                    pool.wait_ge(prep, NT)
                    for h in range(MH):
                        pool.tensor_tensor(kws[:, h], kw[0:NDEC, 2, h, None, :].to_broadcast([NDEC, DEC_B, MDK]),
                                           cm["seq_k"][:, :, None].to_broadcast([NDEC, DEC_B, MDK]),
                                           ALU.mult).then_inc(pooled, 1)
                    pool.wait_ge(pooled, 4 * MH)
                    pool.nop().then_inc(kws_ready, 1)

                def carry_of(act, t, h):
                    u, n = t * MH + h, TILES[t][1]
                    act.wait_ge(summed, u + 1)
                    act.wait_ge(joined, u - 1)
                    act.activation(carry[0:n, u % 2, :], ps_n[u % 2][0:n, 2 * P:2 * P + VW], ACT.Copy,
                                   scale=w_all[0:n, 0, t, h:h + 1]).then_inc(carried, 1)

                @block.scalar
                def _(act):
                    step = Chain(act, sca)

                    def weights(t):
                        n = TILES[t][1]
                        act.wait_ge(arg_ready, t + 1)
                        act.activation(w_all[0:n, :, t, :], arg[0:n, :, t, :], ACT.Exp).then_inc(w_ready, 1)

                    act.wait_ge(az_ready, 1)
                    step(act.activation(z[:, 2], z[:, 1], ACT.Exp, scale=-1.0))
                    act.activation(z[:, 3], z[:, 2], ACT.Ln, bias=1.0).then_inc(l_ready, 1)
                    weights(0)
                    for t, (t0, n) in enumerate(TILES):
                        for h in range(MH):
                            u = t * MH + h
                            act.wait_ge(scored, u + 1)
                            if u >= 2:
                                act.wait_ge(probs, u - 1)
                            act.activation(W[0:n, u % 2, 0:n], ps_s[u % 2][0:n, P:P + n], ACT.Exp,
                                           bias=g[0:n, t, h:h + 1]).then_inc(weighed, 1)
                            if t >= 1 and h >= 1:
                                carry_of(act, t, h - 1)
                            if t + 1 < NT and h == 5:
                                weights(t + 1)
                        if t >= 1:
                            carry_of(act, t, MH - 1)
                    for t, (_, n) in enumerate(TILES):
                        act.wait_ge(ms_ready, t + 1)
                        act.activation(fl[0:n, 3, t], fl[0:n, 2, t], ACT.Sqrt).then_inc(rt_ready, 1)

                @block.vector
                def _(dve):
                    step = Chain(dve, vec)
                    hv = hid[:].rearrange("p t (h v) -> p t h v", h=MH)

                    def gate_answer(t, k):
                        n = TILES[t][1]
                        if k:
                            dve.wait_ge(gate_mm, GP * t + k)
                        if k == 1:
                            step(dve.tensor_copy(b_cum[0:n, t], ps_a[0:n, 0:MH]))
                            step(dve.tensor_tensor(g[0:n, t], li[0:n, t], b_cum[0:n, t], ALU.subtract))
                        elif k == 2:
                            step(dve.tensor_copy(g_T[:, t, 0:n], ps_a[0:MH, 0:n]))
                            if t < 2:
                                start = zero_T[:] if t == 0 else m_end[:, 0, P - 1:P]
                                step(dve.tensor_tensor_scan(top_T[:, t, :], g_T[:, t, :], g_T[:, t, :], start,
                                                            ALU.max, ALU.max))
                            else:
                                gs = g_T[:, t, 0:n].rearrange("p (b s) -> p b s", s=DEC_S)
                                ts = top_T[:, t, 0:n].rearrange("p (b s) -> p b s", s=DEC_S)
                                for s in range(DEC_S):
                                    before = m_T[:] if s == 0 else ts[:, :, s - 1]
                                    step(dve.tensor_tensor(ts[:, :, s], gs[:, :, s], before, ALU.max))
                            step(dve.tensor_scalar(ntop_T[:, t, 0:n], top_T[:, t, 0:n], -1.0, None, ALU.mult))
                        elif k == 3:
                            step(dve.tensor_copy(top[0:n, t], ps_a[0:n, 0:MH]))
                            step(dve.tensor_tensor(m_all[0:n, t], top[0:n, t], b_cum[0:n, t], ALU.add))
                        elif k == 4:
                            step(dve.tensor_tensor(arg[0:n, 1, t], g[0:n, t], ps_a[0:n, 0:MH], ALU.subtract))
                            step(dve.tensor_tensor(arg[0:n, 0, t], m_prev[0:n, t], top[0:n, t], ALU.subtract))
                            step(dve.tensor_scalar(arg[0:n, 2, t], m_all[0:n, t], -1.0, None, ALU.mult))
                            dve.nop().then_inc(arg_ready, 1)
                        elif k == 5:
                            step(dve.tensor_copy(m_end[:, t, 0:n], ps_a[0:MH, 0:n]))
                        elif k == 6:
                            if t == 0:
                                step(dve.tensor_copy(m_prev[:, 1, :], ps_a[:, 0:MH]))
                        elif k == 7:
                            if t < 2:
                                step(dve.tensor_copy(dec[:, 0, :], ps_a[:, 0:MH]))
                            else:
                                step(dve.tensor_copy(dec[:, 1:5, :],
                                                     ps_a[:, 0:4 * MH].rearrange("p (b h) -> p b h", b=4)))
                            dve.wait_ge(w_ready, t + 1)
                            dve.tensor_tensor(kw[0:n, t], kn[0:n, t],
                                              w_all[0:n, 1, t, :, None].to_broadcast([n, MH, MDK]), ALU.mult
                                              ).then_inc(prep, 1)
                        if k < GP:
                            dve.nop().then_inc(gate_cp, 1)

                    def finish(t, k):
                        n = TILES[t][1]
                        if k == 0:
                            dve.wait_ge(joined, (t + 1) * MH)
                            den = nd[0:n, t, :, MDV]
                            step(dve.tensor_scalar(fl[0:n, 0, t], den, -1.0, None, ALU.mult))
                            step(dve.tensor_tensor(fl[0:n, 0, t], fl[0:n, 0, t], den, ALU.max))
                            step(dve.tensor_tensor(fl[0:n, 0, t], fl[0:n, 0, t], w_all[0:n, 2, t], ALU.max))
                            step(dve.reciprocal(fl[0:n, 1, t], fl[0:n, 0, t]))
                        elif k == 1:
                            step(dve.tensor_tensor(hv[0:n, t], nd[0:n, t, :, 0:MDV],
                                                   fl[0:n, 1, t, :, None].to_broadcast([n, MH, MDV]), ALU.mult))
                        elif k == 2:
                            step(dve.tensor_tensor(nd[0:n, t, :, 0:MDV], hv[0:n, t], hv[0:n, t], ALU.mult))
                        elif k == 3:
                            step(dve.tensor_reduce(fl[0:n, 0, t], nd[0:n, t, :, 0:MDV], AX.X, ALU.add))
                            dve.tensor_scalar(fl[0:n, 2, t], fl[0:n, 0, t], 1.0 / MDV, EPS, ALU.mult, ALU.add
                                              ).then_inc(ms_ready, 1)

                    def weigh(u):
                        n = TILES[u // MH][1]
                        dve.wait_ge(weighed, u + 1)
                        if u >= 2:
                            dve.wait_ge(summed, u - 1)
                        dve.tensor_tensor(PT[0:n, u % 2, 0:n], ps_s[u % 2][0:n, 0:n], W[0:n, u % 2, 0:n],
                                          ALU.mult).then_inc(probs, 1)

                    dve.wait_ge(loads_done, 16 * LOADS)
                    bcast = bias[:, None, 0:MH].to_broadcast([P, NT, MH])
                    bcast_f = bias[:, None, MH:2 * MH].to_broadcast([P, NT, MH])
                    step(dve.tensor_tensor(z[:, 0], gates[:, :, MH:2 * MH], bcast_f, ALU.add))
                    step(dve.tensor_scalar(z[:, 1], z[:, 0], -1.0, None, ALU.mult))
                    step(dve.tensor_tensor(z[:, 1], z[:, 0], z[:, 1], ALU.max))
                    dve.nop().then_inc(az_ready, 1)
                    step(dve.tensor_scalar(z[:, 0], z[:, 0], 0.0, None, ALU.min))
                    step(dve.tensor_tensor(li[:], gates[:, :, 0:MH], bcast, ALU.add))
                    step(dve.memset(zero_T[:], 0.0))
                    step(dve.memset(m_prev[:, 0, :], 0.0))
                    step(dve.tensor_copy(m_prev[0:NDEC, 2, :], m_nat[:]))
                    dve.wait_ge(l_ready, 1)
                    step(dve.tensor_tensor(lf[:], z[:, 0], z[:, 3], ALU.subtract))
                    gate_answer(0, 0)
                    for t, (t0, n) in enumerate(TILES):
                        dve.wait_ge(kn_mm, t + 1)
                        dve.tensor_copy(kn[0:n, t], ps_kn[t][0:n, :].rearrange("p (h k) -> p h k", h=MH)
                                        ).then_inc(kn_cp, 1)
                    for k in range(1, 8):
                        if k == 7:
                            dve.wait_ge(kn_cp, NT)
                        gate_answer(0, k)
                    for t, (t0, n) in enumerate(TILES):
                        if t + 1 < NT:
                            gate_answer(t + 1, 0)
                        weigh(t * MH)
                        for h in range(MH):
                            u = t * MH + h
                            hp, hb = h // 2, 64 * (h % 2)
                            if h + 1 < MH:
                                weigh(u + 1)
                            dve.wait_ge(summed, u + 1)
                            if t == 0:
                                step(dve.tensor_copy(C[hb:hb + MDK, hp, :], ps_c[u % 2][hb:hb + MDK, 0, :]))
                                dve.tensor_copy(nd[0:n, t, h, :], ps_n[u % 2][0:n, 0:VW]).then_inc(joined, 1)
                            else:
                                if t == 1:
                                    step(dve.scalar_tensor_tensor(
                                        out=C[hb:hb + MDK, hp, :], in0=C[hb:hb + MDK, hp, :],
                                        scalar=dec[hb:hb + MDK, 0, h:h + 1], in1=ps_c[u % 2][hb:hb + MDK, 0, :],
                                        op0=ALU.mult, op1=ALU.add))
                                else:
                                    for b4 in range(4):
                                        step(dve.scalar_tensor_tensor(
                                            out=state[:, b4, h, :], in0=state[:, b4, h, :],
                                            scalar=dec[:, 1 + b4, h:h + 1], in1=ps_c[b4 // 2][:, b4 % 2, :],
                                            op0=ALU.mult, op1=ALU.add))
                                dve.wait_ge(carried, (t - 1) * MH + h + 1)
                                dve.tensor_tensor(nd[0:n, t, h, :], ps_n[u % 2][0:n, 0:VW], carry[0:n, u % 2, :],
                                                  ALU.add).then_inc(joined, 1)
                            if t + 1 < NT and h < GP:
                                gate_answer(t + 1, h + 1)
                            if t and h < 4:
                                finish(t - 1, h)
                    for k in range(4):
                        finish(NT - 1, k)
                    for t, (_, n) in enumerate(TILES):
                        dve.wait_ge(rt_ready, t + 1)
                        step(dve.reciprocal(fl[0:n, 1, t], fl[0:n, 3, t]))
                        step(dve.tensor_tensor(hv[0:n, t], hv[0:n, t],
                                               fl[0:n, 1, t, :, None].to_broadcast([n, MH, MDV]), ALU.mult))
                        dve.wait_ge(gained, t + 1)
                        step(dve.tensor_tensor(hid[0:n, t], hid[0:n, t], og[0:n, t], ALU.mult))

                @block.sync
                def _(sp):
                    sp.dma_start(O["win_s"][0, :, 0:WIN - DEC_S], I["state_win_kv"][0, :, DEC_S:WIN]
                                 ).then_inc(out_done, 16)
                    sp.wait_ge(joined, NT * MH)
                    for b2 in range(2):
                        sp.dma_start(O["C_p"][0, 0].rearrange("(a b) k v -> b k a v", b=2)[b2],
                                     C[64 * b2:64 * b2 + 64, :, 0:MDV]).then_inc(out_done, 16)
                        for b4 in range(4):
                            sp.dma_start(O["C_s"][0, 2 * b4 + b2].rearrange("h k v -> k h v"),
                                         state[64 * b2:64 * b2 + 64, b4, :, 0:MDV]).then_inc(out_done, 16)
                    with nc.allow_non_contiguous_dma(reason="the normaliser's and stabiliser's few scalars"):
                        for b2 in range(2):
                            sp.dma_start(O["n_p"][0, 0].rearrange("(a b) (k u) -> b k a u", b=2, u=1)[b2],
                                         C[64 * b2:64 * b2 + 64, :, MDV:VW]).then_inc(out_done, 16)
                            for b4 in range(4):
                                sp.dma_start(O["n_s"][0, 2 * b4 + b2].rearrange("h (k u) -> k h u", u=1),
                                             state[64 * b2:64 * b2 + 64, b4, :, MDV:VW]).then_inc(out_done, 16)
                        sp.dma_start(O["m_p"][0, 0].rearrange("(h u) -> h u", u=1), m_end[:, 1, P - 1:P]
                                     ).then_inc(out_done, 16)
                        sp.dma_start(O["m_s"][0].rearrange("b h -> h b"),
                                     m_end[:, 2, DEC_S - 1:NDEC:DEC_S]).then_inc(out_done, 16)
                    sp.wait_ge(out_done, 16 * 23)

        project_stage(nc, "mo", M, I["mlstm_w_out"][0], add_jobs(), turn=hid)


KEY_ROWS = PAST // CSTR
N_CMP = KEY_ROWS - 1
GD = AG * ADH
NPC = SEQ // CSTR - 1
HALF_L = CSTR // 2
HALF_ROW = HALF_L * 2 * GD
GK = CSTR
BEATS = 8


class Compressor:

    def __init__(self, nc, st, n, key_out, value_out):
        self.nc, self.n, self.key_out, self.value_out = nc, n, key_out, value_out
        self.rows = st.sb("rows", [P, 2, HALF_ROW])
        self.w1 = st.sb("w1", [P, 2, CSTR // 2, 2, ADH])
        self.w2 = st.sb("w2", [ADH, 2, ADH])
        self.b1 = st.sb("b1", [ADH, 2])
        self.sub_T = st.sb("sub_T", [P, 4, 4, P])
        self.second = st.sb("second", [ADH, 2, AG, P])
        self.pre = st.sb("pre", [ADH, 2, AG, P])
        self.hid = st.sb("hid", [ADH, 2, AG, P])
        self.tr = [st.ps(f"ctr{i}", [P, 4, P]) for i in range(2)]
        self.ps_h = [st.ps(f"ps_h{i}", [P, AG, P]) for i in range(2)]
        ps_out = st.ps("ps_out", [P, 512])
        self.ps_k = ps_out[:, 0:2 * P].rearrange("p (a n) -> p a n", a=2)
        self.ps_v = ps_out[:, 2 * P:4 * P]
        self.weights_in = st.sem("weights_in")
        self.rows_in = [st.sem(f"rows_in{i}") for i in range(2)]
        self.turned = st.sem("turned")
        self.copied = [st.sem("copied_act"), st.sem("copied_dve")]
        self.multiplied = st.sem("multiplied")
        self.second_ready = st.sem("second_ready")
        self.pre_ready, self.hid_ready = st.sem("pre_ready"), st.sem("hid_ready")
        self.out_mm, self.out_cp = st.sem("out_mm"), st.sem("out_cp")

    LOADS = 2 * 2 + 2 + 1

    def load_weights(self, sp, I):
        for c in range(2):
            for f in range(2):
                sp.dma_start(self.w1[:, c, :, f], I["nsa_cmp_w1"][0, c, f * CSTR:(f + 1) * CSTR].rearrange(
                    "(k l) d h -> (l d) k h", l=2)).then_inc(self.weights_in, 16)
            sp.dma_start(self.w2[:, c], I["nsa_cmp_w2"][0, c]).then_inc(self.weights_in, 16)
        with self.nc.allow_non_contiguous_dma(reason="128 biases"):
            sp.dma_start(self.b1[:], I["nsa_cmp_b1"][0].rearrange("c h -> h c")).then_inc(self.weights_in, 16)

    def start_act(self, act):
        act.nop().then_inc(self.copied[0], 1)
        act.nop().then_inc(self.hid_ready, 2)
        act.nop().then_inc(self.out_cp, 2)
        act.nop().then_inc(self.multiplied, 4)
        act.nop().then_inc(self.out_mm, 2)
        act.wait_ge(self.weights_in, 16 * self.LOADS)

    def start_dve(self, dve):
        dve.nop().then_inc(self.copied[1], 1)
        dve.nop().then_inc(self.pre_ready, 2)


    def turn(self, pe, b, k):
        n, e, c, kk = self.n, k // 8, (k // 4) % 2, k % 4
        tile = self.rows[0:n, e, :].rearrange("p (k l c a gd) -> p k l c a gd", k=4, l=2, c=2, a=2)
        if k % 8 == 0:
            pe.wait_ge(self.rows_in[e], 16 * b + 16)
        pe.wait_ge(self.copied[k % 2], (GK // 2) * b + k // 2 + 1)
        for l in range(2):
            for a in range(2):
                mm = pe.transpose(self.tr[k % 2][:, 2 * l + a, 0:n], tile[:, kk, l, c, a, :], self.ident[0:n, 0:n])
        mm.then_inc(self.turned, 1)

    def product(self, pe, b, k):
        n, e, c, kk = self.n, k // 8, (k // 4) % 2, k % 4
        pe.wait_ge(self.copied[k % 2], (GK // 2) * b + k // 2 + 2)
        if e == 0 and kk == 0:
            pe.wait_ge(self.pre_ready, 2 * b + c + 1)
        pe.matmul(self.ps_h[c][:, :, 0:n], self.w1[:, c, 4 * e + kk].rearrange("p f h -> p (f h)"),
                  self.sub_T[:, k % 4, :, 0:n], start=(e == 0 and kk == 0), stop=(e == 1 and kk == 3)
                  ).then_inc(self.multiplied, 1)

    def outputs(self, pe, b, c):
        n = self.n
        for g in range(AG):
            if c == 0:
                mm = pe.matmul(self.ps_k[ADH * (g % 2):ADH * (g % 2) + ADH, g // 2, 0:n - 1], self.w2[:, 0, :],
                               self.hid[:, 0, g, 0:n - 1], start=True, stop=True)
            else:
                mm = pe.matmul(self.ps_v[0:n - 1, g * ADH:(g + 1) * ADH], self.hid[:, 1, g, 0:n - 1],
                               self.w2[:, 1, :], start=True, stop=True)
        mm.then_inc(self.out_mm, 1)

    def pe_before(self, pe, b, beat, live, prev):
        if prev and beat == 2:
            pe.wait_ge(self.hid_ready, 2 * b + 2)
            pe.wait_ge(self.out_cp, 2 * b)
            self.outputs(pe, b - 1, 1)
        if live:
            self.turn(pe, b, 2 * beat)
            self.turn(pe, b, 2 * beat + 1)

    def pe_after(self, pe, b, beat, live, prev):
        if not live:
            return
        self.product(pe, b, 2 * beat)
        if beat == 7:
            pe.wait_ge(self.hid_ready, 2 * b + 3)
            pe.wait_ge(self.out_cp, 2 * b + 1)
        self.product(pe, b, 2 * beat + 1)
        if beat == 7:
            self.outputs(pe, b, 0)


    def copy(self, engine, b, k):
        n = self.n
        engine.wait_ge(self.turned, GK * b + k + 1)
        engine.wait_ge(self.multiplied, GK * b + k + 1)
        for l in range(2):
            for g2 in range(2):
                dst = self.sub_T[ADH * l:ADH * l + ADH, k % 4].rearrange("p (a g) n -> p a g n", g=2)[:, :, g2, 0:n]
                src = self.tr[k % 2][ADH * g2:ADH * g2 + ADH, 2 * l:2 * l + 2, 0:n]
                ins = engine.activation(dst, src, ACT.Copy) if k % 2 == 0 else engine.tensor_copy(dst, src)
        ins.then_inc(self.copied[k % 2], 1)

    def split(self, act, b, c):
        n = self.n
        act.wait_ge(self.multiplied, GK * b + 8 + 4 * (c + 1) + 4)
        act.wait_ge(self.pre_ready, 2 * b + c + 1)
        act.activation(self.second[:, c, :, 0:n], self.ps_h[c][ADH:P, :, 0:n], ACT.Copy).then_inc(self.second_ready, 1)

    def squash(self, act, b, c):
        n = self.n
        act.wait_ge(self.pre_ready, 2 * b + c + 3)
        act.wait_ge(self.out_mm, 2 * b + c + 1)
        act.activation(self.hid[:, c, :, 0:n - 1], self.pre[:, c, :, 0:n - 1], ACT.Gelu,
                       bias=self.b1[:, c:c + 1]).then_inc(self.hid_ready, 1)

    def store(self, act, b, c):
        n = self.n
        act.wait_ge(self.out_mm, 2 * b + c + 3)
        if c == 0:
            act.activation(self.key_out(b), self.ps_k[:, :, 0:n - 1], ACT.Copy).then_inc(self.out_cp, 1)
        else:
            act.activation(self.value_out(b), self.ps_v[0:n - 1], ACT.Copy).then_inc(self.out_cp, 1)

    def act_after(self, act, b, beat, live, prev):
        if live:
            self.copy(act, b, 2 * beat)
            if beat == 6:
                self.split(act, b, 0)
            if beat == 7:
                self.squash(act, b, 0)
        if prev and beat == 0:
            self.store(act, b - 1, 0)
            self.split(act, b - 1, 1)
        if prev and beat == 1:
            self.squash(act, b - 1, 1)
        if prev and beat == 2:
            self.store(act, b - 1, 1)

    def meet(self, dve, b, c):
        n = self.n
        dve.wait_ge(self.second_ready, 2 * b + c + 1)
        dve.wait_ge(self.hid_ready, 2 * b + c + 1)
        dve.tensor_tensor(self.pre[:, c, :, 0:n - 1], self.ps_h[c][0:ADH, :, 0:n - 1], self.second[:, c, :, 1:n],
                          ALU.add).then_inc(self.pre_ready, 1)

    def dve_after(self, dve, b, beat, live, prev):
        if live:
            self.copy(dve, b, 2 * beat + 1)
            if beat == 6:
                self.meet(dve, b, 0)
        if prev and beat == 0:
            self.meet(dve, b - 1, 1)


GRP = 4
COLS = [P, P, P // 4]
NCOL = sum(COLS)


def top16(dve, vec, values, work, top, index, groups):
    n0 = vec[1]
    steps = (
        lambda k: dve.max(top[k][:, 0:8], values[k]),
        lambda k: dve.max_index(index[k][:, 0:8], top[k][:, 0:8], values[k]),
        lambda k: dve.match_replace(work[k], top[k][:, 0:8], values[k], NEG),
        lambda k: dve.max(top[k][:, 8:16], work[k]),
        lambda k: dve.max_index(index[k][:, 8:16], top[k][:, 8:16], work[k]),
    )
    for s, make in enumerate(steps):
        for k in range(groups):
            if s:
                dve.wait_ge(vec[0], n0 + (s - 1) * groups + k + 1)
            make(k).then_inc(vec[0], 1)
    vec[1] = n0 + len(steps) * groups


HH = 2 * PH
NJ = HH // 4


class Ranker:

    def __init__(self, st, M, idx, gate, in_route):
        self.idx, self.gate, self.in_route = idx, gate, in_route
        self.iota = M.c("iota16")
        self.sc = st.sb("sc", [P, 2, 8, P])
        self.work = st.sb("work", [P, 8, P])
        self.v = st.sb("v", [P, 8, PTOP])
        self.ix = st.sb("ix", [P, 8, PTOP], U32)
        self.ixf = st.sb("ixf", [P, 2, 8, PTOP])
        self.cand = st.sb("cand", [P, 4, PTOP * PTOP])
        self.cwork = st.sb("cwork", [P, 4, PTOP * PTOP])
        self.vals = st.sb("vals", [P, 4, PTOP])
        self.ci = st.sb("ci", [P, 4, PTOP], U32)
        self.half = st.sb("half", [P, 2, 4, PTOP], U32)
        self.halff = st.sb("halff", [P, 2, 4, PTOP])
        self.hot = st.sb("hot", [P, 2, 4, PTOP, PTOP])
        self.part = st.sb("part", [P, 2, 4, PTOP])
        self.gt = st.sb("gt", [P, 2, 4, PTOP])
        self.tot = st.sb("tot", [P, 2, 4])
        self.copied, self.ranked = st.sem("copied"), st.sem("ranked")
        self.shifted, self.expd = st.sem("shifted"), st.sem("expd")
        self.halved, self.placed = st.sem("halved"), st.sem("placed")
        self.vec = [st.sem("vecs"), 0]
        self.pooled = Chain(None, st.sem("pooled"))

    def step(self, dve, ins):
        self.vec[1] += 1
        ins.then_inc(self.vec[0], 1)
        dve.wait_ge(self.vec[0], self.vec[1])

    def rank(self, dve, j):
        self.rank_halves(dve, j)
        self.rank_sums(dve, j)

    def rank_halves(self, dve, j):
        n = 4 if j < NJ else 2
        vec, v, ix = self.vec, self.v, self.ix
        dve.wait_ge(self.copied, 2 * j + 2 if j < NJ else 2 * NJ + 1)
        top16(dve, vec, [self.sc[:, j % 2, k, :] for k in range(2 * n)], [self.work[:, k, :] for k in range(2 * n)],
              [v[:, k, :] for k in range(2 * n)], [ix[:, k, :] for k in range(2 * n)], 2 * n)
        dve.wait_ge(vec[0], vec[1])
        if j >= 2:
            dve.wait_ge(self.placed, j - 1)
        self.step(dve, dve.tensor_copy(self.ixf[:, j % 2, 0:2 * n], ix[:, 0:2 * n]))
        dve.nop().then_inc(self.ranked, 1)

    def rank_sums(self, dve, j):
        n = 4 if j < NJ else 2
        vec, cand = self.vec, self.cand

        def step(ins):
            self.step(dve, ins)

        vv = self.v[:, 0:2 * n].rearrange("p (h s) k -> p h s k", s=2)
        full = [P, n, PTOP, PTOP]
        step(dve.tensor_tensor(cand[:, 0:n].rearrange("p h (a b) -> p h a b", a=PTOP),
                               vv[:, :, 0, :, None].to_broadcast(full),
                               vv[:, :, 1, None, :].to_broadcast(full), ALU.add))
        top16(dve, vec, [cand[:, k, :] for k in range(n)], [self.cwork[:, k, :] for k in range(n)],
              [self.vals[:, k, :] for k in range(n)], [self.ci[:, k, :] for k in range(n)], n)
        dve.wait_ge(vec[0], vec[1])
        dve.tensor_tensor(self.gt[:, j % 2, 0:n], self.vals[:, 0:n], self.vals[:, 0:n, 0:1].to_broadcast([P, n, PTOP]),
                          ALU.subtract).then_inc(self.shifted, 1)
        step(dve.tensor_scalar(self.half[:, 0, 0:n], self.ci[:, 0:n], 4, None, ALU.logical_shift_right))
        step(dve.tensor_scalar(self.half[:, 1, 0:n], self.ci[:, 0:n], PTOP - 1, None, ALU.bitwise_and))
        step(dve.tensor_copy(self.halff[:, :, 0:n], self.half[:, :, 0:n]))
        if j:
            dve.wait_ge(self.placed, j)
        for s in range(2):
            dve.tensor_tensor(self.hot[:, s, 0:n], self.halff[:, s, 0:n, :, None].to_broadcast(full),
                              self.iota[:, None, None, :].to_broadcast(full), ALU.is_equal).then_inc(self.halved, 1)
        dve.wait_ge(self.halved, 2 * j + 2)

    def softmax(self, act, j):
        act.wait_ge(self.shifted, j + 1)
        n = 4 if j < NJ else 2
        act.activation(self.gt[:, j % 2, 0:n], self.gt[:, j % 2, 0:n], ACT.Exp).then_inc(self.expd, 1)

    def gates(self, dve, j):
        n = 4 if j < NJ else 2
        e = self.gt[:, j % 2, 0:n]
        dve.wait_ge(self.expd, j + 1)
        self.step(dve, dve.tensor_reduce(self.tot[:, 0, 0:n], e, AX.X, ALU.add))
        self.step(dve, dve.reciprocal(self.tot[:, 1, 0:n], self.tot[:, 0, 0:n]))
        share = self.tot[:, 1, 0:n, None].to_broadcast([P, n, PTOP])
        for t in range(n // 2):
            c0 = t * P + 2 * PTOP * j if j < NJ else SEQ
            self.step(dve, dve.tensor_tensor(self.gate[:, c0:c0 + 2 * PTOP].rearrange("p (h k) -> p h k", h=2),
                                             e[:, 2 * t:2 * t + 2], share[:, 2 * t:2 * t + 2], ALU.mult))

    def place(self, pool, j):
        self.pooled.engine = pool
        step, hot, part = self.pooled, self.hot, self.part
        n = 4 if j < NJ else 2
        iv = self.ixf[:, j % 2, 0:2 * n].rearrange("p (h s) k -> p h s k", s=2)
        pool.wait_ge(self.halved, 2 * j + 2)
        for s in range(2):
            step(pool.tensor_tensor(hot[:, s, 0:n], hot[:, s, 0:n],
                                    iv[:, :, s, None, :].to_broadcast([P, n, PTOP, PTOP]), ALU.mult))
            for k in (8, 4, 2):
                step(pool.tensor_tensor(hot[:, s, 0:n, :, 0:k], hot[:, s, 0:n, :, 0:k], hot[:, s, 0:n, :, k:2 * k],
                                        ALU.add))
            step(pool.tensor_tensor(part[:, s, 0:n], hot[:, s, 0:n, :, 0], hot[:, s, 0:n, :, 1], ALU.add))
        step(pool.tensor_scalar(part[:, 0, 0:n], part[:, 0, 0:n], float(PK), None, ALU.mult))
        step(pool.tensor_tensor(part[:, 0, 0:n], part[:, 0, 0:n], part[:, 1, 0:n], ALU.add))
        for t in range(n // 2):
            c0 = t * P + 2 * PTOP * j if j < NJ else SEQ
            step(pool.tensor_copy(self.idx[:, c0:c0 + 2 * PTOP].rearrange("p (h k) -> p h k", h=2),
                                  part[:, 0, 2 * t:2 * t + 2]))
        pool.nop().then_inc(self.placed, 1)


def route_stage(nc, name, M, I, layer, h, ranker):
    w_view = I["peer_w_q"][layer].rearrange("(c p) n -> p c n", p=P)
    with Stage(nc, name) as st:
        w = st.sb("w", [P, NJ, DC, WB])
        keys = st.sb("keys", [P, HH, P])
        w_in = [st.sem(f"w_in{i}") for i in range(NJ)]
        gain_b = st.sb("gain", [P, D])
        keys_in, gain_in = st.sem("keys_in"), st.sem("gain_in")
        with nc.Block() as block:

            @block.sync
            def _(sp):
                sp.dma_start(gain_b[:], I["norm_ffn"][layer].partition_broadcast(P)).then_inc(gain_in, 16)
                for j in range(NJ):
                    if j == 0:
                        sp.dma_start(keys[:], I["peer_sub_keys"][layer].rearrange("h s k d -> k (h s) d")
                                     ).then_inc(keys_in, 16)
                    sp.dma_start(w[:, j], w_view[:, :, j * WB:(j + 1) * WB]).then_inc(w_in[j], 16)

        keys_T = st.sb("keys_T", [P, HH, P])
        ps_k = [st.ps(f"ps_k{i}", [P, 4, P]) for i in range(2)]
        keys_turned, keys_copied = st.sem("keys_turned"), st.sem("keys_copied")

        def turn_keys(pe):
            pe.wait_ge(keys_in, 16)
            for k in range(NJ):
                if k >= 2:
                    pe.wait_ge(keys_copied, k - 1)
                for c in range(4):
                    mm = pe.transpose(ps_k[k % 2][:, c, :], keys[:, 4 * k + c, :], M.ident)
                mm.then_inc(keys_turned, 1)

        def copy_keys(act):
            for k in range(NJ):
                act.wait_ge(keys_turned, k + 1)
                act.activation(keys_T[:, 4 * k:4 * k + 4, :], ps_k[k % 2][:], ACT.Copy).then_inc(keys_copied, 1)

        norm_stage(nc, name + "n", M, gain_b, gain_in, keep=h, pe_first=turn_keys, act_first=copy_keys)

        q_T = st.sb("q_T", [P, HH, NTOK])
        sc, copied, ranked, expd = ranker.sc, ranker.copied, ranker.ranked, ranker.expd
        acc = [st.ps(f"acc{i}", [P, 512]) for i in range(4)]
        ps_s = [st.ps(f"ps_s{i}", [P, 4, P]) for i in range(2)]
        summed, stored = st.sem("summed"), st.sem("stored")
        scored, packed = st.sem("scored"), st.sem("packed")
        with nc.Block() as block:

            @block.tensor
            def _(pe):
                def project(q):
                    j, c = q // 4, q % 4
                    pe.wait_ge(w_in[j], 16)
                    if q >= 4:
                        pe.wait_ge(stored, q - 3)
                    for k in range(DC):
                        mm = pe.matmul(acc[q % 4][:, 0:NTOK], w[:, j, k, c * P:(c + 1) * P], M.h_T[:, k, :],
                                       start=(k == 0), stop=(k == DC - 1))
                    mm.then_inc(summed, 1)

                def scores(j):
                    pe.wait_ge(stored, 4 * j + 4)
                    pe.wait_ge(keys_copied, NJ)
                    if j:
                        pe.wait_ge(copied, 2 * j)
                    for t in range(2):
                        for c in range(4):
                            mm = pe.matmul(ps_s[t][:, c, :], q_T[:, 4 * j + c, t * P:(t + 1) * P],
                                           keys_T[:, 4 * j + c, :], start=True, stop=True)
                        mm.then_inc(scored, 1)

                for q in range(4):
                    project(q)
                for j in range(1, NJ):
                    if j > 1:
                        project(4 * j)
                    scores(j - 1)
                    for c in range(1 if j > 1 else 0, 4):
                        project(4 * j + c)
                scores(NJ - 1)
                for j in range(NJ):
                    for c in range(4):
                        mm = pe.matmul(ps_k[0][NDEC * j:NDEC * j + NDEC, c, :], q_T[:, 4 * j + c, SEQ:NTOK],
                                       keys_T[:, 4 * j + c, :], start=True, stop=True)
                mm.then_inc(scored, 1)

            @block.scalar
            def _(act):
                def store(q):
                    act.wait_ge(summed, q + 1)
                    act.activation(q_T[:, q, :], acc[q % 4][:, 0:NTOK], ACT.Copy).then_inc(stored, 1)

                def copy_scores(j):
                    if j >= 2:
                        act.wait_ge(ranked, j - 1)
                    for t in range(2 if j < NJ else 1):
                        act.wait_ge(scored, 2 * j + t + 1)
                        src = ps_s[t] if j < NJ else ps_k[0]
                        act.activation(sc[:, j % 2, 4 * t:4 * t + 4, :], src[:], ACT.Copy).then_inc(copied, 1)

                for q in range(4):
                    store(q)
                for j in range(1, NJ):
                    if j > 1:
                        store(4 * j)
                    copy_scores(j - 1)
                    for c in range(1 if j > 1 else 0, 4):
                        store(4 * j + c)
                    ranker.softmax(act, j - 1)
                copy_scores(NJ - 1)
                copy_scores(NJ)
                for j in range(1, 4):
                    ins = act.activation(h[NDEC * j:NDEC * j + NDEC, 2, :], h[0:NDEC, 2, :], ACT.Copy)
                ins.then_inc(packed, 1)
                for j in range(NJ - 1, ranker.in_route):
                    ranker.softmax(act, j)

            @block.gpsimd
            def _(pool):
                for j in range(ranker.in_route):
                    ranker.place(pool, j)

            @block.vector
            def _(dve):
                for j in range(ranker.in_route):
                    ranker.rank(dve, j)
                    if j:
                        ranker.gates(dve, j - 1)
                ranker.gates(dve, ranker.in_route - 1)


def peer_stage(nc, name, M, I, layer, side=None):
    with Stage(nc, name) as outer:
        h = outer.sb("h", [P, NT, D])
        idx = outer.sb("idx", [P, NCOL], U32)
        gate = outer.sb("gate", [P, NCOL])
        cleared = outer.sem("cleared")
        with nc.Block() as block:

            @block.gpsimd
            def _(pool):
                pool.memset(h[:, NT - 1, :], 0.0).then_inc(cleared, 1)
                pool.wait_ge(cleared, 1)

        with Stage(nc, name + "k") as rank_stage:
            late = side is None
            ranker = Ranker(rank_stage, M, idx, gate, NJ - 1 if late else NJ + 1)
            route_stage(nc, name + "r", M, I, layer, h, ranker)
            if late:
                gather_stage(nc, name + "g", M, I, layer, h, idx, gate, side, ranker)
        if not late:
            gather_stage(nc, name + "g", M, I, layer, h, idx, gate, side, None)


def gather_stage(nc, name, M, I, layer, h, idx, gate, side, ranker):
    u_table = I["peer_u"].rearrange("l e d -> (l e) d")
    v_table = I["peer_v"].rearrange("l e d -> (l e) d")
    off = layer * PK * PK * D
    BLOCKS = [COLS[t] // (BEATS * GRP) for t in range(NT)]
    with Stage(nc, name) as st:
        u = st.sb("u", [P, 2 * GRP, D])
        vrow = st.sb("vrow", [P, 2 * GRP, D])
        cur_u = st.sb("cur_u", [P, 2, GRP], U32)
        cur_v = st.sb("cur_v", [P, 2, GRP], U32)
        cur_row = st.sb("cur_row", [P, 2], U32)
        dot = st.sb("dot", [P, 2, GRP])
        gelu = st.sb("gelu", [P, 2, GRP])
        w = st.sb("w", [P, 2, GRP])
        diag = st.sb("diag", [P, 2 * GRP, P])
        zero = st.sb("zero", [P, P])
        acc = st.ps("acc", [P, 2, 512])
        cur_u_ready, cur_v_ready = st.sem("cur_u_ready"), st.sem("cur_v_ready")
        cur_row_ready = [st.sem(f"cur_row_ready{i}") for i in range(2)]
        u_in = [st.sem(f"u_in{i}") for i in range(2)]
        v_in = [st.sem(f"v_in{i}") for i in range(2)]
        zeroed, dotted, gelu_ready, w_ready = (st.sem(n) for n in ("zeroed", "dotted", "gelu_ready", "w_ready"))
        diag_ready, applied, closed, added = (st.sem(n) for n in ("diag_ready", "applied", "closed", "added"))
        comp = None
        if side is not None:
            half_idx, cmp_kT, cmp_v = side
            cache = I["cache_cmp_kv"][0].rearrange("a (n l) c g d -> (a n) (l c g d)", l=HALF_L)
            comp = Compressor(nc, st, KEY_ROWS,
                              lambda b: cmp_kT[:, bass.ds(b, 1), :, 0:N_CMP].rearrange("p o a k -> p (o a) k"),
                              lambda b: cmp_v[0:N_CMP, bass.ds(b, 1), :].rearrange("p o a -> p (o a)"))
            comp.ident = M.ident

        def blocks(engine, block_of, start=None, end=None):
            for t in range(NT):
                if start is not None:
                    start(t)
                if t == 0:
                    block_of(0, t, True, False)
                if t < NT - 1:
                    with engine.Fori(max(1, 4 * t), 4 * t + 4) as b:
                        block_of(b, t, True, True)
                else:
                    block_of(2 * BLOCKS[0], t, False, True)
                if end is not None:
                    end(t)

        def is_first(b):
            return isinstance(b, int) and b == 0

        with nc.Block() as block:

            if comp is not None:

                @block.sync
                def _(sp):
                    comp.load_weights(sp, I)

            @block.gpsimd
            def _(pool):
                def load_half(e, column, at):
                    pool.wait_ge(dotted, 1)
                    pool.wait_ge(comp.turned, at)
                    pool.tensor_copy(cur_row[:, e:e + 1], half_idx[:, e, bass.ds(column, 1)]
                                     ).then_inc(cur_row_ready[e], GK)
                    pool.wait_ge(dotted, 1)
                    pool.wait_ge(cur_row_ready[e], at)
                    pool.indirect_dma_start(comp.rows[:, e, :], None, cache,
                                            bass.IndirectOffsetOnAxis(ap=cur_row[:, e:e + 1], axis=0)
                                            ).then_inc(comp.rows_in[e], 16)

                def block_of(b, t, live, prev):
                    for beat in range(BEATS):
                        s = beat % 2
                        for cur, ready, free, table, ring, landed in (
                                (cur_u, cur_u_ready, dotted, u_table, u, u_in),
                                (cur_v, cur_v_ready, applied, v_table, vrow, v_in)):
                            pool.wait_ge(dotted, 1)
                            pool.wait_ge(free, BEATS * b + beat + 1)
                            pool.tensor_copy(cur[:, s, :], idx[:, bass.ds((BEATS * b + beat) * GRP, GRP)]
                                             ).then_inc(ready, 1)
                            pool.wait_ge(dotted, 1)
                            pool.wait_ge(ready, BEATS * b + beat + 1)
                            for k in range(GRP):
                                pool.indirect_dma_start(ring[:, s * GRP + k, :], None, table,
                                                        bass.IndirectOffsetOnAxis(ap=cur[:, s, k:k + 1], axis=0),
                                                        element_offset=off).then_inc(landed[s], 16)
                        if ranker is not None and is_first(b) and beat in (5, 7):
                            ranker.place(pool, NJ - 1 if beat == 5 else NJ)
                        if comp is not None and live and beat == 1:
                            load_half(1, b, GK * b + 1)
                        if comp is not None and live and beat == 5:
                            load_half(0, b + 1, GK * b + GK // 2)

                if comp is not None:
                    pool.indirect_dma_start(comp.rows[:, 0, :], None, cache,
                                            bass.IndirectOffsetOnAxis(ap=half_idx[:, 0, 0:1], axis=0)
                                            ).then_inc(comp.rows_in[0], 16)
                blocks(pool, block_of)
                if comp is not None:
                    pool.wait_ge(comp.rows_in[0], 16 * (DEC_B + 1))

            @block.vector
            def _(dve):
                dve.memset(zero[:], 0.0).then_inc(zeroed, 1)
                dve.nop().then_inc(dotted, 2)
                if comp is not None:
                    comp.start_dve(dve)

                def block_of(b, t, live, prev):
                    for beat in range(BEATS):
                        s = beat % 2
                        dve.wait_ge(u_in[s], (BEATS // 2 * b + beat // 2 + 1) * (16 * GRP))
                        for k in range(GRP):
                            row = u[:, s * GRP + k, :]
                            ins = dve.tensor_tensor_reduce(row, row, h[:, t, :], 1.0, 0.0, ALU.mult, ALU.add,
                                                           dot[:, s, k:k + 1])
                        ins.then_inc(dotted, 1)
                        dve.wait_ge(gelu_ready, BEATS * b + beat + 1)
                        dve.tensor_tensor(w[:, s, :], gelu[:, s, :], gate[:, bass.ds((BEATS * b + beat) * GRP, GRP)],
                                          ALU.mult).then_inc(w_ready, 1)
                        if ranker is not None and is_first(b):
                            if beat == 1:
                                ranker.rank_halves(dve, NJ - 1)
                            if beat == 3:
                                ranker.rank_sums(dve, NJ - 1)
                            if beat == 4:
                                ranker.gates(dve, NJ - 1)
                                ranker.rank_halves(dve, NJ)
                            if beat == 6:
                                ranker.rank_sums(dve, NJ)
                            if beat == 7:
                                ranker.gates(dve, NJ)
                        if comp is not None:
                            comp.dve_after(dve, b, beat, live, prev)

                def end(t):
                    n = TILES[t][1]
                    dve.wait_ge(closed, t + 1)
                    dve.tensor_tensor(M.x[0:n, t, :].rearrange("p (a b) -> p a b", a=2), acc[0:n],
                                      M.x[0:n, t, :].rearrange("p (a b) -> p a b", a=2), ALU.add).then_inc(added, 1)

                blocks(dve, block_of, end=end)

            @block.scalar
            def _(act):
                if comp is not None:
                    comp.start_act(act)

                def block_of(b, t, live, prev):
                    base = M.ident if t < 2 else M.c("stack32")
                    n = TILES[t][1]
                    for beat in range(BEATS):
                        s = beat % 2
                        act.wait_ge(dotted, BEATS * b + beat + 3)
                        act.activation(gelu[:, s, :], dot[:, s, :], ACT.Gelu).then_inc(gelu_ready, 1)
                        act.wait_ge(w_ready, BEATS * b + beat + 1)
                        act.wait_ge(applied, BEATS * b + beat + 1)
                        for k in range(GRP):
                            ins = act.activation(diag[:, s * GRP + k, 0:n], base, ACT.Copy, scale=w[:, s, k:k + 1])
                        ins.then_inc(diag_ready, 1)
                        if ranker is not None and is_first(b) and beat in (3, 6):
                            ranker.softmax(act, NJ - 1 if beat == 3 else NJ)
                        if comp is not None:
                            comp.act_after(act, b, beat, live, prev)

                blocks(act, block_of)

            @block.tensor
            def _(pe):
                pe.wait_ge(zeroed, 1)
                if comp is not None:
                    pe.wait_ge(comp.weights_in, 16 * comp.LOADS)

                def start(t):
                    if t:
                        pe.wait_ge(added, t)
                    for a in range(2):
                        mm = pe.matmul(acc[0:TILES[t][1], a, :], zero[:, 0:TILES[t][1]], h[:, 0, 0:512],
                                       start=True, stop=False, skip_group_check=True)
                        if t == 0:
                            mm.then_inc(applied, 1)

                def block_of(b, t, live, prev):
                    n = TILES[t][1]
                    for beat in range(BEATS):
                        s = beat % 2
                        if comp is not None:
                            comp.pe_before(pe, b, beat, live, prev)
                        pe.wait_ge(diag_ready, BEATS * b + beat + 1)
                        pe.wait_ge(v_in[s], (BEATS // 2 * b + beat // 2 + 1) * (16 * GRP))
                        for k in range(GRP):
                            for a in range(2):
                                mm = pe.matmul(acc[0:n, a, :], diag[:, s * GRP + k, 0:n],
                                               vrow[:, s * GRP + k, a * 512:a * 512 + 512],
                                               start=False, stop=False, skip_group_check=True)
                        mm.then_inc(applied, 1)
                        if comp is not None:
                            comp.pe_after(pe, b, beat, live, prev)

                def end(t):
                    n = TILES[t][1]
                    for a in range(2):
                        mm = pe.matmul(acc[0:n, a, :], zero[:, 0:n], h[:, 0, 0:512], start=False, stop=True,
                                       skip_group_check=True)
                    mm.then_inc(closed, 1)

                blocks(pe, block_of, start=start, end=end)


def nsa_stage(nc, M, I, O, quarter_idx, cmp_kT, cmp_v):
    o_dec = nc.dram_tensor("o_dec_scratch", [3, NDEC, D], F32, kind="Internal").ap()
    with Stage(nc, "na") as outer:
        q = outer.sb("q", [P, NT, D])
        kv = outer.sb("kv", [P, NT, 3, 2, GD])
        gate = outer.sb("gate", [P, NT, AH, 3])
        q_T = outer.sb("q_T", [P, 2, AR, NTOK])
        k_T = outer.sb("k_T", [P, 2, 2, NTOK])
        pcmp_kT = outer.sb("pcmp_kT", [P, 2, KEY_ROWS])
        pcmp_v = outer.sb("pcmp_v", [P, GD])
        by_head = q[:].rearrange("p t (a r g d) -> p t a g r d", a=2, r=AR, g=2)
        jobs = [(a * WB, WB, "N", (lambda a: lambda t: (by_head[0:TILES[t][1], t, a], ACT.Copy, 1.0))(a))
                for a in range(2)]
        for br in range(3):
            jobs.append((AQW + br * 2 * GD, WB, "N", (lambda br: lambda t: (
                kv[0:TILES[t][1], t, br].rearrange("p c g -> p (c g)"), ACT.Copy, 1.0))(br)))
        jobs.append((AQW + AKVW, 3 * AH, "N", lambda t: (
            gate[0:TILES[t][1], t].rearrange("p h b -> p (h b)"), ACT.Copy, 1.0)))
        project_stage(nc, "np", M, I["nsa_w_in"][0], jobs, gain=I["norm_mix"][1])
        rotate_stage(nc, M, I, O, q, kv, gate, q_T, k_T)
        compress_stage(nc, M, I, O, pcmp_kT, pcmp_v)
        prompt_stage(nc, M, q, kv, gate, q_T, k_T, pcmp_kT, pcmp_v)
        with Stage(nc, "nd") as st:
            q_blk = st.sb("q_blk", [P, DEC_B, 2, 2 * AR * DEC_S])
            block_mask = st.sb("block_mask", [P, 4, PAST // SBLK])
            group_one = M.c("group_one")
            with Stage(nc, "dr") as ring_stage:
                cached = I["cache_sel_kv"][0].rearrange("a (n l) c g d -> (a n) (l c g d)", l=CSTR // 4)
                ring = Ring(nc, ring_stage, CSTR // 4, 4, 12, lambda pool, dst, b, e: pool.indirect_dma_start(
                    dst, None, cached, bass.IndirectOffsetOnAxis(ap=quarter_idx[:, e, b:b + 1], axis=0)))
                blocks_stage(nc, M, q_T, q_blk, cmp_kT, cmp_v, block_mask, o_dec[0], ring)
                decode_stage(nc, M, "ds", q_T, cmp_kT, q_blk, k_T[:, 0], kv[0:NDEC, NT - 1, 1, 1], CSTR, o_dec[1], block_mask, ring)
            with Stage(nc, "dv") as ring_stage:
                window = I["state_win_kv"][0]
                ring = Ring(nc, ring_stage, WIN // P, 1, DEC_B, lambda sp, dst, b, e: sp.dma_start(
                    dst, window[b].rearrange("(n l) c g d -> n (l c g d)", l=WIN // P)))
                with nc.Block() as block:

                    @block.sync
                    def _(sp):
                        for i in range(ring.slots):
                            ring.load(sp, i)

                decode_stage(nc, M, "dw", q_T, cmp_kT, q_blk, k_T[:, 1], kv[0:NDEC, NT - 1, 2, 1], WIN // P, o_dec[2], None, ring)
        mix_stage(nc, M, q, gate, o_dec)
        project_stage(nc, "no", M, I["nsa_w_out"][0], add_jobs(), turn=q)


def rotate_stage(nc, M, I, O, q, kv, gate, q_T, k_T):
    with Stage(nc, "rt") as st:
        b_gate = st.sb("b_gate", [P, AH, 3])
        tmp = st.sb("tmp", [P, 4, 4, AH, ROT // 2])
        tr = [st.ps(f"tr{i}", [P, 4, P]) for i in range(4)]
        loaded, vec = st.sem("loaded"), st.sem("vec")
        biased, gated, rotated = st.sem("biased"), st.sem("gated"), st.sem("rotated")
        turned, copied, out_done = st.sem("turned"), st.sem("copied"), st.sem("out_done")
        half = ROT // 2
        cos, sin = M.c("cos"), M.c("sin")
        qh = q[:].rearrange("p t (h d) -> p t h d", h=AH)
        kvh = kv[:].rearrange("p t b c (g d) -> p t b c g d", g=AG)
        with nc.Block() as block:

            @block.scalar
            def _(act):
                act.dma_start(b_gate[:], I["nsa_b_gate"][0].partition_broadcast(P)).then_inc(loaded, 16)
                for t, (_, n) in enumerate(TILES):
                    act.wait_ge(biased, t + 1)
                    act.activation(gate[0:n, t], gate[0:n, t], ACT.Sigmoid).then_inc(gated, 1)
                for t, (t0, n) in enumerate(TILES):
                    for k in range(3):
                        act.wait_ge(turned, 3 * t + k + 1)
                        dst = q_T[:, k, :, t0:t0 + n] if k < 2 else (
                            k_T[:, :, :, t0:t0 + n].rearrange("p b a t -> p (b a) t"))
                        act.activation(dst, tr[(3 * t + k) % 4][:, :, 0:n], ACT.Copy,
                                       scale=ADH ** -0.5 if k < 2 else 1.0).then_inc(copied, 1)

            @block.vector
            def _(dve):
                step = Chain(dve, vec)
                dve.wait_ge(loaded, 16)
                for t, (_, n) in enumerate(TILES):
                    dve.tensor_tensor(gate[0:n, t], gate[0:n, t], b_gate[0:n], ALU.add).then_inc(biased, 1)
                for t, (_, n) in enumerate(TILES):
                    places = [qh[0:n, t]] + [kvh[0:n, t, br, 0] for br in range(3)]
                    n0 = step.n
                    for i, x in enumerate(places):
                        heads = x.shape[1]
                        full = [n, heads, half]
                        c = cos[0:n, t, None, :].to_broadcast(full)
                        s = sin[0:n, t, None, :].to_broadcast(full)
                        x1, x2 = x[:, :, 0:half], x[:, :, half:ROT]
                        for k, (a, b) in enumerate(((x1, c), (x2, s), (x2, c), (x1, s))):
                            dve.tensor_tensor(tmp[0:n, i, k, 0:heads], a, b, ALU.mult).then_inc(vec, 1)
                    step.n += 4 * len(places)
                    for i, x in enumerate(places):
                        heads = x.shape[1]
                        dve.wait_ge(vec, n0 + 4 * i + 4)
                        dve.tensor_tensor(x[:, :, 0:half], tmp[0:n, i, 0, 0:heads], tmp[0:n, i, 1, 0:heads],
                                          ALU.subtract).then_inc(vec, 1)
                        dve.tensor_tensor(x[:, :, half:ROT], tmp[0:n, i, 2, 0:heads], tmp[0:n, i, 3, 0:heads],
                                          ALU.add).then_inc(vec, 1)
                    step.n += 2 * len(places)
                    dve.wait_ge(vec, step.n)
                    dve.nop().then_inc(rotated, 1)

            @block.tensor
            def _(pe):
                for t, (t0, n) in enumerate(TILES):
                    pe.wait_ge(rotated, t + 1)
                    for k in range(3):
                        e = 3 * t + k
                        if e >= 4:
                            pe.wait_ge(copied, e - 3)
                        for r in range(4):
                            if k < 2:
                                src = q[0:n, t, (k * AR + r) * P:(k * AR + r + 1) * P]
                            else:
                                src = kv[0:n, t, 1 + r // 2, 0, (r % 2) * P:(r % 2) * P + P]
                            mm = pe.transpose(tr[e % 4][:, r, 0:n], src, M.ident[0:n, 0:n])
                        mm.then_inc(turned, 1)

            @block.sync
            def _(sp):
                def flat(ap):
                    return ap.rearrange("s c g d -> s (c g d)")

                def rows(t, n, br):
                    return kv[0:n, t, br].rearrange("p c g -> p (c g)")

                for t in range(2):
                    sp.wait_ge(rotated, t + 1)
                    for br, name in enumerate(("cmp_p", "sel_p", "win_p")):
                        sp.dma_start(flat(O[name][0, 0, t * P:(t + 1) * P]), rows(t, P, br)).then_inc(out_done, 16)
                sp.wait_ge(rotated, 3)
                for br, name in enumerate(("cmp_s", "sel_s")):
                    sp.dma_start(O[name][0].rearrange("b s c g d -> (b s) (c g d)"), rows(2, NDEC, br)).then_inc(out_done, 16)
                for b in range(DEC_B):
                    sp.dma_start(flat(O["win_s"][0, b, WIN - DEC_S:WIN]),
                                 kv[DEC_S * b:DEC_S * b + DEC_S, 2, 2].rearrange("p c g -> p (c g)")).then_inc(out_done, 16)
                sp.wait_ge(out_done, 16 * 16)


def compress_stage(nc, M, I, O, pcmp_kT, pcmp_v):
    n = NPC + 1
    with Stage(nc, "cp") as st:
        comp = Compressor(nc, st, n, lambda b: pcmp_kT[:, :, 0:n - 1], lambda b: pcmp_v[0:n - 1])
        comp.ident = M.ident
        with nc.Block() as block:

            @block.sync
            def _(sp):
                comp.load_weights(sp, I)
                rows = O["cmp_p"][0, 0].rearrange("(n e l) c g d -> n e (l c g d)", e=2, l=HALF_L)
                for e in range(2):
                    sp.dma_start(comp.rows[0:n, e, :], rows[:, e]).then_inc(comp.rows_in[e], 16)

            @block.tensor
            def _(pe):
                pe.wait_ge(comp.weights_in, 16 * comp.LOADS)
                for b, beat in [(0, beat) for beat in range(BEATS)] + [(1, beat) for beat in range(3)]:
                    comp.pe_before(pe, b, beat, b == 0, b == 1)
                    comp.pe_after(pe, b, beat, b == 0, b == 1)

            @block.scalar
            def _(act):
                comp.start_act(act)
                for b, beat in [(0, beat) for beat in range(BEATS)] + [(1, beat) for beat in range(3)]:
                    comp.act_after(act, b, beat, b == 0, b == 1)

            @block.vector
            def _(dve):
                comp.start_dve(dve)
                for b, beat in [(0, beat) for beat in range(BEATS)] + [(1, beat) for beat in range(3)]:
                    comp.dve_after(dve, b, beat, b == 0, b == 1)


def prompt_stage(nc, M, q, kv, gate, q_T, k_T, pcmp_kT, pcmp_v):
    units = [(br, t, g) for t in range(2) for br in (1, 2) for g in range(AG)]
    with Stage(nc, "pa") as st:
        nmax = st.sb("nmax", [P, 2, AR])
        total = st.sb("total", [P, 4, AR])
        share = st.sb("share", [P, 2, 2, AR])
        e = st.sb("e", [P, 2, AR, 2 * P])
        e_T = st.sb("e_T", [P, 2, 2, AR, P])
        cs = st.sb("cs", [P, AH, NPC])
        csum = st.sb("csum", [P, 3, AH])
        ce_T = st.sb("ce_T", [NPC, AH, P])
        part = st.sb("part", [P, 2, AR, ADH])
        ps_s = [st.ps(f"ps_s{i}", [P, AR, 2 * P]) for i in range(2)]
        ps_t = st.ps("ps_t", [P, 2, AR, P])
        ps_o = [st.ps(f"ps_o{i}", [P, 8, ADH]) for i in range(2)]
        vec = st.sem("vec")
        c_scored, c_ready, c_turned, c_copied, c_summed, c_exp = (st.sem(n) for n in (
            "c_scored", "c_ready", "c_turned", "c_copied", "c_summed", "c_exp"))
        c_gone = st.sem("c_gone")
        scored, maxed, expd, turned, copied, summed, stored = (st.sem(n) for n in (
            "scored", "maxed", "expd", "turned", "copied", "summed", "stored"))
        causal = M.c("causal")
        with nc.Block() as block:

            @block.tensor
            def _(pe):
                for t in range(2):
                    if t:
                        pe.wait_ge(c_ready, t)
                    for h in range(AH):
                        a, g2, r = h // 8, (h // 4) % 2, h % 4
                        d0 = ADH * g2
                        mm = pe.matmul(ps_s[g2][:, a, r * NPC:(r + 1) * NPC], q_T[d0:d0 + ADH, a, r, t * P:(t + 1) * P],
                                       pcmp_kT[d0:d0 + ADH, a, 0:NPC], start=True, stop=True)
                    mm.then_inc(c_scored, 1)
                    pe.wait_ge(c_exp, t + 1)
                    for k in range(2):
                        if k or t:
                            pe.wait_ge(c_copied, 2 * t + k)
                        for h in range(8):
                            mm = pe.transpose(ps_t[0:NPC, h // 4, h % 4, :], cs[:, 8 * k + h, :], M.ident)
                        mm.then_inc(c_turned, 1)
                    pe.wait_ge(c_copied, 2 * t + 2)
                    if t:
                        pe.wait_ge(c_gone, t)
                    for h in range(AH):
                        mm = pe.matmul(ps_o[h // 8][:, h % 8, :], ce_T[:, h, :],
                                       pcmp_v[0:NPC, (h // 4) * ADH:(h // 4 + 1) * ADH], start=True, stop=True)
                    mm.then_inc(c_summed, 1)
                pe.wait_ge(c_gone, 2)

                def scores(u):
                    br, t, g = units[u]
                    d0, nk = ADH * (g % 2), P * (t + 1)
                    if u >= 2:
                        pe.wait_ge(expd, u - 1)
                    for r in range(AR):
                        pe.matmul(ps_s[u % 2][:, r, 0:nk], q_T[d0:d0 + ADH, g // 2, r, t * P:(t + 1) * P],
                                  k_T[d0:d0 + ADH, br - 1, g // 2, 0:nk], start=True, stop=False)
                        mm = pe.matmul(ps_s[u % 2][:, r, nk - P:nk], M.ident, causal, start=False, stop=True)
                    mm.then_inc(scored, 1)

                def turn(u):
                    br, t, g = units[u]
                    pe.wait_ge(expd, u + 1)
                    for kt in range(t + 1):
                        for r in range(AR):
                            mm = pe.transpose(ps_t[:, kt, r, :], e[:, u % 2, r, kt * P:(kt + 1) * P], M.ident)
                    mm.then_inc(turned, 1)

                def values(u):
                    br, t, g = units[u]
                    pe.wait_ge(copied, u + 1)
                    if u >= 2:
                        pe.wait_ge(stored, u - 1)
                    for r in range(AR):
                        for kt in range(t + 1):
                            mm = pe.matmul(ps_o[u % 2][:, r, :], e_T[:, u % 2, kt, r, :],
                                           kv[:, kt, br, 1, g * ADH:(g + 1) * ADH], start=(kt == 0), stop=(kt == t))
                    mm.then_inc(summed, 1)

                scores(0)
                for u in range(len(units)):
                    if u + 1 < len(units):
                        scores(u + 1)
                    if u:
                        values(u - 1)
                    turn(u)
                values(len(units) - 1)

            @block.scalar
            def _(act):
                for t in range(2):
                    act.wait_ge(c_ready, t + 1)
                    act.activation(cs[:], cs[:], ACT.Exp).then_inc(c_exp, 1)
                    for k in range(2):
                        act.wait_ge(c_turned, 2 * t + k + 1)
                        act.activation(ce_T[:, 8 * k:8 * k + 8, :], ps_t[0:NPC].rearrange("p a b c -> p (a b) c"),
                                       ACT.Copy).then_inc(c_copied, 1)

                def copy(u):
                    t = units[u][1]
                    act.wait_ge(turned, u + 1)
                    if u >= 2:
                        act.wait_ge(summed, u - 1)
                    act.activation(e_T[:, u % 2, 0:t + 1], ps_t[:, 0:t + 1], ACT.Copy).then_inc(copied, 1)

                for u, (br, t, g) in enumerate(units):
                    nk = P * (t + 1)
                    act.wait_ge(maxed, u + 1)
                    if u >= 2:
                        act.wait_ge(turned, u - 1)
                    if u >= 4:
                        act.wait_ge(stored, u - 3)
                    for r in range(AR):
                        ins = act.activation(e[:, u % 2, r, 0:nk], ps_s[u % 2][:, r, 0:nk], ACT.Exp,
                                             bias=nmax[:, u % 2, r:r + 1], accum_out=total[:, u % 4, r:r + 1])
                    ins.then_inc(expd, 1)
                    if u:
                        copy(u - 1)
                copy(len(units) - 1)

            def finish(dve, step, u):
                br, t, g = units[u]
                s = u % 2
                dve.wait_ge(expd, u + 1)
                step(dve.reciprocal(share[:, s, 0], total[:, u % 4]))
                step(dve.tensor_tensor(share[:, s, 1], share[:, s, 0], gate[:, t, g * AR:(g + 1) * AR, br], ALU.mult))
                dve.wait_ge(summed, u + 1)
                step(dve.tensor_tensor(part[:, s], ps_o[s][:, 0:AR, :],
                                       share[:, s, 1, :, None].to_broadcast([P, AR, ADH]), ALU.mult))
                out = q[:, t, g * AR * ADH:(g + 1) * AR * ADH].rearrange("p (h d) -> p h d", h=AR)
                dve.tensor_tensor(out, out, part[:, s], ALU.add).then_inc(stored, 1)
                dve.wait_ge(stored, u + 1)

            @block.vector
            def _(dve):
                step = Chain(dve, vec)
                for t in range(2):
                    full = [P, AH, NPC]
                    dve.wait_ge(c_scored, t + 1)
                    if t:
                        dve.wait_ge(c_turned, 2 * t)
                    by_group = cs[:].rearrange("p (a g r) k -> p a g r k", a=2, g=2)
                    for a in range(2):
                        for g2 in range(2):
                            step(dve.tensor_tensor(
                                by_group[:, a, g2], ps_s[g2][:, a, 0:AR * NPC].rearrange("p (r k) -> p r k", r=AR),
                                M.c("cmp_mask")[:, t, None, :].to_broadcast([P, AR, NPC]), ALU.add))
                    step(dve.tensor_reduce(csum[:, 0], cs[:], AX.X, ALU.max))
                    dve.tensor_tensor(cs[:], cs[:], csum[:, 0, :, None].to_broadcast(full),
                                      ALU.subtract).then_inc(c_ready, 1)
                    dve.wait_ge(c_exp, t + 1)
                    step(dve.tensor_reduce(csum[:, 1], cs[:], AX.X, ALU.add))
                    step(dve.reciprocal(csum[:, 2], csum[:, 1]))
                    step(dve.scalar_tensor_tensor(out=csum[:, 1], in0=csum[:, 2], scalar=M.c("cmp_any")[:, t:t + 1],
                                                  in1=gate[:, t, :, 0], op0=ALU.mult, op1=ALU.mult))
                    dve.wait_ge(c_summed, t + 1)
                    for k in range(2):
                        step(dve.tensor_tensor(
                            q[:, t, k * 512:k * 512 + 512].rearrange("p (h d) -> p h d", h=8), ps_o[k][:],
                            csum[:, 1, 8 * k:8 * k + 8, None].to_broadcast([P, 8, ADH]), ALU.mult))
                    dve.nop().then_inc(c_gone, 1)
                for u, (br, t, g) in enumerate(units):
                    nk = P * (t + 1)
                    dve.wait_ge(scored, u + 1)
                    if u >= 2:
                        dve.wait_ge(expd, u - 1)
                    dve.tensor_reduce(nmax[:, u % 2], ps_s[u % 2][:, :, 0:nk], AX.X, ALU.max, negate=True
                                      ).then_inc(maxed, 1)
                    if u >= 2:
                        finish(dve, step, u - 2)
                for u in range(len(units) - 2, len(units)):
                    finish(dve, step, u)


def blocks_stage(nc, M, q_T, q_blk, cmp_kT, cmp_v, block_mask, o_out, ring):
    NB = PAST // SBLK
    with Stage(nc, "db") as st:
        p = st.sb("p", [P, 2, KEY_ROWS])
        p_T = st.sb("p_T", [P, 2, P])
        small = st.sb("small", [P, 4, 4])
        imp = st.sb("imp", [P, 4, NB])
        imp_p = st.sb("imp_p", [P, KEY_ROWS])
        score = st.sb("score", [P, 3, NB + 1])
        top = st.sb("top", [P, 2, 8])
        o = st.sb("o", [P, 4, ADH])
        ps_s = [st.ps(f"ps_s{i}", [P, KEY_ROWS]) for i in range(2)]
        ps_i = [st.ps(f"ps_i{i}", [P, KEY_ROWS]) for i in range(2)]
        ps_t = [st.ps(f"ps_t{i}", [P, P]) for i in range(2)]
        ps_o = [st.ps(f"ps_o{i}", [P, AG, ADH]) for i in range(2)]
        names = ("vec", "blk_ready", "scored", "maxed", "expd", "normed", "turned", "copied", "summed", "o_ready",
                 "saved", "cleared")
        vec, blk_ready, scored, maxed, expd, normed, turned, copied, summed, o_ready, saved, cleared = (
            st.sem(n) for n in names)
        with nc.Block() as block:

            @block.gpsimd
            def _(pool):
                pool.memset(q_blk[:], 0.0).then_inc(cleared, 1)
                pool.memset(p[:], 0.0).then_inc(cleared, 1)
                for i in range(ring.slots):
                    ring.load(pool, i)

            @block.tensor
            def _(pe):
                pe.wait_ge(blk_ready, 1)
                for u in range(4):
                    for b2 in range(2):
                        for a in range(2):
                            r0 = 64 * b2 + 32 * a
                            mm = pe.matmul(ps_s[u % 2][r0:r0 + 32, 0:N_CMP], q_blk[:, 2 * u + b2, a, :],
                                           cmp_kT[:, 2 * u + b2, a, 0:N_CMP], start=True, stop=True)
                    mm.then_inc(scored, 1)
                    pe.wait_ge(normed, u + 1)
                    pe.matmul(ps_i[u % 2][:], M.c("sum_heads"), p[:, u % 2, :], start=True, stop=True)
                    pe.transpose(ps_t[u % 2][:], p[:, u % 2, :], M.ident).then_inc(turned, 1)
                    pe.wait_ge(copied, u + 1)
                    if u >= 2:
                        pe.wait_ge(o_ready, u - 1)
                    for b2 in range(2):
                        mm = pe.matmul(ps_o[u % 2][64 * b2:64 * b2 + 64].rearrange("p g d -> p (g d)"),
                                       p_T[0:N_CMP, u % 2, 64 * b2:64 * b2 + 64], cmp_v[0:N_CMP, 2 * u + b2, :],
                                       start=True, stop=True)
                    mm.then_inc(summed, 1)

            @block.scalar
            def _(act):
                for u in range(4):
                    act.wait_ge(maxed, u + 1)
                    act.activation(p[:, u % 2, 0:N_CMP], ps_s[u % 2][:, 0:N_CMP], ACT.Exp, bias=small[:, u, 0:1],
                                   accum_out=small[:, u, 1:2]).then_inc(expd, 1)
                    act.wait_ge(turned, u + 1)
                    act.activation(p_T[:, u % 2, :], ps_t[u % 2][:], ACT.Copy).then_inc(copied, 1)

            @block.vector
            def _(dve):
                step = Chain(dve, vec)
                dve.wait_ge(cleared, 2)
                for a in range(2):
                    for g2 in range(2):
                        for r in range(AR):
                            d0 = ADH * g2
                            c0 = (g2 * AR + r) * DEC_S
                            step(dve.tensor_copy(q_blk[d0:d0 + ADH, :, a, c0:c0 + DEC_S],
                                                 q_T[d0:d0 + ADH, a, r, SEQ:NTOK].rearrange("p (b s) -> p b s", s=DEC_S)))
                dve.nop().then_inc(blk_ready, 1)
                for u in range(4):
                    dve.wait_ge(scored, u + 1)
                    dve.tensor_reduce(small[:, u, 0:1], ps_s[u % 2][:, 0:N_CMP], AX.X, ALU.max, negate=True
                                      ).then_inc(maxed, 1)
                    dve.wait_ge(expd, u + 1)
                    step(dve.reciprocal(small[:, u, 2:3], small[:, u, 1:2]))
                    dve.tensor_scalar(p[:, u % 2, 0:N_CMP], p[:, u % 2, 0:N_CMP], small[:, u, 2:3], None, ALU.mult
                                      ).then_inc(normed, 1)
                    dve.wait_ge(turned, u + 1)
                    step(dve.tensor_copy(imp_p[:], ps_i[u % 2][:]))
                    four = imp_p[:].rearrange("p (j k) -> p j k", k=4)
                    step(dve.tensor_reduce(imp[:, 0], four, AX.X, ALU.add))
                    step(dve.tensor_reduce(imp[:, 1], four[:, :, 0:3], AX.X, ALU.add))
                    step(dve.tensor_tensor(imp[:, 2], imp[:, 0], imp[:, 1], ALU.add))
                    step(dve.memset(score[:, 0], -NEG))
                    step(dve.tensor_tensor(score[:, 0, 1:NB - 1], imp[:, 2, 1:NB - 1], four[:, 0:NB - 2, 3], ALU.add))
                    for k in range(2):
                        step(dve.max(top[:, k], score[:, k]))
                        step(dve.match_replace(score[:, k + 1], top[:, k], score[:, k], -3e38))
                    step(dve.tensor_scalar(block_mask[:, u], score[:, 2, 0:NB], -1e38, NEG, ALU.is_gt, ALU.mult))
                    dve.wait_ge(summed, u + 1)
                    for g in range(AG):
                        if g == 0:
                            step(dve.tensor_scalar(o[:, u], ps_o[u % 2][:, 0, :], M.c("group_one")[:, 0:1], None,
                                                   ALU.mult))
                        else:
                            step(dve.scalar_tensor_tensor(out=o[:, u], in0=ps_o[u % 2][:, g, :],
                                                          scalar=M.c("group_one")[:, g:g + 1], in1=o[:, u],
                                                          op0=ALU.mult, op1=ALU.add))
                    dve.nop().then_inc(o_ready, 1)

            @block.sync
            def _(sp):
                for u in range(4):
                    sp.wait_ge(o_ready, u + 1)
                    for b2 in range(2):
                        b = 2 * u + b2
                        sp.dma_start(o_out[DEC_S * b:DEC_S * (b + 1)].rearrange("s (h d) -> h s d", h=AH),
                                     o[64 * b2:64 * b2 + 64, u, :]).then_inc(saved, 16)
                sp.wait_ge(saved, 16 * 8)


class Ring:

    def __init__(self, nc, st, tokens, parts, slots, load):
        self.nc, self.parts, self.slots, self.load_item = nc, parts, slots, load
        self.items = [(u, e, b2) for u in range(DEC_B // 2) for e in range(parts) for b2 in range(2)]
        self.rows = st.sb("rows", [P, slots, tokens * 2 * GD])
        self.landed = [st.sem(f"landed{i}") for i in range(slots)]
        self.used = st.sem("used")
        self.tiles = self.rows[:].rearrange("p s (l c g) -> p s l c g", l=tokens, c=2)

    def load(self, engine, i):
        u, e, b2 = self.items[i]
        if i >= self.slots:
            engine.wait_ge(self.used, (i - self.slots) // 2 + 1)
        self.load_item(engine, self.rows[:, i % self.slots, :], 2 * u + b2, e).then_inc(self.landed[i % self.slots], 16)

    def item(self, u, e, b2):
        return (u * self.parts + e) * 2 + b2

    def tile(self, u, e, b2):
        return self.tiles[:, self.item(u, e, b2) % self.slots]

    def wait(self, pe, u, e, b2):
        i = self.item(u, e, b2)
        pe.wait_ge(self.landed[i % self.slots], 16 * (i // self.slots + 1))


def decode_stage(nc, M, name, q_T, cmp_kT, q_blk, new_kT, new_v, tiles, o_out, block_mask, ring):
    QUADS = tiles // 4
    NK = tiles * P
    with Stage(nc, name) as st:
        kt = st.sb("kt", [P, 3, 4, P])
        s = [q_T[:].rearrange("p a r t -> p (a r t)")[:, 0:NK], cmp_kT[:].rearrange("p b a k -> p (b a k)")[:, 0:NK]]
        s_new = st.sb("s_new", [P, 2, NDEC])
        e_T = M.h_T[:].rearrange("p c t -> p (c t)")[:, 0:(tiles + 1) * P].rearrange("p (l j) -> p l j", j=P)
        small = st.sb("small", [P, 4, 7])
        scale = st.sb("scale", [P, AG])
        o = st.sb("o", [P, 4, ADH])
        tr = [st.ps(f"tr{i}", [P, 4, P]) for i in range(3)]
        ps_s = [st.ps(f"ps_s{i}", [P, 4, P]) for i in range(2)]
        ps_t = [st.ps(f"ps_t{i}", [P, 4, P]) for i in range(2)]
        ps_o = st.ps("ps_o", [P, AG, ADH])
        vec = st.sem("vec")
        copied = [st.sem("copied_act"), st.sem("copied_dve")]
        turned, scored, masked, maxed, expd, expd_old = (st.sem(n) for n in (
            "turned", "scored", "masked", "maxed", "expd", "expd_old"))
        e_turned, e_copied, summed, o_ready, saved, multiplied = (st.sem(n) for n in (
            "e_turned", "e_copied", "summed", "o_ready", "saved", "multiplied"))
        PART = tiles // ring.parts
        GK = QUADS * 4
        TQ = QUADS + 1
        SQ = QUADS + 1
        AHEAD = 4
        NG = GK * (DEC_B // 2)
        LEAD = 2 if QUADS > 1 else 1
        new_mask = M.c("new_mask")
        with nc.Block() as block:

            @block.gpsimd
            def _(pool):
                for i in range(ring.slots, len(ring.items)):
                    ring.load(pool, i)

            @block.tensor
            def _(pe):
                def turn(e):
                    u, k = divmod(e, GK)
                    lq, b2, a = k // 4, (k // 2) % 2, k % 2
                    part, first = divmod(4 * lq, PART)
                    if first == 0 and a == 0:
                        ring.wait(pe, u, part, b2)
                    if e >= 3:
                        pe.wait_ge(copied[(e - 3) % 2], (e - 3) // 2 + 1)
                    for l in range(4):
                        mm = pe.transpose(tr[e % 3][:, l, :], ring.tile(u, part, b2)[:, first + l, 0, a * P:(a + 1) * P],
                                          M.ident)
                    mm.then_inc(turned, 1)

                def product(e):
                    u, k = divmod(e, GK)
                    lq, b2, a = k // 4, (k // 2) % 2, k % 2
                    bank = SQ * u + lq
                    pe.wait_ge(copied[e % 2], e // 2 + 1)
                    if k % 4 == 0 and bank >= 2:
                        pe.wait_ge(masked, bank - 1)
                    r0 = 64 * b2 + 32 * a
                    pe.matmul(ps_s[bank % 2][r0:r0 + 32], q_blk[:, 2 * u + b2, a, :], kt[:, e % 3],
                              start=True, stop=True).then_inc(multiplied, 1)

                def new_keys(u):
                    bank = SQ * u + QUADS
                    if bank >= 2:
                        pe.wait_ge(masked, bank - 1)
                    for b2 in range(2):
                        for a in range(2):
                            r0 = 64 * b2 + 32 * a
                            mm = pe.matmul(ps_s[bank % 2][r0:r0 + 32, 0, 0:NDEC], q_blk[:, 2 * u + b2, a, :],
                                           new_kT[:, a, SEQ:NTOK], start=True, stop=True)
                    mm.then_inc(scored, 1)

                def turn_e(u, k):
                    e = TQ * u + k
                    if e >= 2:
                        pe.wait_ge(e_copied, e - 1)
                    if k < QUADS:
                        for l in range(4):
                            mm = pe.transpose(ps_t[e % 2][:, l, :], s[u % 2][:, (4 * k + l) * P:(4 * k + l + 1) * P],
                                              M.ident)
                    else:
                        mm = pe.transpose(ps_t[e % 2][0:NDEC, 0, :], s_new[:, u % 2, :], M.ident)
                    mm.then_inc(e_turned, 1)

                def values(u):
                    pe.wait_ge(expd, u + 1)
                    turn_e(u, 0)
                    if u:
                        pe.wait_ge(o_ready, u)
                    for k in range(TQ):
                        if k + 1 < TQ:
                            turn_e(u, k + 1)
                        pe.wait_ge(e_copied, TQ * u + k + 1)
                        part, first = divmod(4 * k, PART)
                        for l in range(4 if k < QUADS else 1):
                            for b2 in range(2):
                                out = ps_o[64 * b2:64 * b2 + 64].rearrange("p g d -> p (g d)")
                                if k < QUADS:
                                    mm = pe.matmul(out, e_T[:, 4 * k + l, 64 * b2:64 * b2 + 64],
                                                   ring.tile(u, part, b2)[:, first + l, 1, :], start=(k + l == 0),
                                                   stop=False)
                                else:
                                    mm = pe.matmul(out, e_T[0:NDEC, tiles, 64 * b2:64 * b2 + 64], new_v,
                                                   start=False, stop=True)
                        if k < QUADS and first + 4 == PART:
                            mm.then_inc(ring.used, 1)
                    mm.then_inc(summed, 1)

                for e in range(LEAD):
                    turn(e)
                for e in range(NG):
                    u, k = divmod(e, GK)
                    if e + LEAD < NG:
                        turn(e + LEAD)
                    product(e)
                    if k == GK - 1:
                        new_keys(u)
                    if u and k == AHEAD - 1:
                        values(u - 1)
                values(NG // GK - 1)

            def copy_keys(engine, e):
                engine.wait_ge(turned, e + 1)
                if e >= 3:
                    engine.wait_ge(multiplied, e - 2)
                if e % 2 == 0:
                    engine.activation(kt[:, e % 3], tr[e % 3][:], ACT.Copy).then_inc(copied[0], 1)
                else:
                    engine.tensor_copy(kt[:, e % 3], tr[e % 3][:]).then_inc(copied[1], 1)

            @block.scalar
            def _(act):
                def exps(u):
                    act.wait_ge(maxed, u + 1)
                    act.activation(s[u % 2], s[u % 2], ACT.Exp, bias=small[:, u, 0:1], accum_out=small[:, u, 5:6]
                                   ).then_inc(expd_old, 1)
                    act.wait_ge(expd_old, u + 1)
                    act.activation(s_new[:, u % 2], s_new[:, u % 2], ACT.Exp, bias=small[:, u, 0:1],
                                   accum_out=small[:, u, 6:7]).then_inc(expd, 1)

                def copy_e(u):
                    for k in range(TQ):
                        act.wait_ge(e_turned, TQ * u + k + 1)
                        if u and k == 0:
                            act.wait_ge(summed, u)
                        if k < QUADS:
                            act.activation(e_T[:, 4 * k:4 * k + 4, :], ps_t[(TQ * u + k) % 2][:], ACT.Copy
                                           ).then_inc(e_copied, 1)
                        else:
                            act.activation(e_T[0:NDEC, tiles, :], ps_t[(TQ * u + k) % 2][0:NDEC, 0, :], ACT.Copy
                                           ).then_inc(e_copied, 1)

                for e in range(0, NG, 2):
                    u, k = divmod(e, GK)
                    copy_keys(act, e)
                    if u and k == 2:
                        exps(u - 1)
                    if u and k == AHEAD - 2:
                        copy_e(u - 1)
                exps(NG // GK - 1)
                copy_e(NG // GK - 1)

            @block.vector
            def _(dve):
                step = Chain(dve, vec)

                def mask(u, lq):
                    if lq == 0 and u >= 2:
                        dve.wait_ge(e_turned, TQ * (u - 1))
                    out = s[u % 2][:, lq * 4 * P:(lq + 1) * 4 * P]
                    bank = SQ * u + lq
                    dve.wait_ge(multiplied, GK * u + 4 * lq + 4)
                    if block_mask is not None:
                        full = [P, 4, PAST // SBLK, 4]
                        dve.tensor_tensor(out.rearrange("p (l j k) -> p l j k", l=4, k=4),
                                          ps_s[bank % 2][:].rearrange("p l (j k) -> p l j k", k=4),
                                          block_mask[:, u, None, :, None].to_broadcast(full), ALU.add
                                          ).then_inc(masked, 1)
                    else:
                        dve.tensor_tensor(out.rearrange("p (l j) -> p l j", l=4), ps_s[bank % 2][:],
                                          M.c("win_mask"), ALU.add).then_inc(masked, 1)

                def maxima(u):
                    mask(u, QUADS - 1)
                    dve.wait_ge(scored, u + 1)
                    dve.tensor_tensor(s_new[:, u % 2], ps_s[(SQ * u + QUADS) % 2][:, 0, 0:NDEC], new_mask[:, u, :],
                                      ALU.add).then_inc(masked, 1)
                    dve.wait_ge(masked, SQ * (u + 1))
                    step(dve.tensor_reduce(small[:, u, 3:4], s[u % 2], AX.X, ALU.max, negate=True))
                    step(dve.tensor_reduce(small[:, u, 4:5], s_new[:, u % 2], AX.X, ALU.max, negate=True))
                    dve.tensor_tensor(small[:, u, 0:1], small[:, u, 3:4], small[:, u, 4:5], ALU.min
                                      ).then_inc(maxed, 1)

                def finish(u):
                    dve.wait_ge(expd, u + 1)
                    step(dve.tensor_tensor(small[:, u, 1:2], small[:, u, 5:6], small[:, u, 6:7], ALU.add))
                    step(dve.reciprocal(small[:, u, 2:3], small[:, u, 1:2]))
                    step(dve.tensor_scalar(scale[:], M.c("group_one"), small[:, u, 2:3], None, ALU.mult))
                    dve.wait_ge(summed, u + 1)
                    for g in range(AG):
                        if g == 0:
                            step(dve.tensor_scalar(o[:, u], ps_o[:, 0, :], scale[:, 0:1], None, ALU.mult))
                        else:
                            step(dve.scalar_tensor_tensor(out=o[:, u], in0=ps_o[:, g, :], scalar=scale[:, g:g + 1],
                                                          in1=o[:, u], op0=ALU.mult, op1=ALU.add))
                    dve.nop().then_inc(o_ready, 1)

                for e in range(1, NG, 2):
                    u, k = divmod(e, GK)
                    copy_keys(dve, e)
                    if k % 4 == 1 and k > 4:
                        mask(u, k // 4 - 1)
                    if k == 1 and u:
                        maxima(u - 1)
                    if k == AHEAD - 1 and u:
                        finish(u - 1)
                maxima(NG // GK - 1)
                finish(NG // GK - 1)

            @block.sync
            def _(sp):
                for u in range(4):
                    sp.wait_ge(o_ready, u + 1)
                    for b2 in range(2):
                        b = 2 * u + b2
                        sp.dma_start(o_out[DEC_S * b:DEC_S * (b + 1)].rearrange("s (h d) -> h s d", h=AH),
                                     o[64 * b2:64 * b2 + 64, u, :]).then_inc(saved, 16)
                sp.wait_ge(saved, 16 * 8)


def mix_stage(nc, M, q, gate, o_dec):
    with Stage(nc, "mg") as st:
        parts = st.sb("parts", [NDEC, 3, AH, ADH])
        loaded, vec = st.sem("loaded"), st.sem("vec")
        with nc.Block() as block:

            @block.sync
            def _(sp):
                sp.dma_start(parts[:].rearrange("p b h d -> p b (h d)"), o_dec.rearrange("b t d -> t b d")
                             ).then_inc(loaded, 16)

            @block.vector
            def _(dve):
                step = Chain(dve, vec)
                dve.wait_ge(loaded, 16)
                for br in range(3):
                    step(dve.tensor_tensor(parts[:, br], parts[:, br],
                                           gate[0:NDEC, 2, :, br, None].to_broadcast([NDEC, AH, ADH]), ALU.mult))
                step(dve.tensor_tensor(parts[:, 0], parts[:, 0], parts[:, 1], ALU.add))
                step(dve.tensor_tensor(q[0:NDEC, 2, :].rearrange("p (h d) -> p h d", h=AH), parts[:, 0], parts[:, 2],
                                       ALU.add))


class Memory:

    def __init__(self, nc, stack):
        self.x = stack.enter_context(nc.sbuf_tensor("x", [P, NT, D], F32))
        self.h_T = stack.enter_context(nc.sbuf_tensor("h_T", [P, DC, NTOK], F32))
        self.const = stack.enter_context(nc.sbuf_tensor("const", [P, CONST.shape[1]], F32))
        self.ident = view(self.const, "ident")

    def c(self, name, rows=None):
        return view(self.const, name, rows)


def load_stage(nc, M, I, half_idx, quarter_idx):
    with Stage(nc, "ld") as st:
        pages = st.sb("pages", [NPAGE, DEC_B], I32)
        pages_f = st.sb("pages_f", [NPAGE, DEC_B])
        row_f = st.sb("row_f", [P, DEC_B])
        ps_rows = st.ps("ps_rows", [P, DEC_B])
        pages_in, pages_ready, rows_ready, vec = (st.sem(n) for n in ("pages_in", "pages_ready", "rows_ready", "vec"))
        loaded = st.sem("loaded")
        cleared = st.sem("cleared")
        with nc.Block() as block:

            @block.vector
            def _(dve):
                dve.memset(M.x[:, NT - 1, :], 0.0).then_inc(cleared, 1)
                step = Chain(dve, vec)
                dve.wait_ge(pages_in, 16)
                dve.tensor_copy(pages_f[:], pages[:]).then_inc(pages_ready, 1)
                dve.wait_ge(rows_ready, 1)
                step(dve.scalar_tensor_tensor(out=row_f[:], in0=ps_rows[:], scalar=float(PAGE // CSTR),
                                              in1=M.c("pos16"), op0=ALU.mult, op1=ALU.add))
                for e in range(4):
                    step(dve.tensor_scalar(quarter_idx[:, e, :], row_f[:], 4.0, float(e), ALU.mult, ALU.add))
                for e in range(2):
                    step(dve.tensor_scalar(half_idx[:, e, 0:DEC_B], row_f[:], 2.0, float(e), ALU.mult, ALU.add))
                    step(dve.tensor_scalar(half_idx[:, e, DEC_B:DEC_B + 1], row_f[:, 0:1], 2.0, float(e), ALU.mult,
                                           ALU.add))

            @block.scalar
            def _(act):
                with nc.allow_non_contiguous_dma(reason="128 page numbers"):
                    act.dma_start(pages[:], I["page_table"].rearrange("b k -> k b")).then_inc(pages_in, 16)

            @block.tensor
            def _(pe):
                pe.wait_ge(pages_ready, 1)
                pe.wait_ge(loaded, 48)
                pe.matmul(ps_rows[:], M.c("page_rep"), pages_f[:], start=True, stop=True).then_inc(rows_ready, 1)

            @block.sync
            def _(sp):
                sp.dma_start(M.x[:, 0:2, :], I["x_prompt"][0].rearrange("(t p) d -> p t d", p=P)).then_inc(loaded, 16)
                sp.wait_ge(cleared, 1)
                sp.dma_start(M.x[0:NDEC, 2, :], I["x_sample"].rearrange("b s d -> (b s) d")).then_inc(loaded, 16)
                sp.dma_start(M.const[:], I["const"]).then_inc(loaded, 16)
                sp.wait_ge(loaded, 48)


def final_stage(nc, M, I, O):
    with Stage(nc, "fi") as st:
        gain_b = st.sb("gain", [P, D])
        y = st.sb("y", [P, NT, D])
        sq = st.sb("sq", [P, 2, D])
        ss = st.sb("ss", [P, 3, NT])
        gain_in, vec, mean_ready, root_ready, y_ready, saved = (
            st.sem(n) for n in ("gain_in", "vec", "mean_ready", "root_ready", "y_ready", "saved"))
        with nc.Block() as block:

            @block.sync
            def _(sp):
                sp.dma_start(gain_b[:], I["norm_final"].partition_broadcast(P)).then_inc(gain_in, 16)
                for t, (t0, n) in enumerate(TILES):
                    sp.wait_ge(y_ready, t + 1)
                    out = O["y_p"][0, t0:t0 + n] if t < 2 else O["y_s"].rearrange("b s d -> (b s) d")
                    sp.dma_start(out, y[0:n, t, :]).then_inc(saved, 16)
                sp.wait_ge(saved, 16 * NT)

            @block.scalar
            def _(act):
                for t, (_, n) in enumerate(TILES):
                    act.wait_ge(mean_ready, t + 1)
                    act.activation(ss[0:n, 0, t:t + 1], ss[0:n, 1, t:t + 1], ACT.Sqrt).then_inc(root_ready, 1)

            @block.vector
            def _(dve):
                step = Chain(dve, vec)
                for t, (_, n) in enumerate(TILES):
                    step(dve.tensor_tensor_reduce(sq[0:n, t % 2, :], M.x[0:n, t, :], M.x[0:n, t, :], 1.0, 0.0,
                                                  ALU.mult, ALU.add, ss[0:n, 0, t:t + 1]))
                    dve.tensor_scalar(ss[0:n, 1, t:t + 1], ss[0:n, 0, t:t + 1], 1.0 / D, EPS,
                                      ALU.mult, ALU.add).then_inc(mean_ready, 1)
                dve.wait_ge(gain_in, 16)
                for t, (_, n) in enumerate(TILES):
                    dve.wait_ge(root_ready, t + 1)
                    step(dve.reciprocal(ss[0:n, 2, t:t + 1], ss[0:n, 0, t:t + 1]))
                    dve.scalar_tensor_tensor(out=y[0:n, t, :], in0=M.x[0:n, t, :], scalar=ss[0:n, 2, t:t + 1],
                                             in1=gain_b[0:n, :], op0=ALU.mult, op1=ALU.mult).then_inc(y_ready, 1)


def program(nc, I, O):
    with ExitStack() as stack:
        M = Memory(nc, stack)
        with Stage(nc, "cx") as st:
            quarter_idx = st.sb("quarter_idx", [P, 4, DEC_B], U32)
            half_idx = st.sb("half_idx", [P, 2, DEC_B + 1], U32)
            cmp_kT = st.sb("cmp_kT", [P, DEC_B, 2, KEY_ROWS])
            cmp_v = st.sb("cmp_v", [P, DEC_B, GD])
            load_stage(nc, M, I, half_idx, quarter_idx)
            mlstm_stage(nc, M, I, O)
            peer_stage(nc, "f0", M, I, 0, side=(half_idx, cmp_kT, cmp_v))
            nsa_stage(nc, M, I, O, quarter_idx, cmp_kT, cmp_v)
        peer_stage(nc, "f1", M, I, 1)
        final_stage(nc, M, I, O)


OUTPUTS = [
    ("y_p", (1, SEQ, D)), ("y_s", (DEC_B, DEC_S, D)),
    ("cmp_p", (1, 1, SEQ, 2, AG, ADH)), ("sel_p", (1, 1, SEQ, 2, AG, ADH)), ("win_p", (1, 1, SEQ, 2, AG, ADH)),
    ("C_p", (1, 1, MH, MDK, MDV)), ("n_p", (1, 1, MH, MDK)), ("m_p", (1, 1, MH)),
    ("cmp_s", (1, DEC_B, DEC_S, 2, AG, ADH)), ("sel_s", (1, DEC_B, DEC_S, 2, AG, ADH)),
    ("win_s", (1, DEC_B, WIN, 2, AG, ADH)),
    ("C_s", (1, DEC_B, MH, MDK, MDV)), ("n_s", (1, DEC_B, MH, MDK)), ("m_s", (1, DEC_B, MH)),
]


def kernel(**inputs):
    import concourse.bacc as bacc
    from concourse.bass_utils import run_bass_kernel_spmd

    nc = bacc.Bacc("TRN2", target_bir_lowering=False, num_devices=1)
    arrays, I, O = {}, {}, {}
    for name, value in {**inputs, "const": CONST}.items():
        a = np.ascontiguousarray(value)
        arrays[f"in_{name}_dram"] = a
        I[name] = nc.dram_tensor(f"in_{name}_dram", a.shape, mybir.dt.from_np(a.dtype), kind="ExternalInput").ap()
    for name, shape in OUTPUTS:
        O[name] = nc.dram_tensor(f"out_{name}_dram", shape, F32, kind="ExternalOutput").ap()
    program(nc, I, O)
    r = run_bass_kernel_spmd(nc, [arrays], core_ids=[0])
    return tuple(r.results[0][f"out_{name}_dram"] for name, _ in OUTPUTS)
```
